# Optimizing a Trainium2 kernel written in Bass

```python
import math
import jax, jax.numpy as jnp
from jax import lax
import numpy as np

D_MODEL = 1024
BATCH = 1
SEQ = 128
DEPTH = 1
DEC_BATCH = 1
DEC_SEQ = 256
PAST_LEN = 128

GRID_W = 64
EPS = 1e-6
LOG_FLOOR = 1e-30
MASK_NEG = -1e30
N_BRANCH = 4
D_BRANCH = 512
SHORT_CONV_W = 3
HY_ORDER = 2
HY_POS_FREQS = 16
HY_POS_DIM = 1 + 2 * HY_POS_FREQS
HY_FILTER_HIDDEN = 64
HY_SIN_FREQ = 1.0
HY_FAST_DECAY = 0.3
HY_SLOW_DECAY = 1.5
HY_DECAY_TARGET = 1e-2
HG_HEADS = 4
HG_DK = 128
HG_DV = 128
HG_CHUNK = 16
SSD_HEADS = 8
SSD_P = 64
SSD_GROUPS = 2
SSD_N = 128
SSD_CHUNK = 64
GDN_HEADS = 4
GDN_DK = 128
GDN_DV = 128
GDN_CHUNK = 64
N_EXPERTS = 64
TOP_K = 8
N_EXPERT_GROUPS = 8
TOPK_GROUPS = 4
D_EXPERT = 256
D_SHARED = 256
ROUTED_SCALE = 2.5
MOE_BLOCK = 128

CONV_SPLITS = (D_BRANCH, D_BRANCH, D_BRANCH,
               SSD_HEADS * SSD_P, SSD_GROUPS * SSD_N, SSD_GROUPS * SSD_N,
               GDN_HEADS * GDN_DK, GDN_HEADS * GDN_DK, GDN_HEADS * GDN_DV)
D_CONV = sum(CONV_SPLITS)
PLAIN_SPLITS = (HG_HEADS * HG_DK, HG_HEADS * HG_DK, HG_HEADS * HG_DK, HG_HEADS * HG_DV, HG_HEADS * HG_DV,
                SSD_HEADS * SSD_P, SSD_HEADS, SSD_HEADS,
                GDN_HEADS * GDN_DV, GDN_HEADS, GDN_HEADS, GDN_HEADS, GDN_HEADS,
                N_BRANCH * D_MODEL)
D_IN = D_CONV + sum(PLAIN_SPLITS)

kernel_name = "bidir_hybrid_hyena_hgrn2_ssd_gdn_moe_dit"

F32 = jnp.float32

def _split(a, widths):
    cuts = [int(i) for i in np.cumsum(widths)[:-1]]
    return jnp.split(a, cuts, axis=-1)

def _rmsnorm(x, g):
    xf = x.astype(F32)
    return (xf * lax.rsqrt(jnp.mean(xf * xf, axis=-1, keepdims=True) + EPS)).astype(x.dtype) * g

def _l2norm(a):
    af = a.astype(F32)
    return af * lax.rsqrt(jnp.sum(af * af, axis=-1, keepdims=True) + EPS)

def _masked_exp(mask, diff):
    return jnp.where(mask, jnp.exp(jnp.where(mask, diff, 0.0)), 0.0)

def _short_conv(u, w, b, on_grid):
    bsz, L, ch = u.shape
    seq = u.reshape(bsz * (L // GRID_W), GRID_W, ch) if on_grid else u
    n = seq.shape[1]
    pad = SHORT_CONV_W // 2
    sp = jnp.pad(seq, ((0, 0), (pad, pad), (0, 0)))
    out = b + sp[:, 0:n] * w[0]
    for j in range(1, SHORT_CONV_W):
        out = out + sp[:, j:j + n] * w[j]
    return out.reshape(bsz, L, ch)

def _hyena_filters(L, w1, b1, w2, b2, w3):
    t = jnp.arange(L, dtype=F32) / L
    bands = jnp.arange(1, HY_POS_FREQS + 1, dtype=F32)
    ang = 2.0 * math.pi * t[:, None] * bands
    feats = jnp.concatenate([t[:, None], jnp.sin(ang), jnp.cos(ang)], axis=-1)
    hdn = jnp.sin(HY_SIN_FREQ * (feats @ w1 + b1))
    hdn = jnp.sin(HY_SIN_FREQ * (hdn @ w2 + b2))
    filt = (hdn @ w3).astype(F32).reshape(L, 2, HY_ORDER, D_BRANCH)
    max_decay = math.log(HY_DECAY_TARGET) / HY_FAST_DECAY
    min_decay = math.log(HY_DECAY_TARGET) / HY_SLOW_DECAY
    deltas = jnp.linspace(min_decay, max_decay, D_BRANCH, dtype=F32)
    window = jnp.exp(-t[:, None] * jnp.abs(deltas))
    return filt * window[:, None, None, :]

def _fft_bidir_conv(u, h_causal, h_anti, bias):
    L, ch = u.shape[1], u.shape[-1]
    two_sided = jnp.concatenate([h_causal, jnp.zeros((1, ch), F32), h_anti[:0:-1]], axis=0)
    hf = jnp.fft.rfft(two_sided, axis=0)
    uf32 = u.astype(F32)
    uf = jnp.fft.rfft(uf32, n=2 * L, axis=1)
    y = jnp.fft.irfft(uf * hf[None], n=2 * L, axis=1)[:, :L]
    return (y + uf32 * bias).astype(u.dtype)

def _hyena(v, x1, x2, p):
    L = v.shape[1]
    filt = _hyena_filters(L, p["hy_w1"], p["hy_b1"], p["hy_w2"], p["hy_b2"], p["hy_w3"])
    z = x1 * _fft_bidir_conv(v, filt[:, 0, 0], filt[:, 1, 0], p["hy_bias"][0])
    return x2 * _fft_bidir_conv(z, filt[:, 0, 1], filt[:, 1, 1], p["hy_bias"][1])

def _chunk(a, size):
    bsz, L, h = a.shape[:3]
    a = a.astype(F32).reshape((bsz, L // size, size, h) + a.shape[3:])
    return jnp.moveaxis(a, (1, 2), (0, 3))

def _unchunk(a):
    a = jnp.moveaxis(a, (0, 3), (1, 2))
    return a.reshape((a.shape[0], a.shape[1] * a.shape[2]) + a.shape[3:])

def _hgrn2_chunked(q, v, k, log_f, s0):
    qc, vc, kc, gc = (_chunk(a, HG_CHUNK) for a in (q, v, k, log_f))
    incl = jnp.tril(jnp.ones((HG_CHUNK, HG_CHUNK), bool))

    def step(s, inp):
        qi, vi, ki, gi = inp
        b = jnp.cumsum(gi, axis=2)
        pair = _masked_exp(incl[:, :, None], b[:, :, :, None] - b[:, :, None])
        attn = jnp.einsum("bhtk,bhsk,bhtsk->bhts", qi, ki, pair)
        o = jnp.einsum("bhtk,bhkv->bhtv", qi * jnp.exp(b), s) + jnp.einsum("bhts,bhsv->bhtv", attn, vi)
        b_end = b[:, :, -1:]
        s = jnp.exp(b_end)[:, :, 0, :, None] * s + jnp.einsum("bhsk,bhsv->bhkv", ki * jnp.exp(b_end - b), vi)
        return s, o

    s_fin, o = lax.scan(step, s0.astype(F32), (qc, vc, kc, gc))
    return _unchunk(o), s_fin

def _ssd_chunked(x, bm, cm, dt, log_a, s0):
    xc, bc, cc, dtc, lac = (_chunk(a, SSD_CHUNK) for a in (x, bm, cm, dt, log_a))
    incl = jnp.tril(jnp.ones((SSD_CHUNK, SSD_CHUNK), bool))

    def step(s, inp):
        xi, bi, ci, dti, lai = inp
        cum = jnp.cumsum(lai, axis=-1)
        lmat = _masked_exp(incl, cum[..., :, None] - cum[..., None, :])
        scores = jnp.einsum("bhtn,bhsn->bhts", ci, bi) * lmat
        xdt = xi * dti[..., None]
        y = jnp.einsum("bhts,bhsp->bhtp", scores, xdt) + jnp.einsum("bhtn,bhpn->bhtp", ci * jnp.exp(cum)[..., None], s)
        s = jnp.exp(cum[..., -1])[..., None, None] * s + jnp.einsum(
            "bhsp,bhsn->bhpn", xdt * jnp.exp(cum[..., -1:] - cum)[..., None], bi)
        return s, y

    s_fin, y = lax.scan(step, s0.astype(F32), (xc, bc, cc, dtc, lac))
    return _unchunk(y), s_fin

def _gdn_chunked(q, k, v, log_alpha, beta, s0):
    qc, kc, vc, gl, bc = (_chunk(a, GDN_CHUNK) for a in (q, k, v, log_alpha, beta))
    incl = jnp.tril(jnp.ones((GDN_CHUNK, GDN_CHUNK), bool))
    strict = jnp.tril(jnp.ones((GDN_CHUNK, GDN_CHUNK), bool), -1)
    g = jnp.cumsum(gl, axis=-1)
    decay = _masked_exp(incl, g[..., :, None] - g[..., None, :])
    kb = kc * bc[..., None]
    a_strict = jnp.where(strict, jnp.einsum("nbhtk,nbhsk->nbhts", kb, kc) * decay, 0.0)
    u = lax.linalg.triangular_solve(a_strict, vc * bc[..., None], left_side=True, lower=True, unit_diagonal=True)
    w = lax.linalg.triangular_solve(a_strict, kb * jnp.exp(g)[..., None], left_side=True, lower=True, unit_diagonal=True)
    qs = qc * (GDN_DK ** -0.5)
    aqk = jnp.einsum("nbhtk,nbhsk->nbhts", qs, kc) * decay

    def step(s, inp):
        qi, ki, ui, wi, gi, ai = inp
        v_new = ui - jnp.einsum("bhtk,bhkv->bhtv", wi, s)
        o = jnp.einsum("bhtk,bhkv->bhtv", qi * jnp.exp(gi)[..., None], s) + jnp.einsum("bhts,bhsv->bhtv", ai, v_new)
        g_end = gi[..., -1:]
        s = jnp.exp(g_end)[..., None] * s + jnp.einsum("bhsk,bhsv->bhkv", ki * jnp.exp(g_end - gi)[..., None], v_new)
        return s, o

    s_fin, o = lax.scan(step, s0.astype(F32), (qs, kc, u, w, g, aqk))
    return _unchunk(o), s_fin

def _scan_both_directions(scan_fn, shared, fwd_only, bwd_only, s0):
    flip = lambda a: jnp.flip(a, axis=1)
    o_f, s_f = scan_fn(*shared, *fwd_only, s0[:, 0])
    o_b, s_b = scan_fn(*map(flip, shared), *map(flip, bwd_only), s0[:, 1])
    return o_f + flip(o_b), jnp.stack([s_f, s_b], axis=1)

def _hgrn_lower_bounds(hg_lb):
    pr = jax.nn.softmax(hg_lb.astype(F32), axis=1)
    lb = jnp.cumsum(pr, axis=1) - pr[:, :1]
    return lb.reshape(2, DEPTH, HG_HEADS, HG_DK)

def _token_mixers(h, st_hg, st_ssd, st_gdn, p, lb, on_grid):
    bsz, L, _ = h.shape
    heads = lambda a, d: a.reshape(bsz, L, -1, d)
    proj = h @ p["w_in"]
    conv_out = _short_conv(proj[..., :D_CONV], p["conv_w"], p["conv_b"], on_grid)
    hy_v, hy_x1, hy_x2, ssd_x, ssd_b, ssd_c, gdn_q, gdn_k, gdn_v = _split(conv_out, CONV_SPLITS)
    (hg_q, hg_f_fwd, hg_f_bwd, hg_v, hg_g, ssd_z, ssd_dt_fwd, ssd_dt_bwd,
     gdn_g, gdn_a_fwd, gdn_a_bwd, gdn_b_fwd, gdn_b_bwd, merge) = _split(proj[..., D_CONV:], PLAIN_SPLITS)

    y_a = _hyena(hy_v, hy_x1, hy_x2, p)

    def hg_gates(f_raw, lb_dir):
        uf = heads(f_raw, HG_DK).astype(F32)
        f = lb_dir + (1.0 - lb_dir) * jax.nn.sigmoid(uf)
        log_f = jnp.log(jnp.maximum(f, LOG_FLOOR))
        return (1.0 - lb_dir) * jax.nn.sigmoid(-uf), log_f
    o_hg, s_hg = _scan_both_directions(
        _hgrn2_chunked, (heads(jax.nn.silu(hg_q), HG_DK), heads(hg_v, HG_DV)),
        hg_gates(hg_f_fwd, lb[0]), hg_gates(hg_f_bwd, lb[1]), st_hg)
    y_b = (_rmsnorm(o_hg.astype(h.dtype), p["hg_norm"]) * jax.nn.silu(heads(hg_g, HG_DV))).reshape(bsz, L, D_BRANCH)

    x_s = heads(jax.nn.silu(ssd_x), SSD_P)
    rep = SSD_HEADS // SSD_GROUPS
    bm = jnp.repeat(heads(jax.nn.silu(ssd_b), SSD_N), rep, axis=2)
    cm = jnp.repeat(heads(jax.nn.silu(ssd_c), SSD_N), rep, axis=2)
    def ssd_gates(dt_raw, d):
        dt = jax.nn.softplus(dt_raw.astype(F32) + p["ssd_dt_bias"][d])
        return dt, -jnp.exp(p["ssd_a_log"][d].astype(F32)) * dt
    y_ssd, s_ssd = _scan_both_directions(_ssd_chunked, (x_s, bm, cm), ssd_gates(ssd_dt_fwd, 0), ssd_gates(ssd_dt_bwd, 1), st_ssd)
    y_ssd = y_ssd.astype(h.dtype) + x_s * p["ssd_d"][:, None]
    gated = (y_ssd.reshape(bsz, L, D_BRANCH) * jax.nn.silu(ssd_z)).reshape(bsz, L, SSD_GROUPS, -1)
    y_c = _rmsnorm(gated, p["ssd_norm"].reshape(SSD_GROUPS, -1)).reshape(bsz, L, D_BRANCH)

    def gdn_gates(a_raw, b_raw, d):
        log_alpha = -jnp.exp(p["gdn_a_log"][d].astype(F32)) * jax.nn.softplus(a_raw.astype(F32) + p["gdn_dt_bias"][d])
        return log_alpha, jax.nn.sigmoid(b_raw.astype(F32))
    o_gdn, s_gdn = _scan_both_directions(
        _gdn_chunked,
        (_l2norm(heads(jax.nn.silu(gdn_q), GDN_DK)), _l2norm(heads(jax.nn.silu(gdn_k), GDN_DK)), heads(jax.nn.silu(gdn_v), GDN_DV)),
        gdn_gates(gdn_a_fwd, gdn_b_fwd, 0), gdn_gates(gdn_a_bwd, gdn_b_bwd, 1), st_gdn)
    y_d = (_rmsnorm(o_gdn.astype(h.dtype), p["gdn_norm"]) * jax.nn.silu(heads(gdn_g, GDN_DV))).reshape(bsz, L, D_BRANCH)

    branches = jnp.stack([y_a, y_b, y_c, y_d], axis=2)
    lifted = jnp.einsum("blnc,ncd->blnd", branches, p["w_branch"])
    gates = jax.nn.sigmoid(merge).reshape(bsz, L, N_BRANCH, D_MODEL)
    mixed = jnp.einsum("blnd,blnd->bld", gates, lifted)
    return mixed @ p["w_out"], s_hg, s_ssd, s_gdn

def _routed_experts(xt, idx, wts, w1, w3, w2):
    T, D = xt.shape
    A = T * TOP_K
    e_flat = idx.reshape(-1)
    order = jnp.argsort(e_flat)
    e_sorted = e_flat[order]
    counts = jnp.zeros((N_EXPERTS,), jnp.int32).at[e_flat].add(1)
    padded = (counts + MOE_BLOCK - 1) // MOE_BLOCK * MOE_BLOCK
    start = jnp.cumsum(counts) - counts
    ends_pad = jnp.cumsum(padded)
    start_pad = ends_pad - padded
    dest = start_pad[e_sorted] + jnp.arange(A, dtype=jnp.int32) - start[e_sorted]
    n_blocks = (A + N_EXPERTS * (MOE_BLOCK - 1) + MOE_BLOCK - 1) // MOE_BLOCK
    R = n_blocks * MOE_BLOCK
    row_token = jnp.full((R,), T, jnp.int32).at[dest].set((order // TOP_K).astype(jnp.int32))
    row_gate = jnp.zeros((R,), xt.dtype).at[dest].set(wts.reshape(-1)[order].astype(xt.dtype))
    block_expert = jnp.minimum(
        jnp.searchsorted(ends_pad, jnp.arange(n_blocks, dtype=jnp.int32) * MOE_BLOCK, side="right"), N_EXPERTS - 1)
    x_pad = jnp.concatenate([xt, jnp.zeros((1, D), xt.dtype)], axis=0)

    def block(args):
        rows, e = args
        xb = x_pad[rows]
        return (jax.nn.silu(xb @ w1[e]) * (xb @ w3[e])) @ w2[e]

    out = lax.map(block, (row_token.reshape(n_blocks, MOE_BLOCK), block_expert)).reshape(R, D)
    return jax.ops.segment_sum(out * row_gate[:, None], row_token, num_segments=T + 1)[:T]

def _moe(h, p):
    bsz, L, D = h.shape
    xt = h.reshape(-1, D)
    T = xt.shape[0]
    scores = jax.nn.sigmoid((xt @ p["router_w"]).astype(F32))
    biased = scores + p["router_bias"].astype(F32)
    grp_scores = lax.top_k(biased.reshape(T, N_EXPERT_GROUPS, -1), 2)[0].sum(-1)
    _, top_grp = lax.top_k(grp_scores, TOPK_GROUPS)
    grp_mask = jax.nn.one_hot(top_grp, N_EXPERT_GROUPS, dtype=F32).sum(1) > 0
    exp_mask = jnp.repeat(grp_mask, N_EXPERTS // N_EXPERT_GROUPS, axis=1)
    _, idx = lax.top_k(jnp.where(exp_mask, biased, MASK_NEG), TOP_K)
    w = jnp.take_along_axis(scores, idx, axis=1)
    w = w / jnp.sum(w, axis=-1, keepdims=True) * ROUTED_SCALE
    routed = _routed_experts(xt, idx, w, p["exp_w1"], p["exp_w3"], p["exp_w2"])
    shared = (jax.nn.silu(xt @ p["sh_w1"]) * (xt @ p["sh_w3"])) @ p["sh_w2"]
    return (routed + shared).reshape(bsz, L, D)

def _layer(x, cond, st_hg, st_ssd, st_gdn, p, lb, on_grid):
    mod = jax.nn.silu(cond) @ p["ada_w"] + p["ada_b"]
    sh1, sc1, g1, sh2, sc2, g2 = jnp.split(mod[:, None, :], 6, axis=-1)
    h = _rmsnorm(x, p["norm1_g"]) * (1.0 + sc1) + sh1
    mix, s_hg, s_ssd, s_gdn = _token_mixers(h, st_hg, st_ssd, st_gdn, p, lb, on_grid)
    x = x + g1 * mix
    h = _rmsnorm(x, p["norm2_g"]) * (1.0 + sc2) + sh2
    x = x + g2 * _moe(h, p)
    return x, s_hg, s_ssd, s_gdn

def setup_inputs(seed: int = 0) -> dict:
    key = jax.random.key(seed)
    ks = iter(jax.random.split(key, 48))

    def nrm(shape, scale):
        return scale * jax.random.normal(next(ks), shape, F32)

    def gain(shape):
        return 1.0 + nrm(shape, 0.02)

    def a_log(shape):
        return jnp.log(jax.random.uniform(next(ks), shape, F32, 1.0, 16.0))

    def dt_bias(shape):
        dt = jnp.exp(jax.random.uniform(next(ks), shape, F32, math.log(1e-3), math.log(1e-1)))
        return dt + jnp.log(-jnp.expm1(-dt))

    D = D_MODEL
    return {
        "x_prompt": nrm((BATCH, SEQ, D), 1.0),
        "x_sample": nrm((DEC_BATCH, DEC_SEQ, D), 1.0),
        "state_hgrn": nrm((DEC_BATCH, DEPTH, 2, HG_HEADS, HG_DK, HG_DV), 0.1),
        "state_ssd": nrm((DEC_BATCH, DEPTH, 2, SSD_HEADS, SSD_P, SSD_N), 0.1),
        "state_gdn": nrm((DEC_BATCH, DEPTH, 2, GDN_HEADS, GDN_DK, GDN_DV), 0.1),
        "c": nrm((DEC_BATCH, D), 1.0),
        "c_ctx": nrm((D,), 1.0),
        "norm1_g": gain((DEPTH, D)),
        "norm2_g": gain((DEPTH, D)),
        "ada_w": nrm((DEPTH, D, 6 * D), 0.01),
        "ada_b": nrm((DEPTH, 6 * D), 0.02),
        "w_in": nrm((DEPTH, D, D_IN), D ** -0.5),
        "conv_w": nrm((DEPTH, SHORT_CONV_W, D_CONV), SHORT_CONV_W ** -0.5),
        "conv_b": nrm((DEPTH, D_CONV), 0.02),
        "hy_w1": nrm((DEPTH, HY_POS_DIM, HY_FILTER_HIDDEN), HY_POS_DIM ** -0.5),
        "hy_b1": nrm((DEPTH, HY_FILTER_HIDDEN), 0.02),
        "hy_w2": nrm((DEPTH, HY_FILTER_HIDDEN, HY_FILTER_HIDDEN), HY_FILTER_HIDDEN ** -0.5),
        "hy_b2": nrm((DEPTH, HY_FILTER_HIDDEN), 0.02),
        "hy_w3": nrm((DEPTH, HY_FILTER_HIDDEN, 2 * HY_ORDER * D_BRANCH), 0.02 * HY_FILTER_HIDDEN ** -0.5),
        "hy_bias": nrm((DEPTH, HY_ORDER, D_BRANCH), 0.1),
        "hg_lb": nrm((2, DEPTH, HG_HEADS * HG_DK), 1.0),
        "hg_norm": gain((DEPTH, HG_DV)),
        "ssd_a_log": a_log((DEPTH, 2, SSD_HEADS)),
        "ssd_dt_bias": dt_bias((DEPTH, 2, SSD_HEADS)),
        "ssd_d": 1.0 + nrm((DEPTH, SSD_HEADS), 0.1),
        "ssd_norm": gain((DEPTH, D_BRANCH)),
        "gdn_a_log": a_log((DEPTH, 2, GDN_HEADS)),
        "gdn_dt_bias": dt_bias((DEPTH, 2, GDN_HEADS)),
        "gdn_norm": gain((DEPTH, GDN_DV)),
        "w_branch": nrm((DEPTH, N_BRANCH, D_BRANCH, D), D_BRANCH ** -0.5),
        "w_out": nrm((DEPTH, D, D), D ** -0.5),
        "router_w": nrm((DEPTH, D, N_EXPERTS), D ** -0.5),
        "router_bias": nrm((DEPTH, N_EXPERTS), 0.01),
        "exp_w1": nrm((DEPTH, N_EXPERTS, D, D_EXPERT), D ** -0.5),
        "exp_w3": nrm((DEPTH, N_EXPERTS, D, D_EXPERT), D ** -0.5),
        "exp_w2": nrm((DEPTH, N_EXPERTS, D_EXPERT, D), D_EXPERT ** -0.5),
        "sh_w1": nrm((DEPTH, D, D_SHARED), D ** -0.5),
        "sh_w3": nrm((DEPTH, D, D_SHARED), D ** -0.5),
        "sh_w2": nrm((DEPTH, D_SHARED, D), D_SHARED ** -0.5),
        "final_g": gain((D,)),
    }

def reference(x_prompt, x_sample, state_hgrn, state_ssd, state_gdn, c, c_ctx,
              norm1_g, norm2_g, ada_w, ada_b, w_in, conv_w, conv_b,
              hy_w1, hy_b1, hy_w2, hy_b2, hy_w3, hy_bias,
              hg_lb, hg_norm, ssd_a_log, ssd_dt_bias, ssd_d, ssd_norm,
              gdn_a_log, gdn_dt_bias, gdn_norm, w_branch, w_out,
              router_w, router_bias, exp_w1, exp_w3, exp_w2, sh_w1, sh_w3, sh_w2, final_g):
    lb = _hgrn_lower_bounds(hg_lb)
    layers = [dict(norm1_g=norm1_g[l], norm2_g=norm2_g[l], ada_w=ada_w[l], ada_b=ada_b[l],
                   w_in=w_in[l], conv_w=conv_w[l], conv_b=conv_b[l],
                   hy_w1=hy_w1[l], hy_b1=hy_b1[l], hy_w2=hy_w2[l], hy_b2=hy_b2[l], hy_w3=hy_w3[l], hy_bias=hy_bias[l],
                   hg_norm=hg_norm[l], ssd_a_log=ssd_a_log[l], ssd_dt_bias=ssd_dt_bias[l], ssd_d=ssd_d[l],
                   ssd_norm=ssd_norm[l], gdn_a_log=gdn_a_log[l], gdn_dt_bias=gdn_dt_bias[l], gdn_norm=gdn_norm[l],
                   w_branch=w_branch[l], w_out=w_out[l], router_w=router_w[l], router_bias=router_bias[l],
                   exp_w1=exp_w1[l], exp_w3=exp_w3[l], exp_w2=exp_w2[l],
                   sh_w1=sh_w1[l], sh_w3=sh_w3[l], sh_w2=sh_w2[l]) for l in range(DEPTH)]

    x = x_prompt
    bp = x.shape[0]
    cond_ctx = jnp.broadcast_to(c_ctx, (bp, D_MODEL))
    zero_hg = jnp.zeros((bp, 2, HG_HEADS, HG_DK, HG_DV), F32)
    zero_ssd = jnp.zeros((bp, 2, SSD_HEADS, SSD_P, SSD_N), F32)
    zero_gdn = jnp.zeros((bp, 2, GDN_HEADS, GDN_DK, GDN_DV), F32)
    hg_states, ssd_states, gdn_states = [], [], []
    for l in range(DEPTH):
        x, s_hg, s_ssd, s_gdn = _layer(x, cond_ctx, zero_hg, zero_ssd, zero_gdn, layers[l], lb[:, l], False)
        hg_states.append(s_hg)
        ssd_states.append(s_ssd)
        gdn_states.append(s_gdn)
    y_prompt = _rmsnorm(x, final_g)
    new_state_hgrn = jnp.stack(hg_states, axis=1).astype(x_prompt.dtype)
    new_state_ssd = jnp.stack(ssd_states, axis=1).astype(x_prompt.dtype)
    new_state_gdn = jnp.stack(gdn_states, axis=1).astype(x_prompt.dtype)

    x = x_sample
    for l in range(DEPTH):
        x, _, _, _ = _layer(x, c, state_hgrn[:, l], state_ssd[:, l], state_gdn[:, l], layers[l], lb[:, l], True)
    y_sample = _rmsnorm(x, final_g)
    return (y_prompt, y_sample, new_state_hgrn, new_state_ssd, new_state_gdn)


_drawn_inputs = setup_inputs


def setup_inputs(seed=0):
    import zlib

    import numpy as np

    out = dict(_drawn_inputs(seed))
    spreads = {}
    factors = {'state_hgrn': 64.0,
     'state_gdn': 3.6,
     'norm2_g': 2.954,
     'hy_w1': 8.0,
     'hy_b1': 8.0,
     'hy_w2': 8.0,
     'hy_b2': 8.0,
     'hy_w3': 8.0,
     'hy_bias': 8.0,
     'hg_norm': 8.0,
     'ssd_d': 6.442,
     'ssd_norm': 8.0,
     'gdn_norm': 8.0,
     'final_g': 7.355}
    for name, (base, spread) in spreads.items():
        noise = np.random.default_rng([zlib.crc32(name.encode()), seed]).standard_normal(out[name].shape)
        drawn = base * np.exp(spread * noise) if base else spread * noise
        out[name] = __import__('jax').numpy.asarray(drawn.astype(out[name].dtype))
    for name, factor in factors.items():
        out[name] = (out[name] * factor).astype(out[name].dtype)
    return out
```

```python
import math
from contextlib import ExitStack

import numpy as np
import concourse.bass as bass
from concourse import mybir

P = 128
D = 1024
KD = D // P
NT = 3
T = NT * P
W = 512
CW = W // P
GRID = 64
EPS = 1e-6
FLOOR = 1e-30
HG_H, SSD_H, GDN_H = 4, 8, 4
NE, NGRP, TOPG, TOPK, FE = 64, 8, 4, 8, 256
ROUTED = 2.5
NEG = -1e30
LEVELS = 7
FWD, BWD = 0, 1
LN_LOW = 2.0 ** -60
LN_LIFT = 40
ROUND = 1.5 * 2.0 ** 23
TAU_HI = 6.28125
TAU_LO = 2 * math.pi - TAU_HI
PI32 = 3.1415925
TAKEN = -3e38
COL = dict(hy_v=0, hy_x1=512, hy_x2=1024, ssd_x=1536, ssd_bc=2048, gdn_q=2560, gdn_k=3072, gdn_v=3584,
           hg_q=4096, hg_ff=4608, hg_fb=5120, hg_v=5632, hg_g=6144, ssd_z=6656, ssd_dt=7168,
           gdn_g=7184, gdn_ab=7696, merge=7712)

F32 = mybir.dt.float32
U32 = mybir.dt.uint32
ALU = mybir.AluOpType
ACT = mybir.ActivationFunctionType
AX = mybir.AxisListType.X


def shape_tables():
    i = np.arange(P)
    r, t = i[:, None], i[None, :]
    out = {"t_ident": np.eye(P)}
    out["t_sums"] = np.stack([r <= t, r >= t, r > t, r < t, r >= 0 * t], 1)
    out["t_reach"] = np.stack([np.where(m, 0.0, NEG) for m in (r <= t, r >= t, r < t, r > t)], 1)
    lev = np.zeros((P, 2, LEVELS, P))
    for l in range(LEVELS):
        m = 1 << l
        left_s, right_t = (r // m) % 2 == 0, (t // m) % 2 == 1
        lev[:, FWD, l] = (r // (2 * m) == t // (2 * m)) & left_s & right_t
        lev[:, BWD, l] = lev[:, FWD, l].T
    out["t_levels"] = lev
    for L in (P, 2 * P):
        n = np.arange(L)
        th = np.pi * (n[None, :] + 0.5) * n[:, None] / L
        c, s = np.cos(th), np.sin(th)
        for name, m in (("cos", c), ("sin", s), ("icos", c.T / L), ("isin", -s.T / L)):
            out[f"t_{name}{L}"] = m.reshape(L // P, P, L).transpose(1, 0, 2)
    feats, win = [], []
    for L in (P, 2 * P):
        t_ = np.arange(L, dtype=np.float32) / np.float32(L)
        bands = np.arange(1, 17, dtype=np.float32)
        ang = (np.float32(2.0 * math.pi) * t_[:, None] * bands).astype(np.float32)
        feats.append(np.concatenate([t_[:, None], np.sin(ang), np.cos(ang)], 1).T)
        deltas = np.linspace(math.log(1e-2) / 1.5, math.log(1e-2) / 0.3, W)
        w = np.exp(-t_[:, None].astype(np.float64) * np.abs(deltas))
        wa = w.copy()
        wa[0] = 0.0
        win.append(np.stack([w, wa], 1).reshape(L // P, P, 2, W).transpose(1, 0, 2, 3))
    out["t_before"] = np.tril(np.ones((NGRP, NGRP)), -1).reshape(-1)
    out["t_feats"] = np.concatenate(feats, 1)
    out["t_window"] = np.concatenate(win, 1)
    return {k: np.ascontiguousarray(v, dtype=np.float32) for k, v in out.items()}


class Signal:

    def __init__(self, ctx, nc, name):
        self.sem, self.n = ctx.enter_context(nc.semaphore(name)), 0

    def on(self, ins, by=1):
        self.n += by
        ins.then_inc(self.sem, by)


class Lane:

    def __init__(self, eng, signal):
        self.eng, self.own = eng, signal

    def do(self, ins):
        self.own.on(ins)

    def wait_own(self):
        self.eng.wait_ge(self.own.sem, self.own.n)

    def link(self, ins):
        self.do(ins)
        self.wait_own()


class Banks:

    def __init__(self, ctx, nc, psum):
        self.psum, self.jobs, self.now = psum, {}, []
        self.filled = ctx.enter_context(nc.semaphore("bank_filled"))
        self.freed = {by: ctx.enter_context(nc.semaphore(f"bank_freed_{by}")) for by in ("act", "dve")}
        self.count = {"act": 0, "dve": 0}
        self.seen = {"act": 0, "dve": 0}

    def open(self, pe, key, by):
        j = len(self.now)
        assert key not in self.jobs, key
        self.count[by] += 1
        self.jobs[key] = (j, by, self.count[by])
        self.now.append(key)
        if j >= 8:
            _, last_by, n = self.jobs[self.now[j - 8]]
            pe.wait_ge(self.freed[last_by], n)
        return self.psum[:, j % 8, :]

    def close(self, ins):
        ins.then_inc(self.filled, 1)

    def at(self, eng, key):
        j = self.jobs[key][0]
        eng.wait_ge(self.filled, j + 1)
        return self.psum[:, j % 8, :]

    def look(self, key):
        return self.psum[:, self.jobs[key][0] % 8, :]

    def free(self, ins, key):
        _, by, n = self.jobs[key]
        self.seen[by] += 1
        assert self.seen[by] == n, (key, by, n, self.seen[by])
        ins.then_inc(self.freed[by], 1)

    def emptied(self, eng, key):
        _, by, n = self.jobs[key]
        eng.wait_ge(self.freed[by], n)


def decay(mm, banks, pe, key, ident, mask, heads, betas=None):
    ps = banks.open(pe, key, "act").rearrange("p (h t) -> p h t", h=4)
    last = mm(ps, lhsT=ident[:, :], rhs=mask[:, None, :].to_broadcast([P, 4, P]), start=True, stop=False)
    for h, (c, tri) in enumerate(heads):
        last = mm(ps[:, h, :], lhsT=c.to_broadcast([P, P]), rhs=tri, start=False, stop=h == 3 and not betas)
    for h, c in enumerate(betas or []):
        last = mm(ps[:, h, :], lhsT=c.to_broadcast([P, P]), rhs=ident[:, :], start=False, stop=h == 3)
    banks.close(last)


def trunk(nc, a, o):
    ctx = ExitStack()
    with ctx:
        def sb(name, *shape, dt=F32):
            return ctx.enter_context(nc.sbuf_tensor(name, list(shape), dt))

        def sig(name):
            return Signal(ctx, nc, name)

        psum = ctx.enter_context(nc.psum_tensor("banks", [P, 8, 512], F32))
        banks = Banks(ctx, nc, psum)
        gates_dram = nc.dram_tensor("expert_gates", (NE + 1, T), F32).ap()

        x = sb("x", P, NT, D)
        hT = sb("hT", P, KD, T)
        SLABS, SLAB = 4, 2048
        ring = sb("ring", P, SLABS, SLAB)
        mixed = sb("mixed", P, KD, T)
        early = mixed[:, :, :].rearrange("p k t -> p (k t)")
        hbias = early[:, 0:2 * W].rearrange("p (o n) -> p o n", o=2)
        rows = early[:, 1024:1280].rearrange("p (i n) -> p i n", i=2)
        fw1, fw2 = early[0:64, 1280:1344], early[0:64, 1344:1408]
        yT = sb("yT", P, 2, CW, T)
        gate = sb("gate", P, 2, T)
        lifted = sb("lifted", P, 2, T)
        ident = sb("ident", P, P)
        sums = sb("sums", P, 5, P)
        reach = sb("reach", P, 4, P)
        levels = sb("levels", P, 2, LEVELS, P)
        cols = sb("cols", P, 2, P)
        cond = sb("cond", P, KD, 2)
        sq = sb("sq", P, W)
        beta = sb("beta", P, NT, 8)
        bdec = sb("bdec", P, NT, 8)
        dte = sb("dte", P, NT, 16)
        mod = sb("mod", P, 6 * KD, 2)
        scale1 = sb("scale1", P, 2, KD, 2)
        lb = sb("lb", P, 4, 8)
        ss = sb("ss", P, 64)
        small = sb("small", P, NT, 32)
        small2 = sb("small2", P, NT, 32)
        small_row = sb("small_row", P, 2, 32)
        sign_row = sb("sign_row", P, 32)
        cum = sb("cum", P, NT, 5, 32)
        ecum = sb("ecum", P, NT, 5, 32)
        coef = sb("coef", P, 4, 16)
        norm_row = sb("norm_row", P, 2, P)
        ssd_row = sb("ssd_row", P, W + 8)
        hidf = sb("hidf", 64, 4, T)
        fbias = sb("fbias", 64, 2)
        smallw = sb("smallw", P, KD, 32)
        ARENA = 23040
        arena = sb("arena", P, ARENA)

        def part(at, *shape):
            n = int(np.prod(shape))
            assert at + n <= ARENA, (at, n)
            v = arena[:, at:at + n]
            if len(shape) == 1:
                return v
            names = "abcd"[:len(shape)]
            return v.rearrange(f"p ({' '.join(names)}) -> p {' '.join(names)}", **dict(zip(names, shape)))

        U = CW * T
        dft1 = part(0, 4, P)
        dft2 = part(512, 4, 2, 2 * P)
        hf = part(2560, 2, NT, 2, W)
        window = part(8704, NT, 2, W)
        sd = part(11776, 2, 2, NT, W)
        fnet = part(17920, 4, T)
        fw3 = part(19456, 4 * W)
        hyT = part(8704, 3, CW, T)
        hyN = part(8704 + 3 * U, 2, NT, W)
        spec = part(8704 + 5 * U, NT, 2, W)
        hy_t = part(8704 + 7 * U, 4, W)
        normed2 = (part(8704, 2, D), part(12288, 2, D))
        hq = part(0, CW, T)
        hk = part(U, 2, CW, T)
        hb = part(3 * U, 2, CW, T)
        he = part(5 * U, 2, CW, T)
        hqk = part(7 * U, 2, CW, T)
        hv = part(9 * U, NT, W)
        hg = part(10 * U, NT, W)
        hattn = part(11 * U, NT, HG_H, P)
        resets = part(11 * U, U)
        hqe = hb[:, :, :, P:T]
        hst = part(12 * U, 2, 2, HG_H, P)
        hnew = part(12 * U + 2048, 2, HG_H, P)
        hke = part(5 * U, 2, 2, HG_H, P)
        hkn = part(7 * U, 2, 2, HG_H, P)
        hyn = part(5 * U, NT, W)
        sxT = part(0, 2, CW, T)
        sxN = part(2 * U, NT, W)
        sz = part(3 * U, NT, W)
        sbN = part(4 * U, NT, 2, P)
        sdec = part(5 * U, 2, 2, 4, P)
        sxd = part(6 * U + 512, 2, W)
        s_in = part(8 * U, 2, 4, P)
        sst = part(9 * U, 2, 2, W)
        snew = part(11 * U, 2, 4, P)
        sy = part(12 * U, 5, W)
        sy_out = part(12 * U + 5 * W, NT, W)
        gT = part(0, 3, CW, T)
        gqe = part(2 * U, 2, GDN_H, 2 * P)
        gs0 = part(2 * U + 2048, 2, GDN_H, P)
        gN = part(3 * U, 3, NT, W)
        gz = part(6 * U, NT, W)
        gqk = part(7 * U, NT, 2, GDN_H, P)
        gvn = part(9 * U, NT, 2, GDN_H, P)
        gw = part(11 * U, 2, 5, GDN_H, P)
        gs1 = part(11 * U + 5120, 2, GDN_H, P)
        gyn = part(0, NT, W)
        wexp = part(0, 2, 3, SLAB)
        hid = part(12288, 2, 2, T)
        egate = part(13824, 2, T)
        sil = part(14592, 2, T)
        g1row = part(15360, 2, D)
        g2row = part(17408, 2, D)
        fg_row = part(19456, D)
        pick = part(20480, 8, NE)
        router_w = part(20992, KD, NE)
        egN = gate[:, 0, 0:NT * NE].rearrange("p (t e) -> p t e", t=NT)

        small_cols = {"ssd": (slice(0, 8), slice(8, 16)), "gdn": (slice(16, 20), slice(20, 24)),
                      "beta": (slice(24, 28), slice(28, 32))}
        tok = [slice(t * P, (t + 1) * P) for t in range(NT)]
        SECOND = {FWD: 2, BWD: 1}
        FIRST = {FWD: 1, BWD: 2}
        cmod = [0, 1, 1]

        s_const = sig("constants_landed")
        s_vec = sig("vectors_landed")
        s_fconst = sig("filter_tables_landed")
        s_row = sig("rows_landed")
        s_x = sig("tokens_landed")
        s_state = sig("states_landed")
        s_out = sig("outputs_stored")
        s_slab = [sig(f"slab{i}_landed") for i in range(SLABS)]
        s_act, s_dve, s_pool = sig("act_step"), sig("dve_step"), sig("pool_step")
        s_cond = sig("cond_ready")
        s_sin = sig("filter_layer_ready")
        s_sd = sig("filters_ready")
        s_conv = sig("conv_centre_ready")
        s_silu = sig("silu_group_ready")
        s_spec = sig("spectrum_ready")
        s_ss = sig("squares_summed")
        s_rcp = sig("reciprocals_ready")
        s_sg = sig("ssd_output_gated")
        s_x2 = sig("residual_added")
        s_y = sig("moe_added")
        s_fin = sig("tokens_finished")
        s_madd = sig("branch_terms_added")
        s_hgn = sig("gates_times_norms")
        s_gsil = sig("silu_times_gate")
        s_hreset = sig("scan_resets_ready")
        s_rs = sig("roots_ready")
        s_pre = sig("root_arguments_ready")
        s_mod = sig("modulation_ready")
        s_normed = sig("tokens_normalised")
        s_arg = sig("sine_arguments_ready")
        s_hf = sig("forget_gate_argument")
        s_hlog = sig("forget_gate_logs")
        s_hd = sig("level_decays_asked")
        s_he = sig("level_decays_ready")
        s_hqk = sig("level_factors_ready")
        s_hsum = sig("keys_summed")
        s_hke = sig("keys_to_end_ready")
        s_hqe = sig("queries_decayed")
        s_hx = sig("state_decays_asked")
        s_hy = sig("state_decays_ready")
        s_sp = sig("softplus_steps")
        s_spa = sig("softplus_exps")
        s_small = sig("log_decays_ready")
        s_ecum = sig("decay_exps_ready")
        s_sxe = sig("ssd_inputs_to_end_ready")
        s_sw = sig("ssd_weights_ready")
        s_dec = sig("decay_matrices_ready")
        s_gnorm = sig("delta_qk_normalised")
        s_glevel = [sig(f"delta_level_{d}") for d in "fb"]
        s_gat = [sig(f"delta_a_{d}") for d in "fb"]
        s_gvk = [sig(f"delta_values_keys_{d}") for d in "fb"]
        s_gqe = sig("delta_queries_decayed")
        s_yn2 = sig("ssd_output_ready")
        s_gadd = sig("lifted_term_ready")
        s_lb = sig("bound_logits_shifted")
        s_lbe = sig("bound_exps_ready")
        s_hst = sig("hgrn_states_landed")
        s_sst = sig("ssd_states_landed")
        s_gst = sig("delta_states_landed")
        s_late = sig("late_rows_landed")
        s_gates = sig("expert_gates_ready")
        s_gstore = sig("expert_gates_stored")
        s_w13 = [sig(f"up_weights{i}_landed") for i in range(2)]
        s_w2 = [sig(f"down_weights{i}_landed") for i in range(2)]
        s_eg = [sig(f"gate_row{i}_landed") for i in range(2)]
        s_h1, s_h3 = sig("gate_units_ready"), sig("up_units_ready")
        s_sil, s_hid, s_down = sig("silu_ready"), sig("hidden_ready"), sig("expert_added")
        s_store = sig("states_staged")

        w_in, ada = a["w_in"][0], a["ada_w"][0]

        def cols_of(w, c0, n=256):
            return w[:, c0:c0 + n].rearrange("(k p) n -> p k n", p=P)

        slab_plan = []
        for i in range(8):
            slab_plan.append((("ada", i), cols_of(ada, i * 256)))

        def plan(name, halves=2):
            for h in range(halves):
                slab_plan.append(((name, h), cols_of(w_in, COL[name] + h * 256)))

        def plan_lift(n):
            for h in range(4):
                if h % 2 == 0:
                    slab_plan.append((("wb", n, h // 2), a["w_branch"][0, n][:, h // 2 * W:h // 2 * W + W]
                                      .rearrange("(k p) n -> p k n", p=P)))
                slab_plan.append((("merge", n, h), cols_of(w_in, COL["merge"] + n * D + h * 256)))

        for name in ("hy_v", "hy_x1", "hy_x2"):
            plan(name)
        for i in range(8, 24):
            slab_plan.append((("ada", i), cols_of(ada, i * 256)))
        for name in ("hg_q", "hg_ff", "hg_fb", "hg_v", "hg_g"):
            plan(name)
        plan_lift(0)
        for name in ("ssd_x", "ssd_bc", "ssd_z"):
            plan(name)
        plan_lift(1)
        for name in ("gdn_q", "gdn_k", "gdn_v", "gdn_g"):
            plan(name)
        plan_lift(2)
        plan_lift(3)
        for c in range(4):
            slab_plan.append((("w_out", c), cols_of(a["w_out"][0], c * 256)))
        slab_at = {name: i for i, (name, _) in enumerate(slab_plan)}
        slab_last = {}

        def slab(pe, name, kd=KD):
            i = slab_at[name]
            pe.wait_ge(s_slab[i % SLABS].sem, 16 * (i // SLABS + 1))
            return ring[:, i % SLABS, :].rearrange("p (k n) -> p k n", k=kd)

        def slab_done(*names):
            for name in names:
                slab_last[slab_at[name]] = len(banks.now)

        SQ = {"norm": (0, 12), "ho": 3, "ssd": 6, "go": 9, "last": 15}
        N_IDENT, N_CONST, N_VEC, N_FCONST, N_LATE, N_ROW = 1, 4, 8, 16, 4, 10
        ROOT = {"norm": (1, 12), "hg": 2, "ssd": 5, "qk": 8, "gdn": 9, "last": 13}

        block = ctx.enter_context(nc.Block())

        @block.tensor
        def _(pe):
            mm = nc.tensor.matmul

            def contract(out, pairs):
                for i, (lhsT, rhs) in enumerate(pairs):
                    last = mm(out, lhsT=lhsT, rhs=rhs, start=i == 0, stop=i == len(pairs) - 1)
                return last

            def flip4(key, by, sources, n=P):
                ps = banks.open(pe, key, by)
                for i, src in enumerate(sources):
                    last = nc.tensor.transpose(ps[0:n, i * P:(i + 1) * P], src, ident[:, :])
                banks.close(last)

            def project_T(name, by):
                for c in range(CW):
                    w = slab(pe, (name, c // 2))
                    ps = banks.open(pe, (name, c), by)
                    banks.close(contract(ps[:, 0:T], [
                        (w[:, k, c % 2 * P:c % 2 * P + P], hT[:, k, :]) for k in range(KD)]))
                    if c % 2:
                        slab_done((name, c // 2))

            def project_N(name, by):
                w = [slab(pe, (name, h)) for h in range(2)]
                for t in range(NT):
                    ps = banks.open(pe, (name, t), by)
                    for h in range(2):
                        last = contract(ps[:, h * 256:(h + 1) * 256],
                                        [(hT[:, k, tok[t]], w[h][:, k, :]) for k in range(KD)])
                    banks.close(last)
                slab_done((name, 0), (name, 1))

            def ada_columns(lo, hi):
                for i in range(lo, hi):
                    w = slab(pe, ("ada", i))
                    ps = banks.open(pe, ("ada", i), "dve")
                    for c in range(2):
                        last = contract(ps[:, c * 2:c * 2 + 2],
                                        [(w[:, k, c * P:c * P + P], cond[:, k, :]) for k in range(KD)])
                    banks.close(last)
                    slab_done(("ada", i))

            def flip_tokens(which):
                for t in range(NT):
                    pe.wait_ge(s_normed.sem, which * NT + t + 1)
                    for h in range(2):
                        flip4((which, "xt", t, h), ("act", "dve")[h],
                              [normed2[which][:, t % 2, (h * 4 + i) * P:(h * 4 + i + 1) * P] for i in range(4)])

            def lift(n, lo, hi):
                for j in range(lo, hi):
                    w = slab(pe, ("merge", n, j // 2))
                    ps = banks.open(pe, ("merge", n, j), "act")
                    banks.close(contract(ps[:, 0:T], [
                        (w[:, k, j % 2 * P:j % 2 * P + P], hT[:, k, :]) for k in range(KD)]))
                    if j % 2:
                        slab_done(("merge", n, j // 2))
                    wb = slab(pe, ("wb", n, j // 4), CW)
                    if j == 0:
                        banks.emptied(pe, ("yt", n, NT - 1)) if n else banks.emptied(pe, ("yo", CW - 1))
                    ps = banks.open(pe, ("lift", n, j), "dve")
                    banks.close(contract(ps[:, 0:T], [
                        (wb[:, c, j % 4 * P:j % 4 * P + P], yT[:, n % 2, c, :]) for c in range(CW)]))
                    if j % 4 == 3:
                        slab_done(("wb", n, j // 4))

            def flip_output(n, src):
                for t in range(NT):
                    if n == 2:
                        pe.wait_ge(s_yn2.sem, t + 1)
                    else:
                        banks.emptied(pe, ({1: "ho", 3: "go"}[n], t))
                    flip4(("yt", n, t), "act", [src[:, t, c * P:(c + 1) * P] for c in range(CW)])

            pe.wait_ge(s_const.sem, 16 * N_IDENT)
            pe.wait_ge(s_vec.sem, 16 * N_VEC)
            for i in range(2):
                ps = banks.open(pe, ("pack", i), "act")
                n = (P, 88)[i]
                banks.close(nc.tensor.transpose(ps[:, 0:n], rows[0:n, i, :], ident[0:n, 0:n]))

            pe.wait_ge(s_fconst.sem, 16 * N_FCONST)
            ps = banks.open(pe, "f1", "dve")
            banks.close(mm(ps[0:64, 0:T], lhsT=fw1[0:33, :], rhs=fnet[0:33, 0, :], start=True, stop=True))
            pe.wait_ge(s_sin.sem, 1)
            ps = banks.open(pe, "f2", "dve")
            banks.close(mm(ps[0:64, 0:T], lhsT=fw2[0:64, :], rhs=fnet[0:64, 1, :], start=True, stop=True))
            pe.wait_ge(s_sin.sem, 2)
            for t in range(NT):
                for order in range(2):
                    for way in range(2):
                        ps = banks.open(pe, ("filt", t, order, way), "dve")
                        banks.close(mm(ps, lhsT=fnet[0:64, 2, tok[t]], start=True, stop=True,
                                       rhs=fw3[0:64, (way * 2 + order) * W:(way * 2 + order + 1) * W]))
            pe.wait_ge(s_sd.sem, 2 * NT)

            def spectrum(out, ft, ri, src):
                if ft == 0:
                    return contract(out, [(dft1[:, ri, :], src[0])])
                f = tok[ft - 1]
                return contract(out, [(dft2[:, ri, kt, f], src[1 + kt]) for kt in range(2)])

            for order in range(2):
                for ft in range(NT):
                    for ri in range(2):
                        ps = banks.open(pe, ("H", order, ft, ri), "dve" if ri == 0 else "act")
                        banks.close(spectrum(ps, ft, ri, [sd[:, order, ri, t, :] for t in range(NT)]))

            pe.wait_ge(s_cond.sem, 1)
            ada_columns(0, 8)
            flip_tokens(0)
            banks.emptied(pe, (0, "xt", NT - 1, 0))
            banks.emptied(pe, (0, "xt", NT - 1, 1))
            for name in ("hy_v", "hy_x1", "hy_x2"):
                project_T(name, "dve")
            ada_columns(8, 24)

            for i, name in enumerate(("hy_v", "hy_x1")):
                banks.emptied(pe, (name, CW - 1))
                for t in range(NT):
                    flip4(("hyt", i, t), "act", [hyT[:, i, c, tok[t]] for c in range(CW)])
            for order in range(2):
                if order == 0:
                    banks.emptied(pe, ("hyt", 0, NT - 1))
                else:
                    banks.emptied(pe, ("y", NT - 1))
                for ft in range(NT):
                    for ri in range(2):
                        ps = banks.open(pe, ("U", order, ft, ri), "dve")
                        banks.close(spectrum(ps, ft, ri, [hyN[:, 0, t, :] for t in range(NT)]))
                pe.wait_ge(s_spec.sem, (order + 1) * NT)
                if order == 0:
                    for t in range(NT):
                        ps = banks.open(pe, ("y", t), "dve")
                        if t == 0:
                            pairs = [(dft1[:, 2 + ri, :], spec[:, 0, ri, :]) for ri in range(2)]
                        else:
                            pairs = [(dft2[:, 2 + ri, ft, tok[t - 1]], spec[:, 1 + ft, ri, :])
                                     for ft in range(2) for ri in range(2)]
                        banks.close(contract(ps, pairs))
            for c in range(CW):
                ch = slice(c * P, (c + 1) * P)
                ps = banks.open(pe, ("yo", c), "dve")
                contract(ps[:, 0:P], [(spec[:, 0, ri, ch], dft1[:, 2 + ri, :]) for ri in range(2)])
                banks.close(contract(ps[:, P:T], [(spec[:, 1 + ft, ri, ch], dft2[:, 2 + ri, ft, :])
                                                  for ft in range(2) for ri in range(2)]))

            for name in ("hg_q", "hg_ff", "hg_fb"):
                project_T(name, "act")
            for name in ("hg_v", "hg_g"):
                project_N(name, "act")

            pe.wait_ge(s_const.sem, 16 * N_CONST)
            for i in range(2 * LEVELS):
                pe.wait_ge(s_hqk.sem, i + 1)
                for t in range(NT):
                    ps = banks.open(pe, ("level", i, t), "dve")
                    for h in range(HG_H):
                        last = mm(ps[:, h * P:(h + 1) * P], lhsT=hqk[:, i % 2, h, tok[t]],
                                  rhs=hqk[:, i % 2, h, tok[t]], start=True, stop=True)
                    banks.close(last)
                if i < 2 * LEVELS - 6:
                    lift(0, i, i + 1)
            pe.wait_ge(s_hsum.sem, 1)
            for t in range(NT):
                ps = banks.open(pe, ("diag", t), "dve")
                for h in range(HG_H):
                    last = mm(ps[:, h * P:(h + 1) * P], lhsT=hk[:, 0, h, tok[t]], rhs=hq[:, h, tok[t]],
                              start=True, stop=True)
                banks.close(last)
            pe.wait_ge(s_hke.sem, 1)
            for d in range(2):
                for w in range(2):
                    flip4(("hke", d, w), "act", [hke[:, d, w, h, :] for h in range(HG_H)])
            for d in range(2):
                for w, t in ((0, 0), (1, FIRST[d])):
                    banks.emptied(pe, ("hke", d, w))
                    ps = banks.open(pe, ("hstate", d, w), "dve")
                    for h in range(HG_H):
                        last = mm(ps[:, h * P:(h + 1) * P], lhsT=hkn[:, d, w, h, :],
                                  rhs=hv[:, t, h * P:(h + 1) * P], start=True, stop=True)
                    banks.close(last)
            pe.wait_ge(s_hqe.sem, 1)
            pe.wait_ge(s_hst.sem, 32)
            for t in range(NT):
                banks.emptied(pe, ("diag", t))
                if t:
                    banks.emptied(pe, ("hstate", 1, 1))
                ps = banks.open(pe, ("ho", t), "dve")
                for h in range(HG_H):
                    pairs = [(hattn[:, t, h, :], hv[:, t, h * P:(h + 1) * P])]
                    if t:
                        for d in range(2):
                            pairs.append((hqe[:, d, h, (t - 1) * P:t * P], hst[:, d, int(t == SECOND[d]), h, :]))
                    last = contract(ps[:, h * P:(h + 1) * P], pairs)
                banks.close(last)
            flip_output(1, hyn)

            for name in ("ssd_x", "ssd_bc"):
                project_T(name, "dve")
            project_N("ssd_z", "act")
            pe.wait_ge(s_row.sem, 16 * N_ROW)
            for t in range(NT):
                ps = banks.open(pe, ("small", t), "dve")
                banks.close(contract(ps[:, 0:32], [(hT[:, k, tok[t]], smallw[:, k, :]) for k in range(KD)]))

            for t in range(NT):
                pe.wait_ge(s_small.sem, 1)
                ps = banks.open(pe, ("cum", t), "dve")
                for i in range(5):
                    last = mm(ps[:, i * 32:(i + 1) * 32], lhsT=sums[:, i, :], rhs=small[:, t, :],
                              start=True, stop=True)
                banks.close(last)
            pe.wait_ge(s_silu.sem, 1)
            for t in range(NT):
                flip4(("sx", t), "act", [sxT[:, 0, c, tok[t]] for c in range(CW)])
            pe.wait_ge(s_silu.sem, 2)
            for t in range(NT):
                flip4(("sb", t), "act", [sxT[:, 1, g, tok[t]] for g in range(2)])
            pe.wait_ge(s_sst.sem, 32)
            for d in range(2):
                flip4(("sin", d), "act", [s_in[:, d, i, :] for i in range(4)])

            for d in range(2):
                for w, t in ((0, 0), (1, FIRST[d])):
                    banks.emptied(pe, ("sb", NT - 1))
                    pe.wait_ge(s_sxe.sem, 2 * d + w + 1)
                    ps = banks.open(pe, ("sstate", d, w), "dve")
                    for i in range(4):
                        if w == 0:
                            last = mm(ps[:, i * P:(i + 1) * P], lhsT=sxd[:, w, i * P:(i + 1) * P],
                                      rhs=sbN[:, t, i // 2, :], start=True, stop=True)
                        elif i < 2:
                            last = mm(ps[:, i * 256:(i + 1) * 256], lhsT=sbN[:, t, i, :],
                                      rhs=sxd[:, w, i * 256:(i + 1) * 256], start=True, stop=True)
                    banks.close(last)
            banks.emptied(pe, ("sstate", 1, 1))
            banks.emptied(pe, ("sin", 1))
            for t in range(NT):
                ps = banks.open(pe, ("cb", t), "dve")
                for g in range(2):
                    last = mm(ps[:, g * P:(g + 1) * P], lhsT=sxT[:, 1, g, tok[t]], rhs=sxT[:, 1, 2 + g, tok[t]],
                              start=True, stop=True)
                banks.close(last)
                for d in range(2):
                    for q in range(2):
                        decay(mm, banks, pe, ("sdec", t, d, q), ident, reach[:, d, :],
                              [(small[:, t, small_cols["ssd"][d]][:, q * 4 + h:q * 4 + h + 1], sums[:, d, :])
                               for h in range(4)])
                if t:
                    for d in range(2):
                        ps = banks.open(pe, ("sinter", t, d), "dve")
                        for g in range(2):
                            last = mm(ps[:, g * 256:(g + 1) * 256], lhsT=sxT[:, 1, 2 + g, tok[t]],
                                      rhs=sst[:, d, int(t == SECOND[d]), g * 256:(g + 1) * 256],
                                      start=True, stop=True)
                        banks.close(last)
                pe.wait_ge(s_sw.sem, t + 1)
                ps = banks.open(pe, ("sintra", t), "dve")
                for h in range(SSD_H):
                    last = contract(ps[:, h * 64:(h + 1) * 64],
                                    [(sdec[:, d, h // 4, h % 4, :], sxd[:, d, h * 64:(h + 1) * 64])
                                     for d in range(2)])
                banks.close(last)
                lift(1, (0, 3, 6)[t], (3, 6, 8)[t])
            flip_output(2, sy_out)

            for name in ("gdn_q", "gdn_k", "gdn_v"):
                project_T(name, "dve")
            project_N("gdn_g", "act")
            for i in range(3):
                pe.wait_ge(s_silu.sem, 3 + i)
                for t in range(NT):
                    flip4(("gn", i, t), "act", [gT[:, i, c, tok[t]] for c in range(CW)])
            pe.wait_ge(s_gnorm.sem, 1)
            for i in range(2):
                for t in range(NT):
                    flip4(("gt", i, t), "act", [gN[:, i, t, h * P:(h + 1) * P] for h in range(GDN_H)])
            banks.emptied(pe, ("gt", 1, NT - 1))

            for r in range(NT):
                tt = [r, (0, 2, 1)[r]]
                for d in range(2):
                    t = tt[d]
                    la = small[:, t, small_cols["gdn"][d]]
                    lbeta = small[:, t, small_cols["beta"][d]]
                    for key, mask, beta in (("gincl", d, False), ("gstrict", 2 + d, True)):
                        decay(mm, banks, pe, (key, r, d), ident, reach[:, mask, :],
                              [(la[:, h:h + 1], sums[:, d, :]) for h in range(GDN_H)],
                              [lbeta[:, h:h + 1] for h in range(GDN_H)] if beta else None)
                    for key, i in (("gkk", 1), ("gqk", 0)):
                        ps = banks.open(pe, (key, r, d), "dve")
                        for h in range(GDN_H):
                            last = mm(ps[:, h * P:(h + 1) * P], lhsT=gT[:, 1, h, tok[t]],
                                      rhs=gT[:, i, h, tok[t]], start=True, stop=True)
                        banks.close(last)
                for l in range(LEVELS):
                    for d in range(2):
                        pe.wait_ge(s_glevel[d].sem, r * LEVELS + l + 1)
                        if l == 1:
                            banks.emptied(pe, ("gprod", r, 0, d))
                        elif l:
                            banks.emptied(pe, ("ginv", r, l - 1, d))
                            banks.emptied(pe, ("ginvT", r, l - 1, d))
                        ps = banks.open(pe, ("gprod", r, l, d), "dve" if l == 0 else "act")
                        for h in range(GDN_H):
                            last = mm(ps[:, h * P:(h + 1) * P], lhsT=gw[:, d, 1, h, :],
                                      rhs=ident[:, :] if l == 0 else gw[:, d, 2, h, :], start=True, stop=True)
                        banks.close(last)
                    for d in range(2):
                        if l == 0:
                            continue
                        banks.emptied(pe, ("gprod", r, l, d))
                        if l < LEVELS - 1:
                            ps = banks.open(pe, ("ginv", r, l, d), "dve")
                            for h in range(GDN_H):
                                last = mm(ps[:, h * P:(h + 1) * P], lhsT=gw[:, d, 3, h, :],
                                          rhs=gw[:, d, 4, h, :], start=True, stop=True)
                            banks.close(last)
                        ps = banks.open(pe, ("ginvT", r, l, d), "dve")
                        for h in range(GDN_H):
                            last = mm(ps[:, h * P:(h + 1) * P], lhsT=gw[:, d, 4, h, :],
                                      rhs=gw[:, d, 3, h, :], start=True, stop=True)
                        banks.close(last)
                    if r and l in (2, 3, 4, 5):
                        n = (r - 1) * 4 + l - 2
                        lift(2, n, n + 1)
                for d in range(2):
                    t = tt[d]
                    banks.emptied(pe, ("ginvT", r, LEVELS - 1, d))
                    pe.wait_ge(s_gvk[d].sem, r + 1)
                    if r:
                        ps = banks.open(pe, ("gwT", r, d), "act")
                        for h in range(GDN_H):
                            last = mm(ps[:, h * P:(h + 1) * P], lhsT=gw[:, d, 4, h, :], rhs=gw[:, d, 3, h, :],
                                      start=True, stop=True)
                        banks.close(last)
                        banks.emptied(pe, ("gwT", r, d))
                        if r == 2:
                            banks.emptied(pe, ("gstate", 1, d))
                        else:
                            pe.wait_ge(s_gst.sem, 32)
                    ps = banks.open(pe, ("gv", r, d), "act")
                    for h in range(GDN_H):
                        pairs = [(gw[:, d, 3, h, :], gw[:, d, 2, h, :])]
                        if r:
                            pairs.append((gw[:, d, 1, h, :], (gs0, gs1)[r - 1][:, d, h, :]))
                        last = contract(ps[:, h * P:(h + 1) * P], pairs)
                    banks.close(last)
                    if r < 2:
                        banks.emptied(pe, ("gv", r, d))
                        ps = banks.open(pe, ("gstate", r, d), "dve")
                        for h in range(GDN_H):
                            last = mm(ps[:, h * P:(h + 1) * P], lhsT=gw[:, d, 0, h, :], rhs=gvn[:, t, d, h, :],
                                      start=True, stop=True)
                        banks.close(last)
            for d in range(2):
                for t in (1, 2):
                    ps = banks.open(pe, ("grow", t, d), "act")
                    for h in range(GDN_H):
                        c = small[:, t, small_cols["gdn"][d]][:, h:h + 1]
                        last = mm(ps[:, h * P:(h + 1) * P], lhsT=c.to_broadcast([P, P]), rhs=sums[:, d, :],
                                  start=True, stop=True)
                    banks.close(last)
            pe.wait_ge(s_gqe.sem, 4)
            for t in range(NT):
                banks.emptied(pe, ("gv", 2, 1))
                ps = banks.open(pe, ("go", t), "dve")
                for h in range(GDN_H):
                    pairs = []
                    for d in range(2):
                        pairs.append((gqk[:, t, d, h, :], gvn[:, t, d, h, :]))
                        if t:
                            pairs.append((gqe[:, d, h, (t - 1) * P:t * P],
                                          (gs0, gs1)[int(t == SECOND[d])][:, d, h, :]))
                    last = contract(ps[:, h * P:(h + 1) * P], pairs)
                banks.close(last)
            flip_output(3, gyn)
            lift(3, 0, 8)

            for g in (2, 5):
                for cnd in range(2):
                    for h in range(2):
                        ps = banks.open(pe, ("grow", g, cnd, h), "act")
                        for i in range(4):
                            c = mod[:, g * KD + h * 4 + i, cnd:cnd + 1]
                            last = mm(ps[:, i * P:(i + 1) * P], lhsT=c.to_broadcast([P, P]), rhs=ident[:, :],
                                      start=True, stop=True)
                        banks.close(last)
            pe.wait_ge(s_madd.sem, 3 * KD)
            for c in range(4):
                w = slab(pe, ("w_out", c))
                for t in range(NT):
                    ps = banks.open(pe, ("out", c, t), "dve")
                    banks.close(contract(ps[:, 0:256], [(mixed[:, k, tok[t]], w[:, k, :]) for k in range(KD)]))
                slab_done(("w_out", c))
            flip_tokens(1)
            banks.emptied(pe, (1, "xt", NT - 1, 0))
            banks.emptied(pe, (1, "xt", NT - 1, 1))
            pe.wait_ge(s_late.sem, 16 * N_LATE)
            for t in range(NT):
                ps = banks.open(pe, ("router", t), "act")
                banks.close(contract(ps[:, 0:NE], [(hT[:, k, tok[t]], router_w[:, k, :]) for k in range(KD)]))
            ps = banks.open(pe, "gateT", "dve")
            for t in range(NT):
                pe.wait_ge(s_gates.sem, t + 1)
                last = nc.tensor.transpose(ps[0:NE, tok[t]], egN[:, t, :], ident[:, :])
            banks.close(last)

            for by in ("act", "dve"):
                pe.wait_ge(banks.freed[by], banks.count[by])

            def hidden(e, slot):
                pe.wait_ge(s_w13[slot].sem, (e - slot) * 16 + 32)
                for f in range(2):
                    for i in range(2):
                        if not (isinstance(e, int) and e == 0 and f == 0):
                            pe.wait_ge((s_sil, s_hid)[i].sem, e * 2 + f)
                        for k in range(KD):
                            w = wexp[:, slot, i, :].rearrange("p (k n) -> p k n", k=KD)
                            last = mm(psum[:, 6 + i, 0:T], lhsT=w[:, k, f * P:(f + 1) * P], rhs=hT[:, k, :],
                                      start=k == 0, stop=k == KD - 1)
                        last.then_inc((s_h1, s_h3)[i].sem, 1)

            def down(e, slot, first=False, final=False):
                pe.wait_ge(s_w2[slot].sem, (e - slot) * 8 + 16)
                pe.wait_ge(s_hid.sem, e * 2 + 2)
                w = wexp[:, slot, 2, :].rearrange("p (f n) -> p f n", f=2)
                for t in range(NT):
                    for h in range(2):
                        for f in range(2):
                            last = mm(psum[:, t * 2 + h, :], lhsT=hid[:, slot, f, tok[t]],
                                      rhs=w[:, f, h * W:(h + 1) * W], start=first and f == 0,
                                      stop=final and f == 1)
                last.then_inc(s_down.sem, 1)

            hidden(0, 0)
            hidden(1, 1)
            down(0, 0, first=True)
            with pe.Fori(1, NE - 1, 2) as e:
                hidden(e + 1, 0)
                down(e, 1)
                hidden(e + 2, 1)
                down(e + 1, 0)
            hidden(NE, 0)
            down(NE - 1, 1)
            down(NE, 0, final=True)

        C0 = {name: COL[name] // P for name in COL if COL[name] < 4096}
        conv_to = {"hy_v": hyT[:, 0], "hy_x1": hyT[:, 1], "hy_x2": hyT[:, 2], "ssd_x": sxT[:, 0],
                   "ssd_bc": sxT[:, 1], "gdn_q": gT[:, 0], "gdn_k": gT[:, 1], "gdn_v": gT[:, 2]}
        conv_order = {name: i for i, name in enumerate(conv_to)}
        silu_order = {name: i for i, name in enumerate(("ssd_x", "ssd_bc", "gdn_q", "gdn_k", "gdn_v"))}
        cwt, cvec = cols[:, 0, :], cols[:, 1, :]
        flat = lambda v: v.rearrange("p a b -> p (a b)")
        halves4 = lambda v: v.rearrange("p (h k) -> p h k", h=4)

        @block.scalar
        def _(act):
            lane = Lane(act, s_act)
            on = nc.scalar.activation

            def copy(out, key, func=ACT.Copy, **kw):
                banks.free(on(out, banks.at(act, key) if "src" not in kw else kw.pop("src"), func, **kw), key)

            def norm_tokens(which):
                for t in range(NT):
                    s_ss.on(on(early[:, t * D:(t + 1) * D], x[:, t, :], ACT.Square,
                               accum_out=ss[:, which * 3 + t:which * 3 + t + 1]))
                act.wait_ge(s_pre.sem, ROOT["norm"][which])
                s_rs.on(on(ss[:, 8 + which * 3:11 + which * 3], ss[:, 8 + which * 3:11 + which * 3], ACT.Sqrt))
                act.wait_ge(s_rcp.sem, which + 1)
                for t in range(NT):
                    if t == 2:
                        banks.at(act, (which, "xt", 0, 1))
                    s_normed.on(on(normed2[which][:, t % 2, :], x[:, t, :], ACT.Copy,
                                   scale=ss[:, 8 + which * 3 + t:9 + which * 3 + t]))
                    if t:
                        modulate(which, t - 1)
                modulate(which, NT - 1)

            def modulate(which, t):
                ps = banks.at(act, (which, "xt", t, 0))
                if t == 0:
                    act.wait_ge(s_mod.sem, which + 1)
                for i in range(4):
                    ins = on(hT[:, i, tok[t]], ps[:, i * P:(i + 1) * P], ACT.Identity,
                             scale=scale1[:, which, i, cmod[t]:cmod[t] + 1],
                             bias=mod[:, which * 24 + i, cmod[t]:cmod[t] + 1])
                    if i < 3:
                        lane.do(ins)
                banks.free(ins, (which, "xt", t, 0))

            def conv_centre(name):
                for c in range(CW):
                    j = C0[name] + c
                    s_conv.on(on(conv_to[name][:, c, :], banks.at(act, (name, c))[:, 0:T], ACT.Identity,
                                 scale=cwt[:, 32 + j:33 + j], bias=cwt[:, 96 + j:97 + j]))

            def silu(name):
                banks.emptied(act, (name, CW - 1))
                v = flat(conv_to[name])
                s_silu.on(on(v, v, ACT.Silu))

            def merge_gate(n, j):
                key = ("merge", n, j)
                ps = banks.at(act, key)
                if j >= 2 or n:
                    banks.emptied(act, ("lift", n, j - 2) if j >= 2 else ("lift", n - 1, j + 6))
                banks.free(on(gate[:, j % 2, :], ps[:, 0:T], ACT.Sigmoid), key)

            def root(i, cols_):
                act.wait_ge(s_pre.sem, i)
                s_rs.on(on(cols_, cols_, ACT.Sqrt))

            def flip_output(n):
                for t in range(NT):
                    ps = banks.at(act, ("yt", n, t))
                    banks.free(on(yT[:, n % 2, :, tok[t]], halves4(ps), ACT.Copy), ("yt", n, t))

            for i in range(2):
                n = (P, 88)[i]
                copy(cols[:, i, 0:n], ("pack", i), src=banks.at(act, ("pack", i))[:, 0:n])
            banks.emptied(act, ("pack", 1))
            s_cond.on(on(cond[:, :, :].rearrange("p k c -> p c k"),
                         cvec[:, 64:80].rearrange("p (c k) -> p c k", c=2), ACT.Silu))
            act.wait_ge(s_lb.sem, 1)
            s_lbe.on(on(lb[:, 0, :], lb[:, 0, :], ACT.Exp))
            for i in range(2):
                act.wait_ge(s_arg.sem, i + 1)
                s_sin.on(on(fnet[0:64, 1 + i, :], fnet[0:64, 3, :], ACT.Sin))
            for order in range(2):
                for ft in range(NT):
                    copy(hf[:, order, ft, 1, :], ("H", order, ft, 1))
            act.wait_ge(s_x.sem, 16 * NT)
            banks.emptied(act, ("H", 1, NT - 1, 0))
            norm_tokens(0)
            for name in ("hy_v", "hy_x1", "hy_x2"):
                conv_centre(name)
            for i in range(2):
                for t in range(NT):
                    copy(hyN[:, i, t, :], ("hyt", i, t))

            banks.emptied(act, ("yo", CW - 1))
            for d in range(2):
                act.dma_start(hst[:, d, 0], a["state_hgrn"][0, 0, d].rearrange("h k v -> k h v")).then_inc(s_hst.sem, 16)
            for c in range(CW):
                key = ("hg_q", c)
                copy(hq[:, c, :], key, ACT.Silu, src=banks.at(act, key)[:, 0:T])
            for d in range(2):
                for c in range(CW):
                    key = (("hg_ff", "hg_fb")[d], c)
                    ps = banks.at(act, key)[:, 0:T]
                    lane.do(on(he[:, d, c, :], ps, ACT.Sigmoid))
                    banks.free(on(hk[:, d, c, :], ps, ACT.Sigmoid, scale=-1.0), key)
            for t in range(NT):
                copy(hv[:, t, :], ("hg_v", t))
            for t in range(NT):
                copy(hg[:, t, :], ("hg_g", t), ACT.Silu)
            for d in range(2):
                act.wait_ge(s_hf.sem, d + 1)
                s_hlog.on(on(flat(he[:, d]), flat(he[:, d]), ACT.Ln))
            for i in range(2 * LEVELS):
                act.wait_ge(s_hd.sem, i + 1)
                s_he.on(on(flat(he[:, i % 2]), flat(he[:, i % 2]), ACT.Exp))
                if 1 <= i <= 8:
                    merge_gate(0, i - 1)
            act.wait_ge(s_hx.sem, 1)
            lane.do(on(arena[:, 5 * U:5 * U + 2048], arena[:, 5 * U:5 * U + 2048], ACT.Exp))
            for d in range(2):
                lane.link(on(coef[:, d, 0:HG_H], hb[:, d, :, (2 * P - 1, 2 * P)[d]], ACT.Exp))
                lane.do(on(hqe[:, d], hb[:, d, :, P:T], ACT.Exp))
            s_hy.on(on(coef[:, 2, 0:4], coef[:, 0, 0:4], ACT.Copy))
            for d in range(2):
                for w in range(2):
                    key = ("hke", d, w)
                    copy(hkn[:, d, w], key, src=halves4(banks.at(act, key)))
            for t in range(NT):
                ps = banks.at(act, ("ho", t))
                if t:
                    banks.emptied(act, ("ho", t - 1))
                s_ss.on(on(sq[:, :], ps, ACT.Square))
                root(ROOT["hg"] + t, ss[:, 16 + 4 * t:20 + 4 * t])
            flip_output(1)

            for name in ("ssd_x", "ssd_bc"):
                if name == "ssd_x":
                    banks.at(act, ("yt", 1, NT - 1))
                    for d in range(2):
                        banks.emptied(act, ("hstate", d, 0))
                        act.dma_start(o["new_hgrn"][0, 0, d].rearrange("h k v -> k h v"), hnew[:, d]).then_inc(s_out.sem, 16)
                    for d in range(2):
                        act.dma_start(s_in[:, d], a["state_ssd"][0, 0, d].rearrange("(a q) p n -> (q p) a n", q=2)).then_inc(s_sst.sem, 16)
                conv_centre(name)
            silu("ssd_x")
            silu("ssd_bc")
            for t in range(NT):
                copy(sz[:, t, :], ("ssd_z", t), ACT.Silu)
            act.wait_ge(s_sp.sem, 1)
            s_spa.on(on(flat(small2[:, :, :]), flat(small2[:, :, :]), ACT.Exp))
            act.wait_ge(s_sp.sem, 2)
            s_spa.on(on(flat(small2[:, :, :]), flat(small2[:, :, :]), ACT.Ln))
            act.wait_ge(s_row.sem, 16 * N_ROW)
            act.wait_ge(s_pool.sem, 3)
            s_spa.on(on(small_row[:, 1, :], small_row[:, 1, :], ACT.Exp))
            banks.emptied(act, ("cum", NT - 1))
            lane.do(on(beta[:, :, :], small2[:, :, 24:32], ACT.Exp, scale=-1.0))
            s_ecum.on(on(ecum[:, :, :, :].rearrange("p a b c -> p (a b c)"),
                         cum[:, :, :, :].rearrange("p a b c -> p (a b c)"), ACT.Exp, scale=-1.0))
            for t in range(NT):
                copy(sxN[:, t, :], ("sx", t))
            for t in range(NT):
                key = ("sb", t)
                copy(sbN[:, t], key, src=banks.at(act, key)[:, 0:256].rearrange("p (g n) -> p g n", g=2))
            for d in range(2):
                copy(sst[:, d, 0, :], ("sin", d))

            def decays(key, out, t, heads, d):
                ps = banks.at(act, key)
                for h in range(4):
                    c = cum[:, t, d, heads.start + h:heads.start + h + 1]
                    ins = on(out[:, h, :], ps[:, h * P:(h + 1) * P], ACT.Exp, bias=c)
                    if h < 3:
                        lane.do(ins)
                banks.free(ins, key)

            for t in range(NT):
                if t:
                    banks.at(act, ("sintra", t - 1))
                for d in range(2):
                    for q in range(2):
                        heads = slice(small_cols["ssd"][d].start + 4 * q, 0)
                        decays(("sdec", t, d, q), sdec[:, d, q], t, heads, d)
                for j in range((0, 3, 6)[t], (3, 6, 8)[t]):
                    merge_gate(1, j)
                act.wait_ge(s_sg.sem, t + 1)
                s_ss.on(on(sy[:, 2, :], sy[:, 1, :], ACT.Square))
                root(ROOT["ssd"] + t, ss[:, 28 + 2 * t:30 + 2 * t])
            flip_output(2)

            banks.at(act, ("yt", 2, NT - 1))
            for d in range(2):
                act.dma_start(o["new_ssd"][0, 0, d].rearrange("(a q) p n -> (q p) a n", q=2), snew[:, d]).then_inc(s_out.sem, 16)
            act.wait_ge(s_out.sem, 64)
            for name in ("gdn_q", "gdn_k", "gdn_v"):
                conv_centre(name)
            silu("gdn_q")
            for t in range(NT):
                copy(gz[:, t, :], ("gdn_g", t), ACT.Silu)
            silu("gdn_k")
            silu("gdn_v")
            for i in range(3):
                for t in range(NT):
                    copy(gN[:, i, t, :], ("gn", i, t))
            root(ROOT["qk"], ss[:, 34:58])
            for i in range(2):
                for t in range(NT):
                    key = ("gt", i, t)
                    copy(gT[:, i, :, tok[t]], key, src=halves4(banks.at(act, key)))
            for d in range(2):
                act.dma_start(gs0[:, d], a["state_gdn"][0, 0, d].rearrange("h k v -> k h v")).then_inc(s_gst.sem, 16)
            for r in range(NT):
                tt = [r, (0, 2, 1)[r]]
                if r == 1:
                    for d in range(2):
                        banks.emptied(act, ("gstate", 0, d))
                        act.dma_start(o["new_gdn"][0, 0, d].rearrange("h k v -> k h v"), gs1[:, d]).then_inc(s_out.sem, 16)
                for d in range(2):
                    if r:
                        banks.at(act, ("gstate", r - 1, d))
                    t = tt[d]
                    decays(("gincl", r, d), gqk[:, t, d], t, small_cols["gdn"][d], d)
                    decays(("gstrict", r, d), gw[:, d, 0], t, small_cols["gdn"][d], d)
                for l in range(1, LEVELS):
                    for d in range(2):
                        key = ("gprod", r, l, d)
                        copy(gw[:, d, 4], key, src=halves4(banks.at(act, key)))
                    if r and l in (2, 3, 4, 5):
                        merge_gate(2, (r - 1) * 4 + l - 2)
                for d in range(2):
                    if r:
                        key = ("gwT", r, d)
                        copy(gw[:, d, 1], key, src=halves4(banks.at(act, key)), scale=-1.0)
                    key = ("gv", r, d)
                    copy(gvn[:, tt[d], d], key, src=halves4(banks.at(act, key)))
            for d in range(2):
                for t in (1, 2):
                    key = ("grow", t, d)
                    copy(gqe[:, d, :, (t - 1) * P:t * P], key, ACT.Exp, src=halves4(banks.at(act, key)))
            for t in range(NT):
                ps = banks.at(act, ("go", t))
                if t:
                    banks.emptied(act, ("go", t - 1))
                s_ss.on(on(sq[:, :], ps, ACT.Square))
                root(ROOT["gdn"] + t, ss[:, 16 + 4 * t:20 + 4 * t])
            flip_output(3)
            for j in range(8):
                merge_gate(3, j)

            banks.at(act, ("yt", 3, NT - 1))
            for g, to in ((2, g1row), (5, g2row)):
                for cnd in range(2):
                    for h in range(2):
                        copy(to[:, cnd, h * W:(h + 1) * W], ("grow", g, cnd, h))
            act.wait_ge(s_x2.sem, 1)
            norm_tokens(1)
            for t in range(NT):
                key = ("router", t)
                copy(pick[:, t, :], key, ACT.Sigmoid, src=banks.at(act, key)[:, 0:NE])

            def silus(e, f):
                q = e * 2 + f
                act.wait_ge(s_h1.sem, q + 1)
                if not (isinstance(e, int) and e == 0):
                    act.wait_ge(s_hid.sem, q - 1)
                s_sil.on(on(sil[:, f, :], psum[:, 6, 0:T], ACT.Silu))

            for f in range(2):
                silus(0, f)
            with act.Fori(1, NE + 1) as e:
                for f in range(2):
                    silus(e, f)

            for t in range(NT):
                act.wait_ge(s_y.sem, t + 1)
                s_ss.on(on(normed2[1][:, t % 2, :], x[:, t, :], ACT.Square, accum_out=ss[:, 58 + t:59 + t]))
                root(ROOT["last"] + t, ss[:, 58 + t:59 + t])

        @block.vector
        def _(dve):
            lane = Lane(dve, s_dve)
            v = nc.vector
            tt, ts, stt = v.tensor_tensor, v.tensor_scalar, v.scalar_tensor_tensor

            def each(w, n=W):
                return w[:, :, None].to_broadcast([P, w.shape[1], n // w.shape[1]])

            def inverse_root(i, c, scale, eps=EPS):
                lane.wait_own()
                s_pre.on(ts(c, c, scale, eps, ALU.mult, ALU.add))
                assert s_pre.n == i, (s_pre.n, i)
                dve.wait_ge(s_rs.sem, i)
                lane.link(v.reciprocal(c, c))

            def norm_tokens(which):
                dve.wait_ge(s_ss.sem, SQ["norm"][which] + NT)
                c = ss[:, 8 + which * 3:11 + which * 3]
                lane.link(ts(c, ss[:, which * 3:which * 3 + 3], 1.0, None, ALU.mult))
                s_pre.on(ts(c, c, 1.0 / D, EPS, ALU.mult, ALU.add))
                dve.wait_ge(s_rs.sem, ROOT["norm"][which])
                s_rcp.on(v.reciprocal(c, c))

            def modulate(which):
                dve.wait_ge(s_mod.sem, which + 1)
                for t in range(NT):
                    ps = banks.at(dve, (which, "xt", t, 1))
                    for i in range(4):
                        ins = ts(hT[:, 4 + i, tok[t]], ps[:, i * P:(i + 1) * P],
                                 scale1[:, which, 4 + i, cmod[t]:cmod[t] + 1],
                                 mod[:, which * 24 + 4 + i, cmod[t]:cmod[t] + 1], ALU.mult, ALU.add)
                        if i < 3:
                            lane.do(ins)
                    banks.free(ins, (which, "xt", t, 1))

            def ada_columns(lo, hi):
                for i in range(lo, hi):
                    ps = banks.at(dve, ("ada", i))
                    banks.free(tt(mod[:, 2 * i:2 * i + 2, :], ps[:, 0:4].rearrange("p (j c) -> p j c", j=2),
                                  cvec[:, 2 * i:2 * i + 2, None].to_broadcast([P, 2, 2]), ALU.add), ("ada", i))

            def scales(which):
                banks.emptied(dve, ("ada", which * 12 + 7))
                g = cvec[:, 48 + which * 8:56 + which * 8, None].to_broadcast([P, KD, 2])
                s_mod.on(stt(scale1[:, which], mod[:, which * 24 + 8:which * 24 + 16, :], 1.0, g, ALU.add, ALU.mult))

            def conv(name):
                for c in range(CW):
                    j = C0[name] + c
                    ps = banks.at(dve, (name, c))[:, 0:T]
                    out = conv_to[name][:, c, :]
                    out6, ps6 = (m.rearrange("p (r n) -> p r n", n=GRID) for m in (out, ps))
                    dve.wait_ge(s_conv.sem, conv_order[name] * CW + c + 1)
                    lane.do(stt(out6[:, :, 1:], ps6[:, :, :-1], cwt[:, j:j + 1], out6[:, :, 1:], ALU.mult, ALU.add))
                    lane.link(stt(out[:, 64:65], ps[:, 63:64], cwt[:, j:j + 1], out[:, 64:65], ALU.mult, ALU.add))
                    lane.do(stt(out6[:, :, :-1], ps6[:, :, 1:], cwt[:, 64 + j:65 + j], out6[:, :, :-1],
                                ALU.mult, ALU.add))
                    banks.free(stt(out[:, 63:64], ps[:, 64:65], cwt[:, 64 + j:65 + j], out[:, 63:64],
                                   ALU.mult, ALU.add), (name, c))

            def lift(n, lo, hi):
                for j in range(lo, hi):
                    key = ("lift", n, j)
                    ps = banks.at(dve, key)[:, 0:T]
                    banks.emptied(dve, ("merge", n, j))
                    if n == 0:
                        banks.free(tt(mixed[:, j, :], ps, gate[:, j % 2, :], ALU.mult), key)
                    else:
                        k = (n - 1) * KD + j
                        if k >= 2:
                            dve.wait_ge(s_madd.sem, k - 1)
                        banks.free(tt(lifted[:, j % 2, :], ps, gate[:, j % 2, :], ALU.mult), key)

            def head_norm(n, key, t, c, g, out, root):
                ps = banks.at(dve, (key, t))
                dve.wait_ge(s_ss.sem, SQ[key] + t + 1)
                lane.link(v.reduce_sum(c, halves4(sq[:, :]), axis=AX))
                inverse_root(root + t, c, 1.0 / P)
                for h in range(4):
                    hh = slice(h * P, (h + 1) * P)
                    ins = stt(out[:, t, hh], ps[:, hh], c[:, h:h + 1], g[:, t, hh], ALU.mult, ALU.mult)
                    if h < 3:
                        lane.do(ins)
                banks.free(ins, (key, t))

            banks.emptied(dve, ("pack", 1))
            s_lb.on(tt(lb[:, 0, :], cvec[:, 80:88], cvec[:, 80:88], ALU.subtract))
            dve.wait_ge(s_lbe.sem, 1)
            lane.link(v.reciprocal(lb[:, 1, :], lb[:, 0, :]))
            lane.link(tt(lb[:, 1, :], lb[:, 0, :], lb[:, 1, :], ALU.mult))
            lane.link(tt(lb[:, 2, :], lb[:, 1, :], lb[:, 1, :], ALU.subtract))
            lane.link(ts(lb[:, 3, :], lb[:, 2, :], -1.0, 1.0, ALU.mult, ALU.add))

            dve.wait_ge(s_fconst.sem, 16 * N_FCONST)
            for i, (key, work) in enumerate((("f1", 2), ("f2", 0))):
                xx, k = fnet[0:64, 3, :], fnet[0:64, work, :]
                ps = banks.at(dve, key)
                if i:
                    dve.wait_ge(s_sin.sem, 1)
                banks.free(ts(xx, ps[0:64, 0:T], fbias[:, i:i + 1], None, ALU.add), key)
                banks.emptied(dve, key)
                lane.link(ts(k, xx, 1.0 / (2 * math.pi), ROUND, ALU.mult, ALU.add))
                lane.link(ts(k, k, ROUND, None, ALU.subtract))
                lane.link(stt(xx, k, -TAU_HI, xx, ALU.mult, ALU.add))
                lane.link(stt(xx, k, -TAU_LO, xx, ALU.mult, ALU.add))
                s_arg.on(ts(xx, xx, PI32, -PI32, ALU.min, ALU.max))
            for t in range(NT):
                for order in range(2):
                    for way in range(2):
                        key = ("filt", t, order, way)
                        banks.free(tt(hf[:, order, t, way, :], banks.at(dve, key), window[:, t, way, :], ALU.mult), key)
                    banks.emptied(dve, ("filt", t, order, 1))
                    lane.link(tt(sd[:, order, 0, t, :], hf[:, order, t, 0, :], hf[:, order, t, 1, :], ALU.add))
                    s_sd.on(tt(sd[:, order, 1, t, :], hf[:, order, t, 1, :], hf[:, order, t, 0, :], ALU.subtract))
            for order in range(2):
                for ft in range(NT):
                    key = ("H", order, ft, 0)
                    banks.free(tt(hf[:, order, ft, 0, :], banks.at(dve, key), hbias[:, order, :], ALU.add), key)

            norm_tokens(0)
            ada_columns(0, 8)
            scales(0)
            modulate(0)
            for name in ("hy_v", "hy_x1", "hy_x2"):
                conv(name)
            ada_columns(8, 24)
            scales(1)

            for order in range(2):
                for ft in range(NT):
                    U_, H_ = [banks.at(dve, ("U", order, ft, ri)) for ri in range(2)], hf[:, order, ft]
                    if order == 0:
                        banks.emptied(dve, ("H", order, ft, 1))
                    lane.do(tt(hy_t[:, 0, :], U_[0], H_[:, 0, :], ALU.mult))
                    banks.free(tt(hy_t[:, 1, :], U_[0], H_[:, 1, :], ALU.mult), ("U", order, ft, 0))
                    lane.do(tt(hy_t[:, 2, :], U_[1], H_[:, 1, :], ALU.mult))
                    banks.free(tt(hy_t[:, 3, :], U_[1], H_[:, 0, :], ALU.mult), ("U", order, ft, 1))
                    banks.emptied(dve, ("U", order, ft, 1))
                    lane.link(tt(spec[:, ft, 0, :], hy_t[:, 0, :], hy_t[:, 2, :], ALU.add))
                    s_spec.on(tt(spec[:, ft, 1, :], hy_t[:, 1, :], hy_t[:, 3, :], ALU.subtract))
                    dve.wait_ge(s_spec.sem, s_spec.n)
                if order == 0:
                    banks.emptied(dve, ("hyt", 1, NT - 1))
                    for t in range(NT):
                        banks.free(tt(hyN[:, 0, t, :], banks.at(dve, ("y", t)), hyN[:, 1, t, :], ALU.mult), ("y", t))
            for c in range(CW):
                banks.free(tt(yT[:, 0, c, :], banks.at(dve, ("yo", c))[:, 0:T], hyT[:, 2, c, :], ALU.mult), ("yo", c))

            lows = hqk
            for d in range(2):
                name = ("hg_ff", "hg_fb")[d]
                banks.emptied(dve, (name, CW - 1))
                for c in range(CW):
                    k = d * CW + c
                    lane.do(ts(he[:, d, c, :], he[:, d, c, :], lb[:, 3, k:k + 1], lb[:, 2, k:k + 1], ALU.mult, ALU.add))
                    lane.do(ts(hk[:, d, c, :], hk[:, d, c, :], lb[:, 3, k:k + 1], None, ALU.mult))
                lane.wait_own()
                lane.link(ts(flat(he[:, d]), flat(he[:, d]), FLOOR, None, ALU.max))
                lane.link(ts(flat(lows[:, d]), flat(he[:, d]), LN_LOW, 2.0 ** LN_LIFT - 1, ALU.is_lt, ALU.mult))
                s_hf.on(stt(flat(he[:, d]), flat(lows[:, d]), 1.0, flat(he[:, d]), ALU.add, ALU.mult))
            dve.wait_ge(s_hreset.sem, 2)
            for d in range(2):
                dve.wait_ge(s_hlog.sem, d + 1)
                lane.link(stt(flat(he[:, d]), flat(lows[:, d]), -LN_LIFT * math.log(2.0) / (2.0 ** LN_LIFT - 1),
                              flat(he[:, d]), ALU.mult, ALU.add))
                way = slice(None) if d == 0 else slice(None, None, -1)
                lane.link(v.tensor_tensor_scan(flat(hb[:, d])[:, way], resets[:, :], flat(he[:, d])[:, way], 0.0,
                                               ALU.mult, ALU.add))
            lane.link(v.memset(hattn, 0.0))

            def level(i):
                d, m = i // LEVELS, 1 << (i % LEVELS)
                cut = lambda w: w.rearrange("p (n m) -> p n m", m=2 * m)
                right, left = slice(m, 2 * m), slice(0, m)
                qs, ks = (right, left) if d == FWD else (left, right)
                b = cut(flat(hb[:, d]))
                ref = b[:, :, m - 1:m] if d == FWD else b[:, :, m:m + 1]
                return (d, b, cut(flat(he[:, i % 2])), cut(flat(hqk[:, i % 2])), cut(flat(hq)), cut(flat(hk[:, d])),
                        qs, ks, ref.to_broadcast([P, CW * T // (2 * m), m]))

            def ask(i):
                d, b, e, _, _, _, qs, ks, ref = level(i)
                lane.do(tt(e[:, :, qs], b[:, :, qs], ref, ALU.subtract))
                s_hd.on(tt(e[:, :, ks], ref, b[:, :, ks], ALU.subtract))

            def take(i):
                for t in range(NT):
                    key = ("level", i, t)
                    if i:
                        banks.emptied(dve, ("level", i - 1, t))
                    mask = levels[:, i // LEVELS, i % LEVELS, None, :].bitcast(U32).to_broadcast([P, HG_H, P])
                    banks.free(v.copy_predicated(hattn[:, t], mask, halves4(banks.at(dve, key))), key)

            banks.emptied(dve, ("hg_q", CW - 1))
            ask(0)
            for i in range(2 * LEVELS):
                if i + 1 < 2 * LEVELS:
                    ask(i + 1)
                d, _, e, qk, q, k, qs, ks, _ = level(i)
                dve.wait_ge(s_he.sem, i + 1)
                lane.do(tt(qk[:, :, qs], q[:, :, qs], e[:, :, qs], ALU.mult))
                s_hqk.on(tt(qk[:, :, ks], k[:, :, ks], e[:, :, ks], ALU.mult))
                dve.wait_ge(s_hqk.sem, i + 1)
                if i:
                    take(i - 1)
                    if i <= 8:
                        lift(0, i - 1, i)
            for d in range(2):
                for w, t in ((0, 0), (1, FIRST[d])):
                    end = t * P + (P - 1 if d == FWD else 0)
                    ins = tt(hke[:, d, w], hb[:, d, :, end:end + 1].to_broadcast([P, HG_H, P]), hb[:, d, :, tok[t]],
                             ALU.subtract)
                    if (d, w) != (1, 1):
                        lane.do(ins)
            s_hx.on(ins)
            take(2 * LEVELS - 1)
            dve.wait_ge(s_hy.sem, 1)
            for d in range(2):
                for w, t in ((0, 0), (1, FIRST[d])):
                    ins = tt(hke[:, d, w], hke[:, d, w], hk[:, d, :, tok[t]], ALU.mult)
                    if (d, w) != (1, 1):
                        lane.do(ins)
            s_hke.on(ins)
            lane.do(tt(hqe[:, 0], hqe[:, 0], hq[:, :, P:T], ALU.mult))
            s_hqe.on(tt(hqe[:, 1], hqe[:, 1], hq[:, :, P:T], ALU.mult))
            dve.wait_ge(s_hke.sem, 1)
            s_hsum.on(tt(flat(hk[:, 0]), flat(hk[:, 0]), flat(hk[:, 1]), ALU.add))
            for t in range(NT):
                key = ("diag", t)
                banks.emptied(dve, ("level", 2 * LEVELS - 1, t))
                banks.free(v.copy_predicated(
                    hattn[:, t], ident[:, None, :].bitcast(U32).to_broadcast([P, HG_H, P]),
                    halves4(banks.at(dve, key))), key)
            dve.wait_ge(s_hst.sem, 32)
            for d in range(2):
                banks.free(v.tensor_copy(hnew[:, d], halves4(banks.at(dve, ("hstate", d, 0)))), ("hstate", d, 0))
                ps = banks.at(dve, ("hstate", d, 1))
                for h in range(HG_H):
                    ins = stt(hst[:, d, 1, h, :], hst[:, d, 0, h, :], coef[:, d, h:h + 1], ps[:, h * P:(h + 1) * P],
                              ALU.mult, ALU.add)
                    if h < 3:
                        lane.do(ins)
                banks.free(ins, ("hstate", d, 1))
            dve.wait_ge(s_hgn.sem, 1)
            for t in range(NT):
                head_norm(1, "ho", t, ss[:, 16 + 4 * t:20 + 4 * t], hg, hyn, ROOT["hg"])

            for name in ("ssd_x", "ssd_bc"):
                conv(name)
            flat3 = lambda w: w.rearrange("p a b -> p (a b)")
            dve.wait_ge(s_row.sem, 16 * N_ROW)
            dve.wait_ge(s_pool.sem, 3)
            for t in range(NT):
                key = ("small", t)
                banks.free(tt(small[:, t, :], banks.at(dve, key)[:, 0:32], sign_row[:, :], ALU.mult), key)
            banks.emptied(dve, ("small", NT - 1))
            lane.link(tt(small[:, :, :], small[:, :, :], small_row[:, 0:1, :].to_broadcast([P, NT, 32]), ALU.add))
            s_sp.on(stt(small2[:, :, :], small[:, :, :], -1.0, small[:, :, :], ALU.mult, ALU.min))
            dve.wait_ge(s_spa.sem, 1)
            c0, c1 = cum[:, :, 0, :], cum[:, :, 1, :]
            lane.link(ts(c0, small2[:, :, :], 1.0, None, ALU.add))
            lane.link(ts(c1, c0, 1.0, None, ALU.subtract))
            lane.link(tt(c1, small2[:, :, :], c1, ALU.subtract))
            s_sp.on(v.tensor_copy(small2[:, :, :], c0))
            lane.link(v.reciprocal(c0, c0))
            lane.link(tt(c1, c1, c0, ALU.mult))
            dve.wait_ge(s_spa.sem, 3)
            lane.link(tt(small2[:, :, :], small2[:, :, :], c1, ALU.add))
            lane.link(stt(small2[:, :, :], small[:, :, :], 0.0, small2[:, :, :], ALU.max, ALU.add))
            s_small.on(stt(small[:, :, :], small2[:, :, :], -1.0,
                           small_row[:, 1:2, :].to_broadcast([P, NT, 32]), ALU.mult, ALU.mult))
            for t in range(NT):
                key = ("cum", t)
                banks.free(ts(cum[:, t].rearrange("p a b -> p (a b)"), banks.at(dve, key)[:, 0:160], -1.0, None,
                              ALU.mult), key)
            dve.wait_ge(s_ecum.sem, 1)
            for d in range(2):
                sc, gc = small_cols["ssd"][d], small_cols["gdn"][d]
                lane.do(tt(dte[:, :, d * 8:d * 8 + 8], small2[:, :, sc], ecum[:, :, 2 + d, sc], ALU.mult))
                lane.do(tt(bdec[:, :, d * 4:d * 4 + 4], beta[:, :, d * 4:d * 4 + 4], ecum[:, :, d, gc], ALU.mult))
            lane.wait_own()
            banks.emptied(dve, ("sx", NT - 1))
            heads8 = lambda w: w.rearrange("p (h x) -> p h x", h=SSD_H)
            for d in range(2):
                for w, t in ((0, 0), (1, FIRST[d])):
                    if d:
                        banks.at(dve, ("sstate", 0, w))
                    s_sxe.on(tt(heads8(sxd[:, w, :]), heads8(sxN[:, t, :]), each(dte[:, t, d * 8:d * 8 + 8]), ALU.mult))
                if d == 0:
                    take_states(dve, nc, banks, lane, 0, snew, sst, ecum, small_cols, FIRST, halves4, heads8)
            take_states(dve, nc, banks, lane, 1, snew, sst, ecum, small_cols, FIRST, halves4, heads8)
            for t in range(NT):
                cb = banks.at(dve, ("cb", t))
                for d in range(2):
                    for q in range(2):
                        banks.emptied(dve, ("sdec", t, d, q))
                        ins = tt(sdec[:, d, q], sdec[:, d, q],
                                 cb[:, None, q * P:(q + 1) * P].to_broadcast([P, 4, P]), ALU.mult)
                        if (d, q) != (1, 1):
                            lane.do(ins)
                banks.free(ins, ("cb", t))
                banks.emptied(dve, ("cb", t))
                if t == 0:
                    for w in range(2):
                        banks.at(dve, ("sstate", 1, w))
                for d in range(2):
                    ins = tt(heads8(sxd[:, d, :]), heads8(sxN[:, t, :]), each(small2[:, t, small_cols["ssd"][d]]),
                             ALU.mult)
                    if d == 0:
                        lane.do(ins)
                s_sw.on(ins)
                if t:
                    for d in range(2):
                        key = ("sinter", t, d)
                        banks.free(tt(heads8(sy[:, 3 * d, :]), heads8(banks.at(dve, key)),
                                      each(ecum[:, t, d, small_cols["ssd"][d]]), ALU.mult), key)
                    banks.emptied(dve, ("sinter", t, 1))
                    lane.link(tt(sy[:, 0, :], sy[:, 0, :], sy[:, 3, :], ALU.add))
                lane.link(tt(heads8(sy[:, 4, :]), heads8(sxN[:, t, :]), each(ssd_row[:, W:W + 8]), ALU.mult))
                key = ("sintra", t)
                banks.free(tt(sy[:, 4, :], sy[:, 4, :], banks.at(dve, key), ALU.add), key)
                banks.emptied(dve, key)
                if t:
                    lane.link(tt(sy[:, 4, :], sy[:, 4, :], sy[:, 0, :], ALU.add))
                s_sg.on(tt(sy[:, 1, :], sy[:, 4, :], sz[:, t, :], ALU.mult))
                lift(1, (0, 3, 6)[t], (3, 6, 8)[t])
                c = ss[:, 28 + 2 * t:30 + 2 * t]
                dve.wait_ge(s_ss.sem, SQ["ssd"] + t + 1)
                lane.link(v.reduce_sum(c, sy[:, 2, :].rearrange("p (g n) -> p g n", g=2), axis=AX))
                inverse_root(ROOT["ssd"] + t, c, 1.0 / 256)
                for g in range(2):
                    gg = slice(g * 256, (g + 1) * 256)
                    ins = stt(sy_out[:, t, gg], sy[:, 1, gg], c[:, g:g + 1], ssd_row[:, gg], ALU.mult, ALU.mult)
                    if g == 0:
                        lane.do(ins)
                s_yn2.on(ins)
                dve.wait_ge(s_yn2.sem, t + 1)

            for name in ("gdn_q", "gdn_k", "gdn_v"):
                conv(name)
            for i in range(2):
                for t in range(NT):
                    banks.emptied(dve, ("gn", i, t))
                    k = 34 + (i * NT + t) * 4
                    lane.link(tt(sq[:, :], gN[:, i, t, :], gN[:, i, t, :], ALU.mult))
                    lane.link(v.reduce_sum(ss[:, k:k + 4], halves4(sq[:, :]), axis=AX))
            inverse_root(ROOT["qk"], ss[:, 34:58], 1.0)
            lane.link(ts(ss[:, 34:46], ss[:, 34:46], float(P) ** -0.5, None, ALU.mult))
            for i in range(2):
                for t in range(NT):
                    k = 34 + (i * NT + t) * 4
                    ins = tt(halves4(gN[:, i, t, :]), halves4(gN[:, i, t, :]), each(ss[:, k:k + 4]), ALU.mult)
                    if (i, t) != (1, NT - 1):
                        lane.do(ins)
            s_gnorm.on(ins)
            dve.wait_ge(s_gnorm.sem, 1)
            ident4 = ident[:, None, :].to_broadcast([P, 4, P])
            for r in range(NT):
                rt = [r, (0, 2, 1)[r]]
                for d in range(2):
                    t = rt[d]
                    banks.emptied(dve, ("gstrict", r, d))
                    for key, to in (("gkk", gw[:, d, 0]), ("gqk", gqk[:, t, d])):
                        banks.free(tt(to, to, halves4(banks.at(dve, (key, r, d))), ALU.mult), (key, r, d))
                for d in range(2):
                    dve.wait_ge(s_glevel[d].sem, r * LEVELS + 1)
                    lane.link(tt(gw[:, d, 3], ident4, gw[:, d, 1], ALU.subtract))
                    banks.free(tt(gw[:, d, 2], ident4, halves4(banks.at(dve, ("gprod", r, 0, d))), ALU.subtract),
                               ("gprod", r, 0, d))
                for l in range(1, LEVELS):
                    for d in range(2):
                        for key, to in (("ginv", gw[:, d, 2]), ("ginvT", gw[:, d, 3])):
                            if key == "ginv" and l == LEVELS - 1:
                                continue
                            banks.emptied(dve, (key, r, l - 1, d) if l > 1 else ("gprod", r, 0, d))
                            banks.free(tt(to, to, halves4(banks.at(dve, (key, r, l, d))), ALU.subtract),
                                       (key, r, l, d))
                    if r and l in (2, 3, 4, 5):
                        n = (r - 1) * 4 + l - 2
                        lift(2, n, n + 1)
                for d in range(2):
                    t = rt[d]
                    dve.wait_ge(s_glevel[d].sem, (r + 1) * LEVELS)
                    lane.do(tt(gw[:, d, 2], halves4(gN[:, 2, t, :]), each(beta[:, t, d * 4:d * 4 + 4]), ALU.mult))
                    lane.do(tt(gw[:, d, 4], halves4(gN[:, 1, t, :]), each(bdec[:, t, d * 4:d * 4 + 4]), ALU.mult))
                    s_gvk[d].on(tt(gw[:, d, 0], halves4(gN[:, 1, t, :]),
                                   each(ecum[:, t, 2 + d, small_cols["gdn"][d]]), ALU.mult))
                if r < 2:
                    for d in range(2):
                        key = ("gstate", r, d)
                        ps = banks.at(dve, key)
                        if r == 0:
                            banks.free(v.tensor_copy(gs1[:, d], halves4(ps)), key)
                            continue
                        dve.wait_ge(s_out.sem, 16 * 6)
                        dve.wait_ge(s_gst.sem, 32)
                        for h in range(GDN_H):
                            ins = stt(gs1[:, d, h, :], gs0[:, d, h, :],
                                      ecum[:, rt[d], 4, small_cols["gdn"][d]][:, h:h + 1],
                                      ps[:, h * P:(h + 1) * P], ALU.mult, ALU.add)
                            if h < 3:
                                lane.do(ins)
                        banks.free(ins, key)
            for d in range(2):
                for t in (1, 2):
                    banks.emptied(dve, ("grow", t, d))
                    w = gqe[:, d, :, (t - 1) * P:t * P]
                    s_gqe.on(tt(w, w, gT[:, 0, :, tok[t]], ALU.mult))
            dve.wait_ge(s_gqe.sem, 4)
            dve.wait_ge(s_hgn.sem, 2)
            for t in range(NT):
                head_norm(3, "go", t, ss[:, 16 + 4 * t:20 + 4 * t], gz, gyn, ROOT["gdn"])
            lift(3, 0, 8)

            banks.emptied(dve, ("grow", 2, 1, 1))
            for c in range(4):
                cc = slice(c * 256, (c + 1) * 256)
                for t in range(NT):
                    k = c * NT + t
                    key = ("out", c, t)
                    banks.free(tt(sq[:, k % 2 * 256:k % 2 * 256 + 256], banks.at(dve, key)[:, 0:256],
                                  g1row[:, cmod[t], cc], ALU.mult), key)
                    banks.emptied(dve, key)
                    ins = tt(x[:, t, cc], x[:, t, cc], sq[:, k % 2 * 256:k % 2 * 256 + 256], ALU.add)
                    (s_x2.on if k == 11 else lane.link)(ins)
            norm_tokens(1)
            modulate(1)

            dve.wait_ge(s_late.sem, 16 * N_LATE)
            biased, g8, sm, before, rbias = (pick[:, i, :] for i in (3, 4, 5, 6, 7))
            by8 = lambda w: w.rearrange("p (g e) -> p g e", g=NGRP)
            gs, rank, keep, pen, top, tot = (sm[:, i * 8:i * 8 + 8] for i in range(6))
            cmp_, masked, left = sq[:, 0:64], sq[:, 64:128], sq[:, 128:192]
            for t in range(NT):
                banks.emptied(dve, ("router", t))
                scores = pick[:, t, :]
                lane.link(tt(biased, scores, rbias, ALU.add))
                for g in range(NGRP):
                    lane.do(v.max(g8[:, g * 8:g * 8 + 8], biased[:, g * 8:g * 8 + 8]))
                lane.wait_own()
                lane.link(tt(gs, by8(g8)[:, :, 0], by8(g8)[:, :, 1], ALU.add))
                mine, other = gs[:, :, None].to_broadcast([P, 8, 8]), gs[:, None, :].to_broadcast([P, 8, 8])
                lane.link(tt(by8(cmp_), other, mine, ALU.is_equal))
                lane.link(tt(cmp_, cmp_, before, ALU.mult))
                lane.link(tt(by8(masked), other, mine, ALU.is_gt))
                lane.link(tt(cmp_, cmp_, masked, ALU.add))
                lane.link(v.reduce_sum(rank, by8(cmp_), axis=AX))
                lane.link(ts(keep, rank, float(TOPG), None, ALU.is_lt))
                lane.link(ts(pen, keep, -NEG, NEG, ALU.mult, ALU.add))
                lane.link(tt(by8(masked), by8(biased), each(keep, NE), ALU.mult))
                lane.link(tt(by8(masked), by8(masked), each(pen, NE), ALU.add))
                lane.link(v.max(top, masked))
                lane.link(v.match_replace(left, top, masked, TAKEN))
                lane.link(stt(cmp_, left, TAKEN / 2, scores, ALU.is_lt, ALU.mult))
                lane.link(v.reduce_sum(tot[:, 0:1], cmp_, axis=AX))
                lane.link(v.reciprocal(tot[:, 0:1], tot[:, 0:1]))
                s_gates.on(ts(egN[:, t, :], cmp_, tot[:, 0:1], ROUTED, ALU.mult, ALU.mult))
                dve.wait_ge(s_gates.sem, t + 1)
            banks.free(v.tensor_copy(lifted[0:NE, 0, :], banks.at(dve, "gateT")[0:NE, 0:T]), "gateT")

            def hiddens(e, slot):
                dve.wait_ge(s_eg[slot].sem, (e - slot) * 8 + 16)
                if not isinstance(e, int) or e >= 2:
                    dve.wait_ge(s_down.sem, e - 1)
                for f in range(2):
                    q = e * 2 + f
                    dve.wait_ge(s_sil.sem, q + 1)
                    s_gsil.on(tt(sil[:, f, :], sil[:, f, :], egate[:, slot, :], ALU.mult))
                    dve.wait_ge(s_gsil.sem, q + 1)
                    dve.wait_ge(s_h3.sem, q + 1)
                    s_hid.on(tt(hid[:, slot, f, :], psum[:, 7, 0:T], sil[:, f, :], ALU.mult))

            for e in range(3):
                hiddens(e, e % 2)
            with dve.Fori(3, NE + 1, 2) as e:
                hiddens(e, 1)
                hiddens(e + 1, 0)

            dve.wait_ge(s_down.sem, NE + 1)
            for t in range(NT):
                for h in range(2):
                    hh = slice(h * W, (h + 1) * W)
                    lane.link(tt(sq[:, :], psum[:, t * 2 + h, :], g2row[:, cmod[t], hh], ALU.mult))
                    ins = tt(x[:, t, hh], x[:, t, hh], sq[:, :], ALU.add)
                    (s_y.on if h else lane.link)(ins)
                dve.wait_ge(s_y.sem, t + 1)
            for t in range(NT):
                c = ss[:, 58 + t:59 + t]
                dve.wait_ge(s_ss.sem, SQ["last"] + t + 1)
                inverse_root(ROOT["last"] + t, c, 1.0 / D)
                s_fin.on(stt(x[:, t, :], x[:, t, :], c, fg_row, ALU.mult, ALU.mult))

        @block.gpsimd
        def _(pool):
            g = nc.gpsimd
            s_pool.on(g.memset(sign_row[:, 0:24], 1.0))
            s_pool.on(g.memset(sign_row[:, 24:32], -1.0))
            s_pool.on(g.memset(small_row[:, :, 24:32], 0.0))

            def add_branch(n, lo, hi):
                for j in range(lo, hi):
                    banks.emptied(pool, ("lift", n, j))
                    s_madd.on(g.tensor_tensor(mixed[:, j, :], mixed[:, j, :], lifted[:, j % 2, :], ALU.add))

            banks.emptied(pool, ("yo", CW - 1))
            s_hreset.on(g.memset(resets[:, :], 1.0))
            pool.wait_ge(s_hreset.sem, 1)
            s_hreset.on(g.memset(resets[:, 0:CW * T:P], 0.0))
            banks.emptied(pool, ("hg_g", NT - 1))
            pool.wait_ge(s_row.sem, 16 * N_ROW)
            h12 = lambda w: w.rearrange("p t (h n) -> p (t h) n", n=P)
            s_hgn.on(g.tensor_tensor(h12(hg), h12(hg), norm_row[:, 0:1, :].to_broadcast([P, 12, P]), ALU.mult))
            add_branch(1, 0, 8)
            banks.emptied(pool, ("gdn_g", NT - 1))
            s_hgn.on(g.tensor_tensor(h12(gz), h12(gz), norm_row[:, 1:2, :].to_broadcast([P, 12, P]), ALU.mult))
            for r in range(NT):
                for l in range(LEVELS):
                    for d in range(2):
                        if l:
                            banks.at(pool, ("gprod", r, l - 1, d))
                        else:
                            banks.emptied(pool, ("gkk", r, d))
                            if r:
                                banks.at(pool, ("gv", r - 1, d))
                        if l == 1:
                            banks.emptied(pool, ("gprod", r, 0, d))
                        s_glevel[d].on(g.tensor_tensor(
                            gw[:, d, 1], gw[:, d, 0], levels[:, d, l, None, :].to_broadcast([P, 4, P]), ALU.mult))
                    if r and l in (2, 3, 4, 5):
                        n = (r - 1) * 4 + l - 2
                        add_branch(2, n, n + 1)
            add_branch(3, 0, 8)
            pool.wait_ge(s_madd.sem, s_madd.n)
            s_pool.on(g.memset(lifted[0:1, 1, :], 1.0))

        @block.sync
        def _(sp):
            def load(to, src, s):
                sp.dma_start(to, src).then_inc(s.sem, 16)

            def row(w):
                return w.rearrange("(a n) -> a n", a=1).to_broadcast([P, w.shape[0]])

            load(ident[:, :], a["t_ident"], s_const)
            for i, (name, n) in enumerate((("conv_w", 96), ("conv_b", 32))):
                src = a[name][0].rearrange("w (j p) -> (w j) p", p=P) if i == 0 else \
                    a[name][0].rearrange("(j p) -> j p", p=P)
                load(rows[(0, 96)[i]:(96, 128)[i], 0, :], src, s_vec)
            load(rows[0:48, 1, :], a["ada_b"][0].rearrange("(j p) -> j p", p=P), s_vec)
            for i, (src) in enumerate((a["norm1_g"][0], a["norm2_g"][0], a["c_ctx"], a["c"][0])):
                load(rows[48 + 8 * i:56 + 8 * i, 1, :], src.rearrange("(j p) -> j p", p=P), s_vec)
            load(rows[80:88, 1, :], a["hg_lb"][:, 0, :].rearrange("a (j p) -> (a j) p", p=P), s_vec)
            load(fnet[0:33, 0, :], a["t_feats"], s_fconst)
            load(fw1[0:33, :], a["hy_w1"][0], s_fconst)
            load(fw2[:, :], a["hy_w2"][0], s_fconst)
            for i, name in enumerate(("hy_b1", "hy_b2")):
                load(fbias[:, i:i + 1], a[name][0].rearrange("(n a) -> n a", a=1), s_fconst)
            load(fw3[0:64, :], a["hy_w3"][0], s_fconst)
            load(window, a["t_window"], s_fconst)
            for L, to in ((P, dft1[:, :, None, :]), (2 * P, dft2)):
                for i, name in enumerate(("cos", "sin", "icos", "isin")):
                    load(to[:, i], a[f"t_{name}{L}"], s_fconst)
            load(hbias, a["hy_bias"][0][None, :, :].to_broadcast([P, 2, W]), s_fconst)
            for t, src in enumerate((a["x_prompt"][0], a["x_sample"][0][0:P], a["x_sample"][0][P:2 * P])):
                load(x[:, t, :], src, s_x)

            def slabs(lo, hi):
                for i in range(lo, hi):
                    name, src = slab_plan[i]
                    if i >= SLABS:
                        sp.wait_ge(banks.filled, slab_last[i - SLABS])
                    n = src.shape[1]
                    load(ring[:, i % SLABS, :].rearrange("p (k n) -> p k n", k=n), src, s_slab[i % SLABS])

            slabs(0, 8)
            load(sums[:, :, :], a["t_sums"], s_const)
            load(reach[:, :, :], a["t_reach"], s_const)
            load(levels[:, :, :, :], a["t_levels"], s_const)
            slabs(8, 16)
            load(small_row[:, 0, 0:16], row(a["ssd_dt_bias"][0].rearrange("a h -> (a h)")), s_row)
            load(small_row[:, 0, 16:24], row(a["gdn_dt_bias"][0].rearrange("a h -> (a h)")), s_row)
            load(small_row[:, 1, 0:16], row(a["ssd_a_log"][0].rearrange("a h -> (a h)")), s_row)
            load(small_row[:, 1, 16:24], row(a["gdn_a_log"][0].rearrange("a h -> (a h)")), s_row)
            load(ssd_row[:, 0:W], row(a["ssd_norm"][0]), s_row)
            load(ssd_row[:, W:W + 8], row(a["ssd_d"][0]), s_row)
            load(norm_row[:, 0, :], row(a["hg_norm"][0]), s_row)
            load(norm_row[:, 1, :], row(a["gdn_norm"][0]), s_row)
            load(smallw[:, :, 0:16], cols_of(w_in, COL["ssd_dt"], 16), s_row)
            load(smallw[:, :, 16:32], cols_of(w_in, COL["gdn_ab"], 16), s_row)
            slabs(16, len(slab_plan))

            banks.at(sp, ("yt", 3, NT - 1))
            load(fg_row, row(a["final_g"]), s_late)
            load(router_w, a["router_w"][0].rearrange("(k p) n -> p k n", p=P), s_late)
            load(pick[:, 7, :], row(a["router_bias"][0]), s_late)
            load(pick[:, 6, :], row(a["t_before"]), s_late)
            sp.wait_ge(s_late.sem, 64)

            def up(e, slot, w1, w3):
                for i, w in enumerate((w1, w3)):
                    load(wexp[:, slot, i, :].rearrange("p (k n) -> p k n", k=KD),
                         w.rearrange("(k p) n -> p k n", p=P), s_w13[slot])

            def dn(e, slot, w2):
                load(wexp[:, slot, 2, :].rearrange("p (f n) -> p f n", f=2),
                     w2.rearrange("(f p) n -> p f n", p=P), s_w2[slot])

            def gates(e, slot):
                load(egate[:, slot, :], gates_dram[e:e + 1, :].to_broadcast([P, T])
                     if isinstance(e, int) else gates_dram[bass.ds(e, 1), :].to_broadcast([P, T]), s_eg[slot])

            ew = [a[n][0] for n in ("exp_w1", "exp_w3", "exp_w2")]
            up(0, 0, a["sh_w1"][0], a["sh_w3"][0])
            dn(0, 0, a["sh_w2"][0])
            up(1, 1, ew[0][0], ew[1][0])
            dn(1, 1, ew[2][0])
            banks.emptied(sp, "gateT")
            sp.wait_ge(s_pool.sem, 4)
            load(gates_dram[1:NE + 1, :], lifted[0:NE, 0, :], s_gstore)
            load(gates_dram[0:1, :], lifted[0:1, 1, :], s_gstore)
            sp.wait_ge(s_gstore.sem, 32)
            gates(0, 0)
            gates(1, 1)

            def expert(e, slot):
                sp.wait_ge(s_h3.sem, e * 2 - 2)
                up(e, slot, ew[0][e - 1], ew[1][e - 1])
                sp.wait_ge(s_hid.sem, e * 2 - 2)
                gates(e, slot)
                sp.wait_ge(s_down.sem, e - 1)
                dn(e, slot, ew[2][e - 1])

            with sp.Fori(2, NE, 2) as e:
                expert(e, 0)
                expert(e + 1, 1)
            expert(NE, 0)
            for t, to in enumerate((o["y_prompt"][0], o["y_sample"][0][0:P], o["y_sample"][0][P:2 * P])):
                sp.wait_ge(s_fin.sem, t + 1)
                sp.dma_start(to, x[:, t, :]).then_inc(s_out.sem, 16)
            sp.wait_ge(s_out.sem, 16 * 9)


def take_states(dve, nc, banks, lane, d, snew, sst, ecum, small_cols, FIRST, halves4, heads8):
    banks.free(nc.vector.tensor_copy(snew[:, d], halves4(banks.at(dve, ("sstate", d, 0)))), ("sstate", d, 0))
    banks.emptied(dve, ("sin", d))
    ps = banks.at(dve, ("sstate", d, 1))
    total = ecum[:, FIRST[d], 4, small_cols["ssd"][d]]
    lane.link(nc.vector.tensor_tensor(heads8(sst[:, d, 1, :]), heads8(sst[:, d, 0, :]),
                                      total[:, :, None].to_broadcast([P, SSD_H, 64]), ALU.mult))
    banks.free(nc.vector.tensor_tensor(sst[:, d, 1, :], sst[:, d, 1, :], ps, ALU.add), ("sstate", d, 1))


OUTS = {"y_prompt": (1, 128, 1024), "y_sample": (1, 256, 1024), "new_hgrn": (1, 1, 2, 4, 128, 128),
        "new_ssd": (1, 1, 2, 8, 64, 128), "new_gdn": (1, 1, 2, 4, 128, 128)}


def kernel(**inputs):
    import concourse.bacc as bacc
    from concourse.bass_utils import run_bass_kernel_spmd

    nc = bacc.Bacc("TRN2", target_bir_lowering=False, num_devices=1)
    arrays, a = {}, {}
    for name, value in {**inputs, **shape_tables()}.items():
        value = np.ascontiguousarray(value)
        arrays[f"in_{name}"] = value
        a[name] = nc.dram_tensor(f"in_{name}", value.shape, mybir.dt.from_np(value.dtype), kind="ExternalInput").ap()
    o = {name: nc.dram_tensor(f"out_{name}", shape, F32, kind="ExternalOutput").ap() for name, shape in OUTS.items()}
    trunk(nc, a, o)
    r = run_bass_kernel_spmd(nc, [arrays], core_ids=[0])
    return tuple(r.results[0][f"out_{name}"] for name in OUTS)
```

```python
import math
from contextlib import ExitStack

import numpy as np
import concourse.bass as bass
from concourse import mybir

P = 128
D = 1024
KD = D // P
NT = 3
T = NT * P
W = 512
CW = W // P
GRID = 64
EPS = 1e-6
FLOOR = 1e-30
HG_H, SSD_H, GDN_H = 4, 8, 4
NE, NGRP, TOPG, TOPK, FE = 64, 8, 4, 8, 256
ROUTED = 2.5
NEG = -1e30
LEVELS = 7
FWD, BWD = 0, 1
LN_LOW = 2.0 ** -60
LN_LIFT = 40
ROUND = 1.5 * 2.0 ** 23
TAU_HI = 6.28125
TAU_LO = 2 * math.pi - TAU_HI
PI32 = 3.1415925
TAKEN = -3e38
FAR = 1000.0
COL = dict(hy_v=0, hy_x1=512, hy_x2=1024, ssd_x=1536, ssd_bc=2048, gdn_q=2560, gdn_k=3072, gdn_v=3584,
           hg_q=4096, hg_ff=4608, hg_fb=5120, hg_v=5632, hg_g=6144, ssd_z=6656, ssd_dt=7168,
           gdn_g=7184, gdn_ab=7696, merge=7712)

F32 = mybir.dt.float32
F32R = mybir.dt.float32r
U32 = mybir.dt.uint32
ALU = mybir.AluOpType
ACT = mybir.ActivationFunctionType
AX = mybir.AxisListType.X


def shape_tables():
    i = np.arange(P)
    r, t = i[:, None], i[None, :]
    out = {"t_ident": np.eye(P)}
    out["t_sums"] = np.stack([r <= t, r >= t, r > t, r < t, r >= 0 * t], 1)
    out["t_reach"] = np.stack([np.where(m, 0.0, NEG) for m in (r <= t, r >= t, r < t, r > t)], 1)
    lev = np.zeros((P, 2, LEVELS, P))
    for l in range(LEVELS):
        m = 1 << l
        left_s, right_t = (r // m) % 2 == 0, (t // m) % 2 == 1
        lev[:, FWD, l] = (r // (2 * m) == t // (2 * m)) & left_s & right_t
        lev[:, BWD, l] = lev[:, FWD, l].T
    out["t_levels"] = lev
    for L in (P, 2 * P):
        n = np.arange(L)
        th = np.pi * (n[None, :] + 0.5) * n[:, None] / L
        c, s = np.cos(th), np.sin(th)
        for name, m in (("cos", c), ("sin", s), ("icos", c.T / L), ("isin", -s.T / L)):
            out[f"t_{name}{L}"] = m.reshape(L // P, P, L).transpose(1, 0, 2)
    feats, win = [], []
    for L in (P, 2 * P):
        t_ = np.arange(L, dtype=np.float32) / np.float32(L)
        bands = np.arange(1, 17, dtype=np.float32)
        ang = (np.float32(2.0 * math.pi) * t_[:, None] * bands).astype(np.float32)
        feats.append(np.concatenate([t_[:, None], np.sin(ang), np.cos(ang)], 1).T)
        deltas = np.linspace(math.log(1e-2) / 1.5, math.log(1e-2) / 0.3, W)
        w = np.exp(-t_[:, None].astype(np.float64) * np.abs(deltas))
        wa = w.copy()
        wa[0] = 0.0
        win.append(np.stack([w, wa], 1).reshape(L // P, P, 2, W).transpose(1, 0, 2, 3))
    out["t_before"] = np.tril(np.ones((NGRP, NGRP)), -1).reshape(-1)
    out["t_iota"] = np.concatenate([t + 0 * r, r], 1)
    out["t_feats"] = np.concatenate(feats, 1)
    out["t_window"] = np.concatenate(win, 1)
    return {k: np.ascontiguousarray(v, dtype=np.float32) for k, v in out.items()}


class Signal:

    def __init__(self, ctx, nc, name):
        self.sem, self.n = ctx.enter_context(nc.semaphore(name)), 0

    def on(self, ins, by=1):
        self.n += by
        ins.then_inc(self.sem, by)


class Lane:

    def __init__(self, eng, signal):
        self.eng, self.own = eng, signal

    def do(self, ins):
        self.own.on(ins)

    def wait_own(self):
        self.eng.wait_ge(self.own.sem, self.own.n)

    def link(self, ins):
        self.do(ins)
        self.wait_own()


class Banks:

    def __init__(self, ctx, nc, psum):
        self.psum, self.jobs, self.now = psum, {}, []
        self.filled = ctx.enter_context(nc.semaphore("bank_filled"))
        self.freed = {by: ctx.enter_context(nc.semaphore(f"bank_freed_{by}")) for by in ("act", "dve")}
        self.count = {"act": 0, "dve": 0}
        self.seen = {"act": 0, "dve": 0}

    def open(self, pe, key, by):
        j = len(self.now)
        assert key not in self.jobs, key
        self.count[by] += 1
        self.jobs[key] = (j, by, self.count[by])
        self.now.append(key)
        if j >= 8:
            _, last_by, n = self.jobs[self.now[j - 8]]
            pe.wait_ge(self.freed[last_by], n)
        return self.psum[:, j % 8, :]

    def close(self, ins):
        ins.then_inc(self.filled, 1)

    def at(self, eng, key):
        j = self.jobs[key][0]
        eng.wait_ge(self.filled, j + 1)
        return self.psum[:, j % 8, :]

    def look(self, key):
        return self.psum[:, self.jobs[key][0] % 8, :]

    def free(self, ins, key):
        _, by, n = self.jobs[key]
        self.seen[by] += 1
        assert self.seen[by] == n, (key, by, n, self.seen[by])
        ins.then_inc(self.freed[by], 1)

    def emptied(self, eng, key):
        _, by, n = self.jobs[key]
        eng.wait_ge(self.freed[by], n)


def decay(mm, banks, pe, key, ident, mask, heads, betas=None):
    ps = banks.open(pe, key, "act").rearrange("p (h t) -> p h t", h=4)
    last = mm(ps, lhsT=ident[:, :], rhs=mask[:, None, :].to_broadcast([P, 4, P]), start=True, stop=False)
    for h, (c, tri) in enumerate(heads):
        last = mm(ps[:, h, :], lhsT=c.to_broadcast([P, P]), rhs=tri, start=False, stop=h == 3 and not betas)
    for h, c in enumerate(betas or []):
        last = mm(ps[:, h, :], lhsT=c.to_broadcast([P, P]), rhs=ident[:, :], start=False, stop=h == 3)
    banks.close(last)


def trunk(nc, a, o):
    ctx = ExitStack()
    with ctx:
        def sb(name, *shape, dt=F32):
            return ctx.enter_context(nc.sbuf_tensor(name, list(shape), dt))

        def sig(name):
            return Signal(ctx, nc, name)

        psum = ctx.enter_context(nc.psum_tensor("banks", [P, 8, 512], F32))
        banks = Banks(ctx, nc, psum)
        gates_dram = nc.dram_tensor("expert_gates", (NE, T), F32).ap()
        places_dram = nc.dram_tensor("expert_places", (NT * NE, T), F32).ap()

        x = sb("x", P, NT, D)
        ident = sb("ident", P, P)
        sums = sb("sums", P, 5, P)
        mod = sb("mod", P, 6 * KD, 2)
        ss = sb("ss", P, 64)
        sq = sb("sq", P, W)
        places = sb("places", P, NT, NT * NE)
        iota = sb("iota", P, P + 1)
        n_middle = sb("n_middle", P, 1, dt=mybir.dt.int32)

        branches = ctx.enter_context(ExitStack())

        def sb(name, *shape, dt=F32, to=branches):
            return to.enter_context(nc.sbuf_tensor(name, list(shape), dt))

        mixed = sb("mixed", P, KD, T)
        early = mixed[:, :, :].rearrange("p k t -> p (k t)")
        hbias = early[:, 0:2 * W].rearrange("p (o n) -> p o n", o=2)
        rows = early[:, 1024:1280].rearrange("p (i n) -> p i n", i=2)
        fw1, fw2 = early[0:64, 1280:1344], early[0:64, 1344:1408]
        yT = sb("yT", P, 2, CW, T)
        hT = sb("hT", P, KD, T)
        SLABS, SLAB = 4, 2048
        ring = sb("ring", P, SLABS, SLAB)
        gate = sb("gate", P, 2, T)
        lifted = sb("lifted", P, 2, T)
        reach = sb("reach", P, 4, P)
        levels = sb("levels", P, 2, LEVELS, P)
        cols = sb("cols", P, 2, P)
        ada_row = sb("ada_row", P, 2, 256)
        cond = sb("cond", P, KD, 2)
        scale1 = sb("scale1", P, 2, KD, 2)
        lb = sb("lb", P, 4, 8)
        small = sb("small", P, NT, 32)
        small2 = sb("small2", P, NT, 32)
        small_row = sb("small_row", P, 2, 32)
        sign_row = sb("sign_row", P, 32)
        cum = sb("cum", P, NT, 5, 32)
        ecum = sb("ecum", P, NT, 5, 32)
        coef = sb("coef", P, 4, 16)
        beta = sb("beta", P, NT, 8)
        bdec = sb("bdec", P, NT, 8)
        dte = sb("dte", P, NT, 16)
        norm_row = sb("norm_row", P, 2, P)
        ssd_row = sb("ssd_row", P, W + 8)
        fbias = sb("fbias", 64, 2)
        smallw = sb("smallw", P, KD, 32)
        ARENA = 22528
        arena = sb("arena", P, ARENA)

        def part(at, *shape):
            n = int(np.prod(shape))
            assert at + n <= ARENA, (at, n)
            v = arena[:, at:at + n]
            if len(shape) == 1:
                return v
            names = "abcd"[:len(shape)]
            return v.rearrange(f"p ({' '.join(names)}) -> p {' '.join(names)}", **dict(zip(names, shape)))

        U = CW * T
        dft1 = part(0, 4, P)
        dft2 = part(512, 4, 2, 2 * P)
        hf = part(2560, 2, NT, 2, W)
        window = part(8704, NT, 2, W)
        sd = part(11776, 2, 2, NT, W)
        fnet = part(17920, 4, T)
        fw3 = part(19456, 4 * W)
        hyT = part(8704, 3, CW, T)
        hyN = part(8704 + 3 * U, 2, NT, W)
        spec = part(8704 + 5 * U, NT, 2, W)
        hy_t = part(8704 + 7 * U, 4, W)
        normed2 = (part(8704, 2, D), part(12288, 2, D))
        hq = part(0, CW, T)
        hk = part(U, 2, CW, T)
        hb = part(3 * U, 2, CW, T)
        he = part(5 * U, 2, CW, T)
        hqk = part(7 * U, 2, CW, T)
        hv = part(9 * U, NT, W)
        hg = part(10 * U, NT, W)
        hattn = part(11 * U, NT, HG_H, P)
        resets = part(11 * U, U)
        hqe = hb[:, :, :, P:T]
        hst = part(12 * U, 2, 2, HG_H, P)
        hnew = part(12 * U + 2048, 2, HG_H, P)
        hke = part(5 * U, 2, 2, HG_H, P)
        hkn = part(7 * U, 2, 2, HG_H, P)
        hyn = part(5 * U, NT, W)
        sxT = part(0, 2, CW, T)
        sxN = part(2 * U, NT, W)
        sz = part(3 * U, NT, W)
        sbN = part(4 * U, NT, 2, P)
        sdec = part(5 * U, 2, 2, 4, P)
        sxd = part(6 * U + 512, 2, W)
        s_in = part(8 * U, 2, 4, P)
        sst = part(9 * U, 2, 2, W)
        snew = part(11 * U, 2, 4, P)
        sy = part(12 * U, 5, W)
        sy_out = part(12 * U + 5 * W, NT, W)
        gT = part(0, 3, CW, T)
        gqe = part(2 * U, 2, GDN_H, 2 * P)
        gs0 = part(2 * U + 2048, 2, GDN_H, P)
        gN = part(3 * U, 3, NT, W)
        gz = part(10 * U, NT, W)
        gqk = part(6 * U, NT, 2, GDN_H, P)
        gvn = part(8 * U, NT, 2, GDN_H, P)
        gw = part(10 * U, 2, 5, GDN_H, P)
        gs1 = part(10 * U + 5120, 2, GDN_H, P)
        gyn = part(0, NT, W)
        wsh = part(0, 3, SLAB)
        hid = part(12288, 2, T)
        sil = part(13824, 2, T)
        g1row = part(15360, 2, D)
        egN = part(17408, NT, NE)
        chosen = part(17600, NT, NE)
        cnt = part(17792, NE)
        pick = part(20480, 8, NE)
        router_w = part(20992, KD, NE)

        small_cols = {"ssd": (slice(0, 8), slice(8, 16)), "gdn": (slice(16, 20), slice(20, 24)),
                      "beta": (slice(24, 28), slice(28, 32))}
        tok = [slice(t * P, (t + 1) * P) for t in range(NT)]
        SECOND = {FWD: 2, BWD: 1}
        FIRST = {FWD: 1, BWD: 2}
        LATE_ADA = [(i, min(i + 2, 24)) for i in range(11, 24, 2)]
        cmod = [0, 1, 1]

        s_const = sig("constants_landed")
        s_vec = sig("vectors_landed")
        s_fnet = sig("filter_network_landed")
        s_fconst = sig("filter_tables_landed")
        s_row = sig("rows_landed")
        s_x = sig("tokens_landed")
        s_out = sig("outputs_stored")
        s_slab = [sig(f"slab{i}_landed") for i in range(SLABS)]
        s_act, s_dve, s_pool = sig("act_step"), sig("dve_step"), sig("pool_step")
        s_cond = sig("cond_ready")
        s_sin = sig("filter_layer_ready")
        s_sd = sig("filters_ready")
        s_conv = sig("conv_centre_ready")
        s_silu = sig("silu_group_ready")
        s_spec = sig("spectrum_ready")
        s_ss = sig("squares_summed")
        s_rcp = sig("reciprocals_ready")
        s_sg = sig("ssd_output_gated")
        s_x2 = sig("residual_added")
        s_madd = sig("branch_terms_added")
        s_hgn = sig("gates_times_norms")
        s_hreset = sig("scan_resets_ready")
        s_rs = sig("roots_ready")
        s_pre = sig("root_arguments_ready")
        s_mod = sig("modulation_ready")
        s_normed = sig("tokens_normalised")
        s_arg = sig("sine_arguments_ready")
        s_hf = sig("forget_gate_argument")
        s_hlog = sig("forget_gate_logs")
        s_hd = sig("level_decays_asked")
        s_he = sig("level_decays_ready")
        s_hqk = sig("level_factors_ready")
        s_hsum = sig("keys_summed")
        s_hke = sig("keys_to_end_ready")
        s_hqe = sig("queries_decayed")
        s_hx = sig("state_decays_asked")
        s_hy = sig("state_decays_ready")
        s_sp = sig("softplus_steps")
        s_spa = sig("softplus_exps")
        s_small = sig("log_decays_ready")
        s_ecum = sig("decay_exps_ready")
        s_sxe = sig("ssd_inputs_to_end_ready")
        s_sw = sig("ssd_weights_ready")
        s_gnorm = sig("delta_qk_normalised")
        s_glevel = [sig(f"delta_level_{d}") for d in "fb"]
        s_gvk = [sig(f"delta_values_keys_{d}") for d in "fb"]
        s_gqe = sig("delta_queries_decayed")
        s_yn2 = sig("ssd_output_ready")
        s_lb = sig("bound_logits_shifted")
        s_lbe = sig("bound_exps_ready")
        s_hst = sig("hgrn_states_landed")
        s_sst = sig("ssd_states_landed")
        s_gst = sig("delta_states_landed")
        s_late = sig("late_rows_landed")
        s_gates = sig("expert_gates_ready")
        s_gstore = sig("expert_gates_stored")
        s_shared = sig("shared_expert_landed")
        s_h2 = sig("high_parts_ready")
        s_ranks, s_placed = sig("ranks_ready"), sig("places_ready")
        s_rowsT, s_rowsN = sig("rows_transposed"), sig("rows_ready")
        s_h1, s_h3 = sig("gate_units_ready"), sig("up_units_ready")
        s_sil, s_hid = sig("silu_ready"), sig("hidden_ready")

        w_in, ada = a["w_in"][0], a["ada_w"][0]

        def cols_of(w, c0, n=256):
            return w[:, c0:c0 + n].rearrange("(k p) n -> p k n", p=P)

        slab_plan = []
        for i in range(8):
            slab_plan.append((("ada", i), cols_of(ada, i * 256)))

        def plan(name, halves=2):
            for h in range(halves):
                slab_plan.append(((name, h), cols_of(w_in, COL[name] + h * 256)))

        def plan_lift(n):
            for h in range(4):
                if h % 2 == 0:
                    slab_plan.append((("wb", n, h // 2), a["w_branch"][0, n][:, h // 2 * W:h // 2 * W + W]
                                      .rearrange("(k p) n -> p k n", p=P)))
                slab_plan.append((("merge", n, h), cols_of(w_in, COL["merge"] + n * D + h * 256)))

        for name in ("hy_v", "hy_x1", "hy_x2"):
            plan(name)
        for name in ("hg_q", "hg_ff", "hg_fb", "hg_v", "hg_g"):
            plan(name)
        plan_lift(0)
        for name in ("ssd_x", "ssd_bc", "ssd_z"):
            plan(name)
        plan_lift(1)
        for name in ("gdn_q", "gdn_k", "gdn_v"):
            plan(name)
        for i in range(8, 24):
            slab_plan.append((("ada", i), cols_of(ada, i * 256)))
        plan_lift(2)
        plan("gdn_g")
        plan_lift(3)
        for c in range(4):
            slab_plan.append((("w_out", c), cols_of(a["w_out"][0], c * 256)))
        slab_at = {name: i for i, (name, _) in enumerate(slab_plan)}
        slab_last = {}

        def slab(pe, name, kd=KD):
            i = slab_at[name]
            pe.wait_ge(s_slab[i % SLABS].sem, 16 * (i // SLABS + 1))
            return ring[:, i % SLABS, :].rearrange("p (k n) -> p k n", k=kd)

        def slab_done(*names):
            for name in names:
                slab_last[slab_at[name]] = len(banks.now)

        SQ = {"norm": (0, 12), "ho": 3, "ssd": 6, "go": 9}
        N_IDENT, N_CONST, N_VEC, N_FNET, N_FCONST, N_LATE, N_ROW = 1, 4, 8, 5, 11, 4, 10
        ROOT = {"norm": (1, 12), "hg": 2, "ssd": 5, "qk": 8, "gdn": 9}

        branches.close()
        h2 = [ctx.enter_context(nc.sbuf_tensor(f"h2_{n}", [P, NT, D], F32R)) for n in ("high", "low")]

        branch_work = ExitStack()
        block = branch_work.enter_context(nc.Block())

        @block.tensor
        def _(pe):
            mm = nc.tensor.matmul

            def contract(out, pairs):
                for i, (lhsT, rhs) in enumerate(pairs):
                    last = mm(out, lhsT=lhsT, rhs=rhs, start=i == 0, stop=i == len(pairs) - 1)
                return last

            def flip4(key, by, sources, n=P):
                ps = banks.open(pe, key, by)
                for i, src in enumerate(sources):
                    last = nc.tensor.transpose(ps[0:n, i * P:(i + 1) * P], src, ident[:, :])
                banks.close(last)

            def project_T(name, by):
                for c in range(CW):
                    w = slab(pe, (name, c // 2))
                    ps = banks.open(pe, (name, c), by)
                    banks.close(contract(ps[:, 0:T], [
                        (w[:, k, c % 2 * P:c % 2 * P + P], hT[:, k, :]) for k in range(KD)]))
                    if c % 2:
                        slab_done((name, c // 2))

            def project_N(name, by):
                w = [slab(pe, (name, h)) for h in range(2)]
                for t in range(NT):
                    ps = banks.open(pe, (name, t), by)
                    for h in range(2):
                        last = contract(ps[:, h * 256:(h + 1) * 256],
                                        [(hT[:, k, tok[t]], w[h][:, k, :]) for k in range(KD)])
                    banks.close(last)
                slab_done((name, 0), (name, 1))

            def ada_columns(i):
                banks.emptied(pe, ("ada_row", i))
                ps = banks.open(pe, ("ada", i), "dve")
                for c in range(2):
                    last = nc.tensor.transpose(ps[:, c * 2:c * 2 + 2], ada_row[0:2, i % 2, c * P:c * P + P],
                                               ident[0:2, 0:2])
                banks.close(last)

            def modulation(lo, hi, end):
                for i in range(lo, hi):
                    w = slab(pe, ("ada", i))
                    ps = banks.open(pe, ("ada_row", i), "act")
                    banks.close(contract(ps[0:2, 0:256], [(cond[:, k, :], w[:, k, :]) for k in range(KD)]))
                    slab_done(("ada", i))
                    if i not in (0, 8):
                        ada_columns(i - 1)
                if hi == end:
                    ada_columns(hi - 1)

            def flip_tokens(which):
                for t in range(NT):
                    pe.wait_ge(s_normed.sem, which * NT + t + 1)
                    for h in range(2):
                        flip4((which, "xt", t, h), ("act", "dve")[h],
                              [normed2[which][:, t % 2, (h * 4 + i) * P:(h * 4 + i + 1) * P] for i in range(4)])

            def merge(n, j):
                w = slab(pe, ("merge", n, j // 2))
                ps = banks.open(pe, ("merge", n, j), "act")
                banks.close(contract(ps[:, 0:T], [
                    (w[:, k, j % 2 * P:j % 2 * P + P], hT[:, k, :]) for k in range(KD)]))
                if j % 2:
                    slab_done(("merge", n, j // 2))

            def lift(n, lo, hi, merged=False):
                for j in range(lo, hi):
                    if not merged:
                        merge(n, j)
                    wb = slab(pe, ("wb", n, j // 4), CW)
                    if j == 0:
                        banks.emptied(pe, ("yt", n, NT - 1)) if n else banks.emptied(pe, ("yo", CW - 1))
                    ps = banks.open(pe, ("lift", n, j), "dve")
                    banks.close(contract(ps[:, 0:T], [
                        (wb[:, c, j % 4 * P:j % 4 * P + P], yT[:, n % 2, c, :]) for c in range(CW)]))
                    if j % 4 == 3:
                        slab_done(("wb", n, j // 4))

            def flip_output(n, src):
                for t in range(NT):
                    if n == 2:
                        pe.wait_ge(s_yn2.sem, t + 1)
                    else:
                        banks.emptied(pe, ({1: "ho", 3: "go"}[n], t))
                    flip4(("yt", n, t), "act", [src[:, t, c * P:(c + 1) * P] for c in range(CW)])

            pe.wait_ge(s_const.sem, 16 * N_IDENT)
            pe.wait_ge(s_vec.sem, 16 * N_VEC)
            for i in range(2):
                ps = banks.open(pe, ("pack", i), "act")
                n = (P, 88)[i]
                banks.close(nc.tensor.transpose(ps[:, 0:n], rows[0:n, i, :], ident[0:n, 0:n]))

            pe.wait_ge(s_fnet.sem, 16 * N_FNET)
            ps = banks.open(pe, "f1", "dve")
            banks.close(mm(ps[0:64, 0:T], lhsT=fw1[0:33, :], rhs=fnet[0:33, 0, :], start=True, stop=True))
            pe.wait_ge(s_sin.sem, 1)
            ps = banks.open(pe, "f2", "dve")
            banks.close(mm(ps[0:64, 0:T], lhsT=fw2[0:64, :], rhs=fnet[0:64, 1, :], start=True, stop=True))
            pe.wait_ge(s_sin.sem, 2)
            pe.wait_ge(s_fconst.sem, 16 * N_FCONST)
            for t in range(NT):
                for order in range(2):
                    for way in range(2):
                        ps = banks.open(pe, ("filt", t, order, way), "dve")
                        banks.close(mm(ps, lhsT=fnet[0:64, 2, tok[t]], start=True, stop=True,
                                       rhs=fw3[0:64, (way * 2 + order) * W:(way * 2 + order + 1) * W]))
            pe.wait_ge(s_sd.sem, 2 * NT)

            def spectrum(out, ft, ri, src):
                if ft == 0:
                    return contract(out, [(dft1[:, ri, :], src[0])])
                f = tok[ft - 1]
                return contract(out, [(dft2[:, ri, kt, f], src[1 + kt]) for kt in range(2)])

            for order in range(2):
                for ft in range(NT):
                    for ri in range(2):
                        ps = banks.open(pe, ("H", order, ft, ri), "dve" if ri == 0 else "act")
                        banks.close(spectrum(ps, ft, ri, [sd[:, order, ri, t, :] for t in range(NT)]))

            pe.wait_ge(s_cond.sem, 1)
            modulation(0, 8, 8)
            flip_tokens(0)
            banks.emptied(pe, (0, "xt", NT - 1, 0))
            banks.emptied(pe, (0, "xt", NT - 1, 1))
            for name in ("hy_v", "hy_x1", "hy_x2"):
                project_T(name, "dve")

            for i, name in enumerate(("hy_v", "hy_x1")):
                banks.emptied(pe, (name, CW - 1))
                for t in range(NT):
                    flip4(("hyt", i, t), "act", [hyT[:, i, c, tok[t]] for c in range(CW)])
            for order in range(2):
                if order == 0:
                    banks.emptied(pe, ("hyt", 0, NT - 1))
                else:
                    banks.emptied(pe, ("y", NT - 1))
                for ft in range(NT):
                    for ri in range(2):
                        ps = banks.open(pe, ("U", order, ft, ri), "dve")
                        banks.close(spectrum(ps, ft, ri, [hyN[:, 0, t, :] for t in range(NT)]))
                pe.wait_ge(s_spec.sem, (order + 1) * NT)
                if order == 0:
                    for t in range(NT):
                        ps = banks.open(pe, ("y", t), "dve")
                        if t == 0:
                            pairs = [(dft1[:, 2 + ri, :], spec[:, 0, ri, :]) for ri in range(2)]
                        else:
                            pairs = [(dft2[:, 2 + ri, ft, tok[t - 1]], spec[:, 1 + ft, ri, :])
                                     for ft in range(2) for ri in range(2)]
                        banks.close(contract(ps, pairs))
            for c in range(CW):
                ch = slice(c * P, (c + 1) * P)
                ps = banks.open(pe, ("yo", c), "dve")
                contract(ps[:, 0:P], [(spec[:, 0, ri, ch], dft1[:, 2 + ri, :]) for ri in range(2)])
                banks.close(contract(ps[:, P:T], [(spec[:, 1 + ft, ri, ch], dft2[:, 2 + ri, ft, :])
                                                  for ft in range(2) for ri in range(2)]))

            for name in ("hg_q", "hg_ff", "hg_fb"):
                project_T(name, "act")
            for name in ("hg_v", "hg_g"):
                project_N(name, "act")

            pe.wait_ge(s_const.sem, 16 * N_CONST)
            lift(0, 0, 2)
            for i in range(2 * LEVELS):
                pe.wait_ge(s_hqk.sem, i + 1)
                for t in range(NT):
                    ps = banks.open(pe, ("level", i, t), "dve")
                    for h in range(HG_H):
                        last = mm(ps[:, h * P:(h + 1) * P], lhsT=hqk[:, i % 2, h, tok[t]],
                                  rhs=hqk[:, i % 2, h, tok[t]], start=True, stop=True)
                    banks.close(last)
                if i < 10:
                    if i % 2 == 0:
                        merge(0, i // 2 + 2)
                    else:
                        lift(0, i // 2 + 2, i // 2 + 3, merged=True)
            lift(0, 7, 8)
            pe.wait_ge(s_hsum.sem, 1)
            for t in range(NT):
                ps = banks.open(pe, ("diag", t), "dve")
                for h in range(HG_H):
                    last = mm(ps[:, h * P:(h + 1) * P], lhsT=hk[:, 0, h, tok[t]], rhs=hq[:, h, tok[t]],
                              start=True, stop=True)
                banks.close(last)
            pe.wait_ge(s_hke.sem, 1)
            for d in range(2):
                for w in range(2):
                    flip4(("hke", d, w), "act", [hke[:, d, w, h, :] for h in range(HG_H)])
            for d in range(2):
                for w, t in ((0, 0), (1, FIRST[d])):
                    banks.emptied(pe, ("hke", d, w))
                    ps = banks.open(pe, ("hstate", d, w), "dve")
                    for h in range(HG_H):
                        last = mm(ps[:, h * P:(h + 1) * P], lhsT=hkn[:, d, w, h, :],
                                  rhs=hv[:, t, h * P:(h + 1) * P], start=True, stop=True)
                    banks.close(last)
            pe.wait_ge(s_hqe.sem, 1)
            pe.wait_ge(s_hst.sem, 32)
            for t in range(NT):
                banks.emptied(pe, ("diag", t))
                if t:
                    banks.emptied(pe, ("hstate", 1, 1))
                ps = banks.open(pe, ("ho", t), "dve")
                for h in range(HG_H):
                    pairs = [(hattn[:, t, h, :], hv[:, t, h * P:(h + 1) * P])]
                    if t:
                        for d in range(2):
                            pairs.append((hqe[:, d, h, (t - 1) * P:t * P], hst[:, d, int(t == SECOND[d]), h, :]))
                    last = contract(ps[:, h * P:(h + 1) * P], pairs)
                banks.close(last)
            flip_output(1, hyn)

            for name in ("ssd_x", "ssd_bc"):
                project_T(name, "dve")
            project_N("ssd_z", "act")
            pe.wait_ge(s_row.sem, 16 * N_ROW)
            for t in range(NT):
                ps = banks.open(pe, ("small", t), "dve")
                banks.close(contract(ps[:, 0:32], [(hT[:, k, tok[t]], smallw[:, k, :]) for k in range(KD)]))

            for t in range(NT):
                pe.wait_ge(s_small.sem, 1)
                ps = banks.open(pe, ("cum", t), "dve")
                for i in range(5):
                    last = mm(ps[:, i * 32:(i + 1) * 32], lhsT=sums[:, i, :], rhs=small[:, t, :],
                              start=True, stop=True)
                banks.close(last)
            pe.wait_ge(s_silu.sem, 1)
            for t in range(NT):
                flip4(("sx", t), "act", [sxT[:, 0, c, tok[t]] for c in range(CW)])
            pe.wait_ge(s_silu.sem, 2)
            for t in range(NT):
                flip4(("sb", t), "act", [sxT[:, 1, g, tok[t]] for g in range(2)])
            pe.wait_ge(s_sst.sem, 32)
            for d in range(2):
                flip4(("sin", d), "act", [s_in[:, d, i, :] for i in range(4)])

            for d in range(2):
                for w, t in ((0, 0), (1, FIRST[d])):
                    banks.emptied(pe, ("sb", NT - 1))
                    pe.wait_ge(s_sxe.sem, 2 * d + w + 1)
                    ps = banks.open(pe, ("sstate", d, w), "dve")
                    for i in range(4):
                        if w == 0:
                            last = mm(ps[:, i * P:(i + 1) * P], lhsT=sxd[:, w, i * P:(i + 1) * P],
                                      rhs=sbN[:, t, i // 2, :], start=True, stop=True)
                        elif i < 2:
                            last = mm(ps[:, i * 256:(i + 1) * 256], lhsT=sbN[:, t, i, :],
                                      rhs=sxd[:, w, i * 256:(i + 1) * 256], start=True, stop=True)
                    banks.close(last)
            banks.emptied(pe, ("sstate", 1, 1))
            banks.emptied(pe, ("sin", 1))
            for t in range(NT):
                ps = banks.open(pe, ("cb", t), "dve")
                for g in range(2):
                    last = mm(ps[:, g * P:(g + 1) * P], lhsT=sxT[:, 1, g, tok[t]], rhs=sxT[:, 1, 2 + g, tok[t]],
                              start=True, stop=True)
                banks.close(last)
                for d in range(2):
                    for q in range(2):
                        decay(mm, banks, pe, ("sdec", t, d, q), ident, reach[:, d, :],
                              [(small[:, t, small_cols["ssd"][d]][:, q * 4 + h:q * 4 + h + 1], sums[:, d, :])
                               for h in range(4)])
                if t:
                    for d in range(2):
                        ps = banks.open(pe, ("sinter", t, d), "dve")
                        for g in range(2):
                            last = mm(ps[:, g * 256:(g + 1) * 256], lhsT=sxT[:, 1, 2 + g, tok[t]],
                                      rhs=sst[:, d, int(t == SECOND[d]), g * 256:(g + 1) * 256],
                                      start=True, stop=True)
                        banks.close(last)
                pe.wait_ge(s_sw.sem, t + 1)
                ps = banks.open(pe, ("sintra", t), "dve")
                for h in range(SSD_H):
                    last = contract(ps[:, h * 64:(h + 1) * 64],
                                    [(sdec[:, d, h // 4, h % 4, :], sxd[:, d, h * 64:(h + 1) * 64])
                                     for d in range(2)])
                banks.close(last)
                lift(1, (0, 3, 6)[t], (3, 6, 8)[t])
            flip_output(2, sy_out)

            for name in ("gdn_q", "gdn_k", "gdn_v"):
                project_T(name, "dve")
            for i in range(3):
                pe.wait_ge(s_silu.sem, 3 + i)
                for t in range(NT):
                    flip4(("gn", i, t), "act", [gT[:, i, c, tok[t]] for c in range(CW)])
            modulation(8, 11, 24)
            pe.wait_ge(s_gnorm.sem, 1)
            for i in range(2):
                for t in range(NT):
                    flip4(("gt", i, t), "act", [gN[:, i, t, h * P:(h + 1) * P] for h in range(GDN_H)])
            banks.emptied(pe, ("gt", 1, NT - 1))

            for r in range(NT):
                tt = [r, (0, 2, 1)[r]]
                for d in range(2):
                    t = tt[d]
                    la = small[:, t, small_cols["gdn"][d]]
                    lbeta = small[:, t, small_cols["beta"][d]]
                    for key, mask, beta in (("gincl", d, False), ("gstrict", 2 + d, True)):
                        decay(mm, banks, pe, (key, r, d), ident, reach[:, mask, :],
                              [(la[:, h:h + 1], sums[:, d, :]) for h in range(GDN_H)],
                              [lbeta[:, h:h + 1] for h in range(GDN_H)] if beta else None)
                    for key, i in (("gkk", 1), ("gqk", 0)):
                        ps = banks.open(pe, (key, r, d), "dve")
                        for h in range(GDN_H):
                            last = mm(ps[:, h * P:(h + 1) * P], lhsT=gT[:, 1, h, tok[t]],
                                      rhs=gT[:, i, h, tok[t]], start=True, stop=True)
                        banks.close(last)
                for l in range(LEVELS):
                    for d in range(2):
                        pe.wait_ge(s_glevel[d].sem, r * LEVELS + l + 1)
                        if l == 1:
                            banks.emptied(pe, ("gprod", r, 0, d))
                        elif l:
                            banks.emptied(pe, ("ginv", r, l - 1, d))
                            banks.emptied(pe, ("ginvT", r, l - 1, d))
                        ps = banks.open(pe, ("gprod", r, l, d), "dve" if l == 0 else "act")
                        for h in range(GDN_H):
                            last = mm(ps[:, h * P:(h + 1) * P], lhsT=gw[:, d, 1, h, :],
                                      rhs=ident[:, :] if l == 0 else gw[:, d, 2, h, :], start=True, stop=True)
                        banks.close(last)
                    for d in range(2):
                        if l == 0:
                            continue
                        if d == 0:
                            if r and l in (2, 3, 4, 5):
                                merge(2, (r - 1) * 4 + l - 2)
                            elif r == 0 and l < LEVELS - 1:
                                modulation(LATE_ADA[l][0], LATE_ADA[l][0] + 1, 24)
                        banks.emptied(pe, ("gprod", r, l, d))
                        if l < LEVELS - 1:
                            ps = banks.open(pe, ("ginv", r, l, d), "dve")
                            for h in range(GDN_H):
                                last = mm(ps[:, h * P:(h + 1) * P], lhsT=gw[:, d, 3, h, :],
                                          rhs=gw[:, d, 4, h, :], start=True, stop=True)
                            banks.close(last)
                        ps = banks.open(pe, ("ginvT", r, l, d), "dve")
                        for h in range(GDN_H):
                            last = mm(ps[:, h * P:(h + 1) * P], lhsT=gw[:, d, 4, h, :],
                                      rhs=gw[:, d, 3, h, :], start=True, stop=True)
                        banks.close(last)
                    if r == 0:
                        lo, hi = LATE_ADA[l]
                        modulation(lo + int(0 < l < LEVELS - 1), hi, 24)
                    elif l in (2, 3, 4, 5):
                        n = (r - 1) * 4 + l - 2
                        lift(2, n, n + 1, merged=True)
                for d in range(2):
                    t = tt[d]
                    banks.emptied(pe, ("ginvT", r, LEVELS - 1, d))
                    pe.wait_ge(s_gvk[d].sem, r + 1)
                    if r:
                        ps = banks.open(pe, ("gwT", r, d), "act")
                        for h in range(GDN_H):
                            last = mm(ps[:, h * P:(h + 1) * P], lhsT=gw[:, d, 4, h, :], rhs=gw[:, d, 3, h, :],
                                      start=True, stop=True)
                        banks.close(last)
                        banks.emptied(pe, ("gwT", r, d))
                        if r == 2:
                            banks.emptied(pe, ("gstate", 1, d))
                        else:
                            pe.wait_ge(s_gst.sem, 32)
                    ps = banks.open(pe, ("gv", r, d), "act")
                    for h in range(GDN_H):
                        pairs = [(gw[:, d, 3, h, :], gw[:, d, 2, h, :])]
                        if r:
                            pairs.append((gw[:, d, 1, h, :], (gs0, gs1)[r - 1][:, d, h, :]))
                        last = contract(ps[:, h * P:(h + 1) * P], pairs)
                    banks.close(last)
                    if r < 2:
                        banks.emptied(pe, ("gv", r, d))
                        ps = banks.open(pe, ("gstate", r, d), "dve")
                        for h in range(GDN_H):
                            last = mm(ps[:, h * P:(h + 1) * P], lhsT=gw[:, d, 0, h, :], rhs=gvn[:, t, d, h, :],
                                      start=True, stop=True)
                        banks.close(last)
            for d in range(2):
                for t in (1, 2):
                    ps = banks.open(pe, ("grow", t, d), "act")
                    for h in range(GDN_H):
                        c = small[:, t, small_cols["gdn"][d]][:, h:h + 1]
                        last = mm(ps[:, h * P:(h + 1) * P], lhsT=c.to_broadcast([P, P]), rhs=sums[:, d, :],
                                  start=True, stop=True)
                    banks.close(last)
            project_N("gdn_g", "act")
            pe.wait_ge(s_gqe.sem, 4)
            for t in range(NT):
                banks.emptied(pe, ("gv", 2, 1))
                ps = banks.open(pe, ("go", t), "dve")
                for h in range(GDN_H):
                    pairs = []
                    for d in range(2):
                        pairs.append((gqk[:, t, d, h, :], gvn[:, t, d, h, :]))
                        if t:
                            pairs.append((gqe[:, d, h, (t - 1) * P:t * P],
                                          (gs0, gs1)[int(t == SECOND[d])][:, d, h, :]))
                    last = contract(ps[:, h * P:(h + 1) * P], pairs)
                banks.close(last)
            flip_output(3, gyn)
            lift(3, 0, 8)

            for cnd in range(2):
                for h in range(2):
                    ps = banks.open(pe, ("grow", 2, cnd, h), "act")
                    for i in range(4):
                        c = mod[:, 2 * KD + h * 4 + i, cnd:cnd + 1]
                        last = mm(ps[:, i * P:(i + 1) * P], lhsT=c.to_broadcast([P, P]), rhs=ident[:, :],
                                  start=True, stop=True)
                    banks.close(last)
            pe.wait_ge(s_madd.sem, 3 * KD)
            for c in range(4):
                w = slab(pe, ("w_out", c))
                for t in range(NT):
                    ps = banks.open(pe, ("out", c, t), "dve")
                    banks.close(contract(ps[:, 0:256], [(mixed[:, k, tok[t]], w[:, k, :]) for k in range(KD)]))
                slab_done(("w_out", c))
            flip_tokens(1)
            banks.emptied(pe, (1, "xt", NT - 1, 0))
            banks.emptied(pe, (1, "xt", NT - 1, 1))
            pe.wait_ge(s_late.sem, 16 * N_LATE)
            for t in range(NT):
                ps = banks.open(pe, ("router", t), "act")
                banks.close(contract(ps[:, 0:NE], [(hT[:, k, tok[t]], router_w[:, k, :]) for k in range(KD)]))
            for t in range(NT):
                for h in range(2):
                    flip4(("h2", t, h), "dve", [hT[:, h * 4 + i, tok[t]] for i in range(4)])

            for by in ("act", "dve"):
                pe.wait_ge(banks.freed[by], banks.count[by])
            pe.wait_ge(s_shared.sem, 48)
            for f in range(2):
                for i in range(2):
                    if f:
                        pe.wait_ge((s_sil, s_hid)[i].sem, 1)
                    w = wsh[:, i, :].rearrange("p (k n) -> p k n", k=KD)
                    contract(psum[:, 6 + i, 0:T], [(w[:, k, f * P:(f + 1) * P], hT[:, k, :]) for k in range(KD)]
                             ).then_inc((s_h1, s_h3)[i].sem, 1)
            pe.wait_ge(s_hid.sem, 2)
            w = wsh[:, 2, :].rearrange("p (f n) -> p f n", f=2)
            for t in range(NT):
                for h in range(2):
                    for f in range(2):
                        mm(psum[:, t * 2 + h, :], lhsT=hid[:, f, tok[t]], rhs=w[:, f, h * W:(h + 1) * W],
                           start=f == 0, stop=False)
            pe.wait_ge(s_gates.sem, NT)
            for t in range(NT):
                pairs = [(sums[:, 3, :], chosen[:, t, :])] + [(sums[:, 4, :], chosen[:, u, :]) for u in range(t)]
                contract(psum[:, 6, t * NE:(t + 1) * NE], pairs)
            contract(psum[:, 6, NT * NE:(NT + 1) * NE], [(sums[:, 4, :], chosen[:, t, :]) for t in range(NT)]
                     ).then_inc(s_ranks.sem, 1)
            for t in range(NT):
                last = nc.tensor.transpose(psum[0:NE, 7, tok[t]], egN[:, t, :], ident[:, :])
            last.then_inc(s_rowsT.sem, 1)
            pe.wait_ge(s_placed.sem, 1)
            for t in range(NT):
                last = nc.tensor.transpose(psum[0:NE, 6, tok[t]], places[:, t, 0:NE], ident[:, :])
            last.then_inc(s_rowsT.sem, 1)

        C0 = {name: COL[name] // P for name in COL if COL[name] < 4096}
        conv_to = {"hy_v": hyT[:, 0], "hy_x1": hyT[:, 1], "hy_x2": hyT[:, 2], "ssd_x": sxT[:, 0],
                   "ssd_bc": sxT[:, 1], "gdn_q": gT[:, 0], "gdn_k": gT[:, 1], "gdn_v": gT[:, 2]}
        conv_order = {name: i for i, name in enumerate(conv_to)}
        silu_order = {name: i for i, name in enumerate(("ssd_x", "ssd_bc", "gdn_q", "gdn_k", "gdn_v"))}
        cwt, cvec = cols[:, 0, :], cols[:, 1, :]
        flat = lambda v: v.rearrange("p a b -> p (a b)")
        halves4 = lambda v: v.rearrange("p (h k) -> p h k", h=4)

        @block.scalar
        def _(act):
            lane = Lane(act, s_act)
            on = nc.scalar.activation

            def copy(out, key, func=ACT.Copy, **kw):
                banks.free(on(out, banks.at(act, key) if "src" not in kw else kw.pop("src"), func, **kw), key)

            def modulation(lo, hi):
                for i in range(lo, hi):
                    key = ("ada_row", i)
                    copy(ada_row[0:2, i % 2, :], key, src=banks.at(act, key)[0:2, 0:256])

            def norm_tokens(which):
                for t in range(NT):
                    s_ss.on(on(early[:, t * D:(t + 1) * D], x[:, t, :], ACT.Square,
                               accum_out=ss[:, which * 3 + t:which * 3 + t + 1]))
                if which == 0:
                    modulation(0, 8)
                act.wait_ge(s_pre.sem, ROOT["norm"][which])
                s_rs.on(on(ss[:, 8 + which * 3:11 + which * 3], ss[:, 8 + which * 3:11 + which * 3], ACT.Sqrt))
                act.wait_ge(s_rcp.sem, which + 1)
                for t in range(NT):
                    if t == 2:
                        banks.at(act, (which, "xt", 0, 1))
                    s_normed.on(on(normed2[which][:, t % 2, :], x[:, t, :], ACT.Copy,
                                   scale=ss[:, 8 + which * 3 + t:9 + which * 3 + t]))
                    if t:
                        modulate(which, t - 1)
                modulate(which, NT - 1)

            def modulate(which, t):
                ps = banks.at(act, (which, "xt", t, 0))
                if t == 0:
                    act.wait_ge(s_mod.sem, which + 1)
                for i in range(4):
                    ins = on(hT[:, i, tok[t]], ps[:, i * P:(i + 1) * P], ACT.Identity,
                             scale=scale1[:, which, i, cmod[t]:cmod[t] + 1],
                             bias=mod[:, which * 24 + i, cmod[t]:cmod[t] + 1])
                    if i < 3:
                        lane.do(ins)
                banks.free(ins, (which, "xt", t, 0))

            def conv_centre(name):
                for c in range(CW):
                    j = C0[name] + c
                    s_conv.on(on(conv_to[name][:, c, :], banks.at(act, (name, c))[:, 0:T], ACT.Identity,
                                 scale=cwt[:, 32 + j:33 + j], bias=cwt[:, 96 + j:97 + j]))

            def silu(name):
                banks.emptied(act, (name, CW - 1))
                v = flat(conv_to[name])
                s_silu.on(on(v, v, ACT.Silu))

            def merge_gate(n, j):
                key = ("merge", n, j)
                ps = banks.at(act, key)
                if j >= 2 or n:
                    banks.emptied(act, ("lift", n, j - 2) if j >= 2 else ("lift", n - 1, j + 6))
                banks.free(on(gate[:, j % 2, :], ps[:, 0:T], ACT.Sigmoid), key)

            def root(i, cols_):
                act.wait_ge(s_pre.sem, i)
                s_rs.on(on(cols_, cols_, ACT.Sqrt))

            def flip_output(n):
                for t in range(NT):
                    ps = banks.at(act, ("yt", n, t))
                    banks.free(on(yT[:, n % 2, :, tok[t]], halves4(ps), ACT.Copy), ("yt", n, t))

            for i in range(2):
                n = (P, 88)[i]
                copy(cols[:, i, 0:n], ("pack", i), src=banks.at(act, ("pack", i))[:, 0:n])
            banks.emptied(act, ("pack", 1))
            s_cond.on(on(cond[:, :, :].rearrange("p k c -> p c k"),
                         cvec[:, 64:80].rearrange("p (c k) -> p c k", c=2), ACT.Silu))
            act.wait_ge(s_lb.sem, 1)
            s_lbe.on(on(lb[:, 0, :], lb[:, 0, :], ACT.Exp))
            for i in range(2):
                act.wait_ge(s_arg.sem, i + 1)
                s_sin.on(on(fnet[0:64, 1 + i, :], fnet[0:64, 3, :], ACT.Sin))
            for order in range(2):
                for ft in range(NT):
                    copy(hf[:, order, ft, 1, :], ("H", order, ft, 1))
            act.wait_ge(s_x.sem, 16 * NT)
            banks.emptied(act, ("H", 1, NT - 1, 0))
            norm_tokens(0)
            for name in ("hy_v", "hy_x1", "hy_x2"):
                conv_centre(name)
            for i in range(2):
                for t in range(NT):
                    copy(hyN[:, i, t, :], ("hyt", i, t))

            banks.emptied(act, ("yo", CW - 1))
            for d in range(2):
                act.dma_start(hst[:, d, 0], a["state_hgrn"][0, 0, d].rearrange("h k v -> k h v")).then_inc(s_hst.sem, 16)
            for c in range(CW):
                key = ("hg_q", c)
                copy(hq[:, c, :], key, ACT.Silu, src=banks.at(act, key)[:, 0:T])
            for d in range(2):
                for c in range(CW):
                    key = (("hg_ff", "hg_fb")[d], c)
                    ps = banks.at(act, key)[:, 0:T]
                    lane.do(on(he[:, d, c, :], ps, ACT.Sigmoid))
                    banks.free(on(hk[:, d, c, :], ps, ACT.Sigmoid, scale=-1.0), key)
            for t in range(NT):
                copy(hv[:, t, :], ("hg_v", t))
            for t in range(NT):
                copy(hg[:, t, :], ("hg_g", t), ACT.Silu)
            for d in range(2):
                act.wait_ge(s_hf.sem, d + 1)
                s_hlog.on(on(flat(he[:, d]), flat(he[:, d]), ACT.Ln))
            for i in range(2 * LEVELS):
                act.wait_ge(s_hd.sem, i + 1)
                s_he.on(on(flat(he[:, i % 2]), flat(he[:, i % 2]), ACT.Exp))
                if i == 0:
                    merge_gate(0, 0)
                    merge_gate(0, 1)
                elif i < 10 and i % 2:
                    merge_gate(0, i // 2 + 2)
            act.wait_ge(s_hx.sem, 1)
            lane.do(on(arena[:, 5 * U:5 * U + 2048], arena[:, 5 * U:5 * U + 2048], ACT.Exp))
            for d in range(2):
                lane.link(on(coef[:, d, 0:HG_H], hb[:, d, :, (2 * P - 1, 2 * P)[d]], ACT.Exp))
                lane.do(on(hqe[:, d], hb[:, d, :, P:T], ACT.Exp))
            s_hy.on(on(coef[:, 2, 0:4], coef[:, 0, 0:4], ACT.Copy))
            merge_gate(0, 7)
            for d in range(2):
                for w in range(2):
                    key = ("hke", d, w)
                    copy(hkn[:, d, w], key, src=halves4(banks.at(act, key)))
            for t in range(NT):
                ps = banks.at(act, ("ho", t))
                if t:
                    banks.emptied(act, ("ho", t - 1))
                s_ss.on(on(sq[:, :], ps, ACT.Square))
                root(ROOT["hg"] + t, ss[:, 16 + 4 * t:20 + 4 * t])
            flip_output(1)

            for name in ("ssd_x", "ssd_bc"):
                if name == "ssd_x":
                    banks.at(act, ("yt", 1, NT - 1))
                    for d in range(2):
                        banks.emptied(act, ("hstate", d, 0))
                        act.dma_start(o["new_hgrn"][0, 0, d].rearrange("h k v -> k h v"), hnew[:, d]).then_inc(s_out.sem, 16)
                    for d in range(2):
                        act.dma_start(s_in[:, d], a["state_ssd"][0, 0, d].rearrange("(a q) p n -> (q p) a n", q=2)).then_inc(s_sst.sem, 16)
                conv_centre(name)
            silu("ssd_x")
            silu("ssd_bc")
            for t in range(NT):
                copy(sz[:, t, :], ("ssd_z", t), ACT.Silu)
            act.wait_ge(s_sp.sem, 1)
            s_spa.on(on(flat(small2[:, :, :]), flat(small2[:, :, :]), ACT.Exp))
            act.wait_ge(s_sp.sem, 2)
            s_spa.on(on(flat(small2[:, :, :]), flat(small2[:, :, :]), ACT.Ln))
            act.wait_ge(s_row.sem, 16 * N_ROW)
            act.wait_ge(s_pool.sem, 3)
            s_spa.on(on(small_row[:, 1, :], small_row[:, 1, :], ACT.Exp))
            banks.emptied(act, ("cum", NT - 1))
            lane.do(on(beta[:, :, :], small2[:, :, 24:32], ACT.Exp, scale=-1.0))
            s_ecum.on(on(ecum[:, :, :, :].rearrange("p a b c -> p (a b c)"),
                         cum[:, :, :, :].rearrange("p a b c -> p (a b c)"), ACT.Exp, scale=-1.0))
            for t in range(NT):
                copy(sxN[:, t, :], ("sx", t))
            for t in range(NT):
                key = ("sb", t)
                copy(sbN[:, t], key, src=banks.at(act, key)[:, 0:256].rearrange("p (g n) -> p g n", g=2))
            for d in range(2):
                copy(sst[:, d, 0, :], ("sin", d))

            def decays(key, out, t, heads, d):
                ps = banks.at(act, key)
                for h in range(4):
                    c = cum[:, t, d, heads.start + h:heads.start + h + 1]
                    ins = on(out[:, h, :], ps[:, h * P:(h + 1) * P], ACT.Exp, bias=c)
                    if h < 3:
                        lane.do(ins)
                banks.free(ins, key)

            for t in range(NT):
                if t:
                    banks.at(act, ("sintra", t - 1))
                for d in range(2):
                    for q in range(2):
                        heads = slice(small_cols["ssd"][d].start + 4 * q, 0)
                        decays(("sdec", t, d, q), sdec[:, d, q], t, heads, d)
                for j in range((0, 3, 6)[t], (3, 6, 8)[t]):
                    merge_gate(1, j)
                act.wait_ge(s_sg.sem, t + 1)
                s_ss.on(on(sy[:, 2, :], sy[:, 1, :], ACT.Square))
                root(ROOT["ssd"] + t, ss[:, 28 + 2 * t:30 + 2 * t])
            flip_output(2)

            banks.at(act, ("yt", 2, NT - 1))
            for d in range(2):
                act.dma_start(o["new_ssd"][0, 0, d].rearrange("(a q) p n -> (q p) a n", q=2), snew[:, d]).then_inc(s_out.sem, 16)
            act.wait_ge(s_out.sem, 64)
            for name in ("gdn_q", "gdn_k", "gdn_v"):
                conv_centre(name)
            silu("gdn_q")
            silu("gdn_k")
            silu("gdn_v")
            for i in range(3):
                for t in range(NT):
                    copy(gN[:, i, t, :], ("gn", i, t))
            modulation(8, 11)
            root(ROOT["qk"], ss[:, 34:58])
            for i in range(2):
                for t in range(NT):
                    key = ("gt", i, t)
                    copy(gT[:, i, :, tok[t]], key, src=halves4(banks.at(act, key)))
            for d in range(2):
                act.dma_start(gs0[:, d], a["state_gdn"][0, 0, d].rearrange("h k v -> k h v")).then_inc(s_gst.sem, 16)
            for r in range(NT):
                tt = [r, (0, 2, 1)[r]]
                if r == 1:
                    for d in range(2):
                        banks.emptied(act, ("gstate", 0, d))
                        act.dma_start(o["new_gdn"][0, 0, d].rearrange("h k v -> k h v"), gs1[:, d]).then_inc(s_out.sem, 16)
                for d in range(2):
                    if r:
                        banks.at(act, ("gstate", r - 1, d))
                    t = tt[d]
                    decays(("gincl", r, d), gqk[:, t, d], t, small_cols["gdn"][d], d)
                    decays(("gstrict", r, d), gw[:, d, 0], t, small_cols["gdn"][d], d)
                if r == 0:
                    modulation(*LATE_ADA[0])
                for l in range(1, LEVELS):
                    for d in range(2):
                        key = ("gprod", r, l, d)
                        copy(gw[:, d, 4], key, src=halves4(banks.at(act, key)))
                    if r == 0:
                        modulation(*LATE_ADA[l])
                    if r and l in (2, 3, 4, 5):
                        merge_gate(2, (r - 1) * 4 + l - 2)
                for d in range(2):
                    if r:
                        key = ("gwT", r, d)
                        copy(gw[:, d, 1], key, src=halves4(banks.at(act, key)), scale=-1.0)
                    key = ("gv", r, d)
                    copy(gvn[:, tt[d], d], key, src=halves4(banks.at(act, key)))
            for d in range(2):
                for t in (1, 2):
                    key = ("grow", t, d)
                    copy(gqe[:, d, :, (t - 1) * P:t * P], key, ACT.Exp, src=halves4(banks.at(act, key)))
            for t in range(NT):
                copy(gz[:, t, :], ("gdn_g", t), ACT.Silu)
            for t in range(NT):
                ps = banks.at(act, ("go", t))
                if t:
                    banks.emptied(act, ("go", t - 1))
                s_ss.on(on(sq[:, :], ps, ACT.Square))
                root(ROOT["gdn"] + t, ss[:, 16 + 4 * t:20 + 4 * t])
            flip_output(3)
            for j in range(8):
                merge_gate(3, j)

            banks.at(act, ("yt", 3, NT - 1))
            for cnd in range(2):
                for h in range(2):
                    copy(g1row[:, cnd, h * W:(h + 1) * W], ("grow", 2, cnd, h))
            act.wait_ge(s_x2.sem, 1)
            norm_tokens(1)
            for t in range(NT):
                key = ("router", t)
                copy(pick[:, t, :], key, ACT.Sigmoid, src=banks.at(act, key)[:, 0:NE])

            for t in range(NT):
                for h in range(2):
                    banks.at(act, ("h2", t, h))
                    s_h2.on(on(h2[0][:, t, h * W:(h + 1) * W], banks.look(("h2", t, h)), ACT.Copy))
            for f in range(2):
                act.wait_ge(s_h1.sem, f + 1)
                s_sil.on(on(sil[:, f, :], psum[:, 6, 0:T], ACT.Silu))

        @block.vector
        def _(dve):
            lane = Lane(dve, s_dve)
            v = nc.vector
            tt, ts, stt = v.tensor_tensor, v.tensor_scalar, v.scalar_tensor_tensor

            def each(w, n=W):
                return w[:, :, None].to_broadcast([P, w.shape[1], n // w.shape[1]])

            def inverse_root(i, c, scale, eps=EPS):
                lane.wait_own()
                s_pre.on(ts(c, c, scale, eps, ALU.mult, ALU.add))
                assert s_pre.n == i, (s_pre.n, i)
                dve.wait_ge(s_rs.sem, i)
                lane.link(v.reciprocal(c, c))

            def norm_tokens(which):
                dve.wait_ge(s_ss.sem, SQ["norm"][which] + NT)
                c = ss[:, 8 + which * 3:11 + which * 3]
                lane.link(ts(c, ss[:, which * 3:which * 3 + 3], 1.0, None, ALU.mult))
                s_pre.on(ts(c, c, 1.0 / D, EPS, ALU.mult, ALU.add))
                dve.wait_ge(s_rs.sem, ROOT["norm"][which])
                s_rcp.on(v.reciprocal(c, c))

            def modulate(which):
                dve.wait_ge(s_mod.sem, which + 1)
                for t in range(NT):
                    ps = banks.at(dve, (which, "xt", t, 1))
                    for i in range(4):
                        ins = ts(hT[:, 4 + i, tok[t]], ps[:, i * P:(i + 1) * P],
                                 scale1[:, which, 4 + i, cmod[t]:cmod[t] + 1],
                                 mod[:, which * 24 + 4 + i, cmod[t]:cmod[t] + 1], ALU.mult, ALU.add)
                        if i < 3:
                            lane.do(ins)
                    banks.free(ins, (which, "xt", t, 1))

            def ada_columns(lo, hi):
                for i in range(lo, hi):
                    ps = banks.at(dve, ("ada", i))
                    banks.free(tt(mod[:, 2 * i:2 * i + 2, :], ps[:, 0:4].rearrange("p (j c) -> p j c", j=2),
                                  cvec[:, 2 * i:2 * i + 2, None].to_broadcast([P, 2, 2]), ALU.add), ("ada", i))

            def scales(which):
                banks.emptied(dve, ("ada", which * 12 + 7))
                g = cvec[:, 48 + which * 8:56 + which * 8, None].to_broadcast([P, KD, 2])
                s_mod.on(stt(scale1[:, which], mod[:, which * 24 + 8:which * 24 + 16, :], 1.0, g, ALU.add, ALU.mult))

            def conv(name):
                for c in range(CW):
                    j = C0[name] + c
                    ps = banks.at(dve, (name, c))[:, 0:T]
                    out = conv_to[name][:, c, :]
                    out6, ps6 = (m.rearrange("p (r n) -> p r n", n=GRID) for m in (out, ps))
                    dve.wait_ge(s_conv.sem, conv_order[name] * CW + c + 1)
                    lane.do(stt(out6[:, :, 1:], ps6[:, :, :-1], cwt[:, j:j + 1], out6[:, :, 1:], ALU.mult, ALU.add))
                    lane.link(stt(out[:, 64:65], ps[:, 63:64], cwt[:, j:j + 1], out[:, 64:65], ALU.mult, ALU.add))
                    lane.do(stt(out6[:, :, :-1], ps6[:, :, 1:], cwt[:, 64 + j:65 + j], out6[:, :, :-1],
                                ALU.mult, ALU.add))
                    banks.free(stt(out[:, 63:64], ps[:, 64:65], cwt[:, 64 + j:65 + j], out[:, 63:64],
                                   ALU.mult, ALU.add), (name, c))

            def lift(n, lo, hi):
                for j in range(lo, hi):
                    key = ("lift", n, j)
                    ps = banks.at(dve, key)[:, 0:T]
                    banks.emptied(dve, ("merge", n, j))
                    if n == 0:
                        banks.free(tt(mixed[:, j, :], ps, gate[:, j % 2, :], ALU.mult), key)
                    else:
                        k = (n - 1) * KD + j
                        if k >= 2:
                            dve.wait_ge(s_madd.sem, k - 1)
                        banks.free(tt(lifted[:, j % 2, :], ps, gate[:, j % 2, :], ALU.mult), key)

            def head_norm(n, key, t, c, g, out, root):
                ps = banks.at(dve, (key, t))
                dve.wait_ge(s_ss.sem, SQ[key] + t + 1)
                lane.link(v.reduce_sum(c, halves4(sq[:, :]), axis=AX))
                inverse_root(root + t, c, 1.0 / P)
                for h in range(4):
                    hh = slice(h * P, (h + 1) * P)
                    ins = stt(out[:, t, hh], ps[:, hh], c[:, h:h + 1], g[:, t, hh], ALU.mult, ALU.mult)
                    if h < 3:
                        lane.do(ins)
                banks.free(ins, (key, t))

            banks.emptied(dve, ("pack", 1))
            s_lb.on(tt(lb[:, 0, :], cvec[:, 80:88], cvec[:, 80:88], ALU.subtract))
            dve.wait_ge(s_lbe.sem, 1)
            lane.link(v.reciprocal(lb[:, 1, :], lb[:, 0, :]))
            lane.link(tt(lb[:, 1, :], lb[:, 0, :], lb[:, 1, :], ALU.mult))
            lane.link(tt(lb[:, 2, :], lb[:, 1, :], lb[:, 1, :], ALU.subtract))
            lane.link(ts(lb[:, 3, :], lb[:, 2, :], -1.0, 1.0, ALU.mult, ALU.add))

            dve.wait_ge(s_fnet.sem, 16 * N_FNET)
            for i, (key, work) in enumerate((("f1", 2), ("f2", 0))):
                xx, k = fnet[0:64, 3, :], fnet[0:64, work, :]
                ps = banks.at(dve, key)
                if i:
                    dve.wait_ge(s_sin.sem, 1)
                banks.free(ts(xx, ps[0:64, 0:T], fbias[:, i:i + 1], None, ALU.add), key)
                banks.emptied(dve, key)
                lane.link(ts(k, xx, 1.0 / (2 * math.pi), ROUND, ALU.mult, ALU.add))
                lane.link(ts(k, k, ROUND, None, ALU.subtract))
                lane.link(stt(xx, k, -TAU_HI, xx, ALU.mult, ALU.add))
                lane.link(stt(xx, k, -TAU_LO, xx, ALU.mult, ALU.add))
                s_arg.on(ts(xx, xx, PI32, -PI32, ALU.min, ALU.max))
            dve.wait_ge(s_fconst.sem, 16 * N_FCONST)
            for t in range(NT):
                for order in range(2):
                    for way in range(2):
                        key = ("filt", t, order, way)
                        banks.free(tt(hf[:, order, t, way, :], banks.at(dve, key), window[:, t, way, :], ALU.mult), key)
                    banks.emptied(dve, ("filt", t, order, 1))
                    lane.link(tt(sd[:, order, 0, t, :], hf[:, order, t, 0, :], hf[:, order, t, 1, :], ALU.add))
                    s_sd.on(tt(sd[:, order, 1, t, :], hf[:, order, t, 1, :], hf[:, order, t, 0, :], ALU.subtract))
            for order in range(2):
                for ft in range(NT):
                    key = ("H", order, ft, 0)
                    banks.free(tt(hf[:, order, ft, 0, :], banks.at(dve, key), hbias[:, order, :], ALU.add), key)

            ada_columns(0, 8)
            norm_tokens(0)
            scales(0)
            modulate(0)
            for name in ("hy_v", "hy_x1", "hy_x2"):
                conv(name)

            for order in range(2):
                for ft in range(NT):
                    U_, H_ = [banks.at(dve, ("U", order, ft, ri)) for ri in range(2)], hf[:, order, ft]
                    if order == 0:
                        banks.emptied(dve, ("H", order, ft, 1))
                    lane.do(tt(hy_t[:, 0, :], U_[0], H_[:, 0, :], ALU.mult))
                    banks.free(tt(hy_t[:, 1, :], U_[0], H_[:, 1, :], ALU.mult), ("U", order, ft, 0))
                    lane.do(tt(hy_t[:, 2, :], U_[1], H_[:, 1, :], ALU.mult))
                    banks.free(tt(hy_t[:, 3, :], U_[1], H_[:, 0, :], ALU.mult), ("U", order, ft, 1))
                    banks.emptied(dve, ("U", order, ft, 1))
                    lane.link(tt(spec[:, ft, 0, :], hy_t[:, 0, :], hy_t[:, 2, :], ALU.add))
                    s_spec.on(tt(spec[:, ft, 1, :], hy_t[:, 1, :], hy_t[:, 3, :], ALU.subtract))
                    dve.wait_ge(s_spec.sem, s_spec.n)
                if order == 0:
                    banks.emptied(dve, ("hyt", 1, NT - 1))
                    for t in range(NT):
                        banks.free(tt(hyN[:, 0, t, :], banks.at(dve, ("y", t)), hyN[:, 1, t, :], ALU.mult), ("y", t))
            for c in range(CW):
                banks.free(tt(yT[:, 0, c, :], banks.at(dve, ("yo", c))[:, 0:T], hyT[:, 2, c, :], ALU.mult), ("yo", c))

            lows = hqk
            for d in range(2):
                name = ("hg_ff", "hg_fb")[d]
                banks.emptied(dve, (name, CW - 1))
                for c in range(CW):
                    k = d * CW + c
                    lane.do(ts(he[:, d, c, :], he[:, d, c, :], lb[:, 3, k:k + 1], lb[:, 2, k:k + 1], ALU.mult, ALU.add))
                    lane.do(ts(hk[:, d, c, :], hk[:, d, c, :], lb[:, 3, k:k + 1], None, ALU.mult))
                lane.wait_own()
                lane.link(ts(flat(he[:, d]), flat(he[:, d]), FLOOR, None, ALU.max))
                lane.link(ts(flat(lows[:, d]), flat(he[:, d]), LN_LOW, 2.0 ** LN_LIFT - 1, ALU.is_lt, ALU.mult))
                s_hf.on(stt(flat(he[:, d]), flat(lows[:, d]), 1.0, flat(he[:, d]), ALU.add, ALU.mult))
            dve.wait_ge(s_hreset.sem, 2)
            for d in range(2):
                dve.wait_ge(s_hlog.sem, d + 1)
                lane.link(stt(flat(he[:, d]), flat(lows[:, d]), -LN_LIFT * math.log(2.0) / (2.0 ** LN_LIFT - 1),
                              flat(he[:, d]), ALU.mult, ALU.add))
                way = slice(None) if d == 0 else slice(None, None, -1)
                lane.link(v.tensor_tensor_scan(flat(hb[:, d])[:, way], resets[:, :], flat(he[:, d])[:, way], 0.0,
                                               ALU.mult, ALU.add))
            lane.link(v.memset(hattn, 0.0))

            def level(i):
                d, m = i // LEVELS, 1 << (i % LEVELS)
                cut = lambda w: w.rearrange("p (n m) -> p n m", m=2 * m)
                right, left = slice(m, 2 * m), slice(0, m)
                qs, ks = (right, left) if d == FWD else (left, right)
                b = cut(flat(hb[:, d]))
                ref = b[:, :, m - 1:m] if d == FWD else b[:, :, m:m + 1]
                return (d, b, cut(flat(he[:, i % 2])), cut(flat(hqk[:, i % 2])), cut(flat(hq)), cut(flat(hk[:, d])),
                        qs, ks, ref.to_broadcast([P, CW * T // (2 * m), m]))

            def ask(i):
                d, b, e, _, _, _, qs, ks, ref = level(i)
                lane.do(tt(e[:, :, qs], b[:, :, qs], ref, ALU.subtract))
                s_hd.on(tt(e[:, :, ks], ref, b[:, :, ks], ALU.subtract))

            def take(i):
                for t in range(NT):
                    key = ("level", i, t)
                    if i:
                        banks.emptied(dve, ("level", i - 1, t))
                    mask = levels[:, i // LEVELS, i % LEVELS, None, :].bitcast(U32).to_broadcast([P, HG_H, P])
                    banks.free(v.copy_predicated(hattn[:, t], mask, halves4(banks.at(dve, key))), key)

            banks.emptied(dve, ("hg_q", CW - 1))
            ask(0)
            for i in range(2 * LEVELS):
                if i + 1 < 2 * LEVELS:
                    ask(i + 1)
                d, _, e, qk, q, k, qs, ks, _ = level(i)
                dve.wait_ge(s_he.sem, i + 1)
                lane.do(tt(qk[:, :, qs], q[:, :, qs], e[:, :, qs], ALU.mult))
                s_hqk.on(tt(qk[:, :, ks], k[:, :, ks], e[:, :, ks], ALU.mult))
                dve.wait_ge(s_hqk.sem, i + 1)
                if i:
                    take(i - 1)
                    if i <= 10 and i % 2 == 0:
                        lift(0, i // 2 + 1, i // 2 + 2)
                else:
                    lift(0, 0, 2)
            for d in range(2):
                for w, t in ((0, 0), (1, FIRST[d])):
                    end = t * P + (P - 1 if d == FWD else 0)
                    ins = tt(hke[:, d, w], hb[:, d, :, end:end + 1].to_broadcast([P, HG_H, P]), hb[:, d, :, tok[t]],
                             ALU.subtract)
                    if (d, w) != (1, 1):
                        lane.do(ins)
            s_hx.on(ins)
            take(2 * LEVELS - 1)
            dve.wait_ge(s_hy.sem, 1)
            for d in range(2):
                for w, t in ((0, 0), (1, FIRST[d])):
                    ins = tt(hke[:, d, w], hke[:, d, w], hk[:, d, :, tok[t]], ALU.mult)
                    if (d, w) != (1, 1):
                        lane.do(ins)
            s_hke.on(ins)
            lane.do(tt(hqe[:, 0], hqe[:, 0], hq[:, :, P:T], ALU.mult))
            s_hqe.on(tt(hqe[:, 1], hqe[:, 1], hq[:, :, P:T], ALU.mult))
            dve.wait_ge(s_hke.sem, 1)
            s_hsum.on(tt(flat(hk[:, 0]), flat(hk[:, 0]), flat(hk[:, 1]), ALU.add))
            lift(0, 7, 8)
            for t in range(NT):
                key = ("diag", t)
                banks.emptied(dve, ("level", 2 * LEVELS - 1, t))
                banks.free(v.copy_predicated(
                    hattn[:, t], ident[:, None, :].bitcast(U32).to_broadcast([P, HG_H, P]),
                    halves4(banks.at(dve, key))), key)
            dve.wait_ge(s_hst.sem, 32)
            for d in range(2):
                banks.free(v.tensor_copy(hnew[:, d], halves4(banks.at(dve, ("hstate", d, 0)))), ("hstate", d, 0))
                ps = banks.at(dve, ("hstate", d, 1))
                for h in range(HG_H):
                    ins = stt(hst[:, d, 1, h, :], hst[:, d, 0, h, :], coef[:, d, h:h + 1], ps[:, h * P:(h + 1) * P],
                              ALU.mult, ALU.add)
                    if h < 3:
                        lane.do(ins)
                banks.free(ins, ("hstate", d, 1))
            dve.wait_ge(s_hgn.sem, 1)
            for t in range(NT):
                head_norm(1, "ho", t, ss[:, 16 + 4 * t:20 + 4 * t], hg, hyn, ROOT["hg"])

            for name in ("ssd_x", "ssd_bc"):
                conv(name)
            flat3 = lambda w: w.rearrange("p a b -> p (a b)")
            dve.wait_ge(s_row.sem, 16 * N_ROW)
            dve.wait_ge(s_pool.sem, 3)
            for t in range(NT):
                key = ("small", t)
                banks.free(tt(small[:, t, :], banks.at(dve, key)[:, 0:32], sign_row[:, :], ALU.mult), key)
            banks.emptied(dve, ("small", NT - 1))
            lane.link(tt(small[:, :, :], small[:, :, :], small_row[:, 0:1, :].to_broadcast([P, NT, 32]), ALU.add))
            s_sp.on(stt(small2[:, :, :], small[:, :, :], -1.0, small[:, :, :], ALU.mult, ALU.min))
            dve.wait_ge(s_spa.sem, 1)
            c0, c1 = cum[:, :, 0, :], cum[:, :, 1, :]
            lane.link(ts(c0, small2[:, :, :], 1.0, None, ALU.add))
            lane.link(ts(c1, c0, 1.0, None, ALU.subtract))
            lane.link(tt(c1, small2[:, :, :], c1, ALU.subtract))
            s_sp.on(v.tensor_copy(small2[:, :, :], c0))
            lane.link(v.reciprocal(c0, c0))
            lane.link(tt(c1, c1, c0, ALU.mult))
            dve.wait_ge(s_spa.sem, 3)
            lane.link(tt(small2[:, :, :], small2[:, :, :], c1, ALU.add))
            lane.link(stt(small2[:, :, :], small[:, :, :], 0.0, small2[:, :, :], ALU.max, ALU.add))
            s_small.on(stt(small[:, :, :], small2[:, :, :], -1.0,
                           small_row[:, 1:2, :].to_broadcast([P, NT, 32]), ALU.mult, ALU.mult))
            for t in range(NT):
                key = ("cum", t)
                banks.free(ts(cum[:, t].rearrange("p a b -> p (a b)"), banks.at(dve, key)[:, 0:160], -1.0, None,
                              ALU.mult), key)
            dve.wait_ge(s_ecum.sem, 1)
            for d in range(2):
                sc, gc = small_cols["ssd"][d], small_cols["gdn"][d]
                lane.do(tt(dte[:, :, d * 8:d * 8 + 8], small2[:, :, sc], ecum[:, :, 2 + d, sc], ALU.mult))
                lane.do(tt(bdec[:, :, d * 4:d * 4 + 4], beta[:, :, d * 4:d * 4 + 4], ecum[:, :, d, gc], ALU.mult))
            lane.wait_own()
            banks.emptied(dve, ("sx", NT - 1))
            heads8 = lambda w: w.rearrange("p (h x) -> p h x", h=SSD_H)
            for d in range(2):
                for w, t in ((0, 0), (1, FIRST[d])):
                    if d:
                        banks.at(dve, ("sstate", 0, w))
                    s_sxe.on(tt(heads8(sxd[:, w, :]), heads8(sxN[:, t, :]), each(dte[:, t, d * 8:d * 8 + 8]), ALU.mult))
                if d == 0:
                    take_states(dve, nc, banks, lane, 0, snew, sst, ecum, small_cols, FIRST, halves4, heads8)
            take_states(dve, nc, banks, lane, 1, snew, sst, ecum, small_cols, FIRST, halves4, heads8)
            for t in range(NT):
                cb = banks.at(dve, ("cb", t))
                for d in range(2):
                    for q in range(2):
                        banks.emptied(dve, ("sdec", t, d, q))
                        ins = tt(sdec[:, d, q], sdec[:, d, q],
                                 cb[:, None, q * P:(q + 1) * P].to_broadcast([P, 4, P]), ALU.mult)
                        if (d, q) != (1, 1):
                            lane.do(ins)
                banks.free(ins, ("cb", t))
                banks.emptied(dve, ("cb", t))
                if t == 0:
                    for w in range(2):
                        banks.at(dve, ("sstate", 1, w))
                for d in range(2):
                    ins = tt(heads8(sxd[:, d, :]), heads8(sxN[:, t, :]), each(small2[:, t, small_cols["ssd"][d]]),
                             ALU.mult)
                    if d == 0:
                        lane.do(ins)
                s_sw.on(ins)
                if t:
                    for d in range(2):
                        key = ("sinter", t, d)
                        banks.free(tt(heads8(sy[:, 3 * d, :]), heads8(banks.at(dve, key)),
                                      each(ecum[:, t, d, small_cols["ssd"][d]]), ALU.mult), key)
                    banks.emptied(dve, ("sinter", t, 1))
                    lane.link(tt(sy[:, 0, :], sy[:, 0, :], sy[:, 3, :], ALU.add))
                lane.link(tt(heads8(sy[:, 4, :]), heads8(sxN[:, t, :]), each(ssd_row[:, W:W + 8]), ALU.mult))
                key = ("sintra", t)
                banks.free(tt(sy[:, 4, :], sy[:, 4, :], banks.at(dve, key), ALU.add), key)
                banks.emptied(dve, key)
                if t:
                    lane.link(tt(sy[:, 4, :], sy[:, 4, :], sy[:, 0, :], ALU.add))
                s_sg.on(tt(sy[:, 1, :], sy[:, 4, :], sz[:, t, :], ALU.mult))
                lift(1, (0, 3, 6)[t], (3, 6, 8)[t])
                c = ss[:, 28 + 2 * t:30 + 2 * t]
                dve.wait_ge(s_ss.sem, SQ["ssd"] + t + 1)
                lane.link(v.reduce_sum(c, sy[:, 2, :].rearrange("p (g n) -> p g n", g=2), axis=AX))
                inverse_root(ROOT["ssd"] + t, c, 1.0 / 256)
                for g in range(2):
                    gg = slice(g * 256, (g + 1) * 256)
                    ins = stt(sy_out[:, t, gg], sy[:, 1, gg], c[:, g:g + 1], ssd_row[:, gg], ALU.mult, ALU.mult)
                    if g == 0:
                        lane.do(ins)
                s_yn2.on(ins)
                dve.wait_ge(s_yn2.sem, t + 1)

            for name in ("gdn_q", "gdn_k", "gdn_v"):
                conv(name)
            for i in range(2):
                for t in range(NT):
                    banks.emptied(dve, ("gn", i, t))
                    k = 34 + (i * NT + t) * 4
                    lane.link(tt(sq[:, :], gN[:, i, t, :], gN[:, i, t, :], ALU.mult))
                    lane.link(v.reduce_sum(ss[:, k:k + 4], halves4(sq[:, :]), axis=AX))
            inverse_root(ROOT["qk"], ss[:, 34:58], 1.0)
            lane.link(ts(ss[:, 34:46], ss[:, 34:46], float(P) ** -0.5, None, ALU.mult))
            for i in range(2):
                for t in range(NT):
                    k = 34 + (i * NT + t) * 4
                    ins = tt(halves4(gN[:, i, t, :]), halves4(gN[:, i, t, :]), each(ss[:, k:k + 4]), ALU.mult)
                    if (i, t) != (1, NT - 1):
                        lane.do(ins)
            s_gnorm.on(ins)
            ada_columns(8, 10)
            dve.wait_ge(s_gnorm.sem, 1)
            ident4 = ident[:, None, :].to_broadcast([P, 4, P])
            for r in range(NT):
                rt = [r, (0, 2, 1)[r]]
                for d in range(2):
                    t = rt[d]
                    banks.emptied(dve, ("gstrict", r, d))
                    for key, to in (("gkk", gw[:, d, 0]), ("gqk", gqk[:, t, d])):
                        banks.free(tt(to, to, halves4(banks.at(dve, (key, r, d))), ALU.mult), (key, r, d))
                for d in range(2):
                    dve.wait_ge(s_glevel[d].sem, r * LEVELS + 1)
                    lane.link(tt(gw[:, d, 3], ident4, gw[:, d, 1], ALU.subtract))
                    banks.free(tt(gw[:, d, 2], ident4, halves4(banks.at(dve, ("gprod", r, 0, d))), ALU.subtract),
                               ("gprod", r, 0, d))
                if r == 0:
                    ada_columns(LATE_ADA[0][0] - 1, LATE_ADA[0][1] - 1)
                for l in range(1, LEVELS):
                    if r == 0 and l < LEVELS - 1:
                        ada_columns(LATE_ADA[l][0] - 1, LATE_ADA[l][0])
                    for d in range(2):
                        for key, to in (("ginv", gw[:, d, 2]), ("ginvT", gw[:, d, 3])):
                            if key == "ginv" and l == LEVELS - 1:
                                continue
                            banks.emptied(dve, (key, r, l - 1, d) if l > 1 else ("gprod", r, 0, d))
                            banks.free(tt(to, to, halves4(banks.at(dve, (key, r, l, d))), ALU.subtract),
                                       (key, r, l, d))
                    if r == 0:
                        lo, hi = LATE_ADA[l]
                        ada_columns(lo - int(l == LEVELS - 1), hi if hi == 24 else hi - 1)
                    elif l in (2, 3, 4, 5):
                        n = (r - 1) * 4 + l - 2
                        lift(2, n, n + 1)
                if r == 0:
                    scales(1)
                for d in range(2):
                    t = rt[d]
                    dve.wait_ge(s_glevel[d].sem, (r + 1) * LEVELS)
                    lane.do(tt(gw[:, d, 2], halves4(gN[:, 2, t, :]), each(beta[:, t, d * 4:d * 4 + 4]), ALU.mult))
                    lane.do(tt(gw[:, d, 4], halves4(gN[:, 1, t, :]), each(bdec[:, t, d * 4:d * 4 + 4]), ALU.mult))
                    s_gvk[d].on(tt(gw[:, d, 0], halves4(gN[:, 1, t, :]),
                                   each(ecum[:, t, 2 + d, small_cols["gdn"][d]]), ALU.mult))
                if r < 2:
                    for d in range(2):
                        key = ("gstate", r, d)
                        ps = banks.at(dve, key)
                        if r == 0:
                            banks.free(v.tensor_copy(gs1[:, d], halves4(ps)), key)
                            continue
                        dve.wait_ge(s_out.sem, 16 * 6)
                        dve.wait_ge(s_gst.sem, 32)
                        for h in range(GDN_H):
                            ins = stt(gs1[:, d, h, :], gs0[:, d, h, :],
                                      ecum[:, rt[d], 4, small_cols["gdn"][d]][:, h:h + 1],
                                      ps[:, h * P:(h + 1) * P], ALU.mult, ALU.add)
                            if h < 3:
                                lane.do(ins)
                        banks.free(ins, key)
            for d in range(2):
                for t in (1, 2):
                    banks.emptied(dve, ("grow", t, d))
                    w = gqe[:, d, :, (t - 1) * P:t * P]
                    s_gqe.on(tt(w, w, gT[:, 0, :, tok[t]], ALU.mult))
            dve.wait_ge(s_gqe.sem, 4)
            dve.wait_ge(s_hgn.sem, 2)
            for t in range(NT):
                head_norm(3, "go", t, ss[:, 16 + 4 * t:20 + 4 * t], gz, gyn, ROOT["gdn"])
            lift(3, 0, 8)

            banks.emptied(dve, ("grow", 2, 1, 1))
            for c in range(4):
                cc = slice(c * 256, (c + 1) * 256)
                for t in range(NT):
                    k = c * NT + t
                    key = ("out", c, t)
                    banks.free(tt(sq[:, k % 2 * 256:k % 2 * 256 + 256], banks.at(dve, key)[:, 0:256],
                                  g1row[:, cmod[t], cc], ALU.mult), key)
                    banks.emptied(dve, key)
                    ins = tt(x[:, t, cc], x[:, t, cc], sq[:, k % 2 * 256:k % 2 * 256 + 256], ALU.add)
                    (s_x2.on if k == 11 else lane.link)(ins)
            norm_tokens(1)
            modulate(1)

            for t in range(NT):
                for h in range(2):
                    key = ("h2", t, h)
                    hh = slice(h * W, (h + 1) * W)
                    dve.wait_ge(s_h2.sem, t * 2 + h + 1)
                    banks.free(tt(h2[1][:, t, hh], banks.at(dve, key), h2[0][:, t, hh].bitcast(F32), ALU.subtract), key)

            dve.wait_ge(s_late.sem, 16 * N_LATE)
            biased, g8, sm, before, rbias = (pick[:, i, :] for i in (3, 4, 5, 6, 7))
            by8 = lambda w: w.rearrange("p (g e) -> p g e", g=NGRP)
            gs, rank, keep, pen, top, tot = (sm[:, i * 8:i * 8 + 8] for i in range(6))
            cmp_, masked, left = sq[:, 0:64], sq[:, 64:128], sq[:, 128:192]
            for t in range(NT):
                banks.emptied(dve, ("router", t))
                scores = pick[:, t, :]
                lane.link(tt(biased, scores, rbias, ALU.add))
                for g in range(NGRP):
                    lane.do(v.max(g8[:, g * 8:g * 8 + 8], biased[:, g * 8:g * 8 + 8]))
                lane.wait_own()
                lane.link(tt(gs, by8(g8)[:, :, 0], by8(g8)[:, :, 1], ALU.add))
                mine, other = gs[:, :, None].to_broadcast([P, 8, 8]), gs[:, None, :].to_broadcast([P, 8, 8])
                lane.link(tt(by8(cmp_), other, mine, ALU.is_equal))
                lane.link(tt(cmp_, cmp_, before, ALU.mult))
                lane.link(tt(by8(masked), other, mine, ALU.is_gt))
                lane.link(tt(cmp_, cmp_, masked, ALU.add))
                lane.link(v.reduce_sum(rank, by8(cmp_), axis=AX))
                lane.link(ts(keep, rank, float(TOPG), None, ALU.is_lt))
                lane.link(ts(pen, keep, -NEG, NEG, ALU.mult, ALU.add))
                lane.link(tt(by8(masked), by8(biased), each(keep, NE), ALU.mult))
                lane.link(tt(by8(masked), by8(masked), each(pen, NE), ALU.add))
                lane.link(v.max(top, masked))
                lane.link(v.match_replace(left, top, masked, TAKEN))
                lane.link(ts(chosen[:, t, :], left, TAKEN / 2, None, ALU.is_lt))
                lane.link(tt(cmp_, chosen[:, t, :], scores, ALU.mult))
                lane.link(v.reduce_sum(tot[:, 0:1], cmp_, axis=AX))
                lane.link(v.reciprocal(tot[:, 0:1], tot[:, 0:1]))
                s_gates.on(ts(egN[:, t, :], cmp_, tot[:, 0:1], ROUTED, ALU.mult, ALU.mult))
                dve.wait_ge(s_gates.sem, t + 1)
            for f in range(2):
                dve.wait_ge(s_sil.sem, f + 1)
                dve.wait_ge(s_h3.sem, f + 1)
                s_hid.on(tt(hid[:, f, :], psum[:, 7, 0:T], sil[:, f, :], ALU.mult))
            dve.wait_ge(s_ranks.sem, 1)
            lane.link(ts(places[:, :, 0:NE], chosen[:, :, :], -FAR, FAR, ALU.mult, ALU.add))
            rank3 = psum[:, 6, 0:NT * NE].rearrange("p (t e) -> p t e", t=NT)
            work3 = sq[:, 0:NT * NE].rearrange("p (t e) -> p t e", t=NT)
            lane.link(tt(work3, chosen[:, :, :], rank3, ALU.mult))
            lane.link(v.tensor_copy(cnt, psum[:, 6, NT * NE:(NT + 1) * NE]))
            s_placed.on(tt(places[:, :, 0:NE], places[:, :, 0:NE], work3, ALU.add))
            dve.wait_ge(s_placed.sem, 1)
            for p in range(1, NT):
                lane.do(ts(places[:, :, p * NE:(p + 1) * NE], places[:, :, 0:NE], float(p * P), None, ALU.subtract))
            lane.link(v.max(top, cnt))
            lane.link(ts(gs[:, 0:1], top[:, 0:1], float(P), NE / 2.0, ALU.is_gt, ALU.mult))
            lane.link(ts(gs[:, 1:2], top[:, 0:1], float(2 * P), NE / 2.0, ALU.is_gt, ALU.mult))
            lane.link(tt(gs[:, 0:1], gs[:, 0:1], gs[:, 1:2], ALU.add))
            lane.link(ts(n_middle[:, :], gs[:, 0:1], NE / 2.0 - 2, None, ALU.add))
            dve.wait_ge(s_rowsT.sem, 1)
            s_rowsN.on(v.tensor_copy(lifted[0:NE, 0, :], psum[0:NE, 7, 0:T]))
            dve.wait_ge(s_rowsT.sem, 2)
            for p, to in enumerate((lifted[0:NE, 1, :], gate[0:NE, 0, :], gate[0:NE, 1, :])):
                s_rowsN.on(ts(to, psum[0:NE, 6, 0:T], float(p * P), None, ALU.subtract))

        @block.gpsimd
        def _(pool):
            g = nc.gpsimd
            s_pool.on(g.memset(sign_row[:, 0:24], 1.0))
            s_pool.on(g.memset(sign_row[:, 24:32], -1.0))
            s_pool.on(g.memset(small_row[:, :, 24:32], 0.0))

            def add_branch(n, lo, hi):
                for j in range(lo, hi):
                    banks.emptied(pool, ("lift", n, j))
                    s_madd.on(g.tensor_tensor(mixed[:, j, :], mixed[:, j, :], lifted[:, j % 2, :], ALU.add))

            banks.emptied(pool, ("yo", CW - 1))
            s_hreset.on(g.memset(resets[:, :], 1.0))
            pool.wait_ge(s_hreset.sem, 1)
            s_hreset.on(g.memset(resets[:, 0:CW * T:P], 0.0))
            banks.emptied(pool, ("hg_g", NT - 1))
            pool.wait_ge(s_row.sem, 16 * N_ROW)
            h12 = lambda w: w.rearrange("p t (h n) -> p (t h) n", n=P)
            s_hgn.on(g.tensor_tensor(h12(hg), h12(hg), norm_row[:, 0:1, :].to_broadcast([P, 12, P]), ALU.mult))
            add_branch(1, 0, 8)
            for r in range(NT):
                for l in range(LEVELS):
                    for d in range(2):
                        if l:
                            banks.at(pool, ("gprod", r, l - 1, d))
                        else:
                            banks.emptied(pool, ("gkk", r, d))
                            if r:
                                banks.at(pool, ("gv", r - 1, d))
                        if l == 1:
                            banks.emptied(pool, ("gprod", r, 0, d))
                        s_glevel[d].on(g.tensor_tensor(
                            gw[:, d, 1], gw[:, d, 0], levels[:, d, l, None, :].to_broadcast([P, 4, P]), ALU.mult))
                    if r and l in (2, 3, 4, 5):
                        n = (r - 1) * 4 + l - 2
                        add_branch(2, n, n + 1)
            banks.emptied(pool, ("gdn_g", NT - 1))
            s_hgn.on(g.tensor_tensor(h12(gz), h12(gz), norm_row[:, 1:2, :].to_broadcast([P, 12, P]), ALU.mult))
            add_branch(3, 0, 8)

        @block.sync
        def _(sp):
            def load(to, src, s):
                sp.dma_start(to, src).then_inc(s.sem, 16)

            def row(w):
                return w.rearrange("(a n) -> a n", a=1).to_broadcast([P, w.shape[0]])

            load(ident[:, :], a["t_ident"], s_const)
            for i, (name, n) in enumerate((("conv_w", 96), ("conv_b", 32))):
                src = a[name][0].rearrange("w (j p) -> (w j) p", p=P) if i == 0 else \
                    a[name][0].rearrange("(j p) -> j p", p=P)
                load(rows[(0, 96)[i]:(96, 128)[i], 0, :], src, s_vec)
            load(rows[0:48, 1, :], a["ada_b"][0].rearrange("(j p) -> j p", p=P), s_vec)
            for i, (src) in enumerate((a["norm1_g"][0], a["norm2_g"][0], a["c_ctx"], a["c"][0])):
                load(rows[48 + 8 * i:56 + 8 * i, 1, :], src.rearrange("(j p) -> j p", p=P), s_vec)
            load(rows[80:88, 1, :], a["hg_lb"][:, 0, :].rearrange("a (j p) -> (a j) p", p=P), s_vec)
            load(fnet[0:33, 0, :], a["t_feats"], s_fnet)
            load(fw1[0:33, :], a["hy_w1"][0], s_fnet)
            load(fw2[:, :], a["hy_w2"][0], s_fnet)
            for i, name in enumerate(("hy_b1", "hy_b2")):
                load(fbias[:, i:i + 1], a[name][0].rearrange("(n a) -> n a", a=1), s_fnet)
            load(fw3[0:64, :], a["hy_w3"][0], s_fconst)
            load(window, a["t_window"], s_fconst)
            for L, to in ((P, dft1[:, :, None, :]), (2 * P, dft2)):
                for i, name in enumerate(("cos", "sin", "icos", "isin")):
                    load(to[:, i], a[f"t_{name}{L}"], s_fconst)
            load(hbias, a["hy_bias"][0][None, :, :].to_broadcast([P, 2, W]), s_fconst)
            for t, src in enumerate((a["x_prompt"][0], a["x_sample"][0][0:P], a["x_sample"][0][P:2 * P])):
                load(x[:, t, :], src, s_x)

            def slabs(lo, hi):
                for i in range(lo, hi):
                    name, src = slab_plan[i]
                    if i >= SLABS:
                        sp.wait_ge(banks.filled, slab_last[i - SLABS])
                    n = src.shape[1]
                    load(ring[:, i % SLABS, :].rearrange("p (k n) -> p k n", k=n), src, s_slab[i % SLABS])

            slabs(0, 8)
            load(sums[:, :, :], a["t_sums"], s_const)
            load(reach[:, :, :], a["t_reach"], s_const)
            load(levels[:, :, :, :], a["t_levels"], s_const)
            slabs(8, 16)
            load(small_row[:, 0, 0:16], row(a["ssd_dt_bias"][0].rearrange("a h -> (a h)")), s_row)
            load(small_row[:, 0, 16:24], row(a["gdn_dt_bias"][0].rearrange("a h -> (a h)")), s_row)
            load(small_row[:, 1, 0:16], row(a["ssd_a_log"][0].rearrange("a h -> (a h)")), s_row)
            load(small_row[:, 1, 16:24], row(a["gdn_a_log"][0].rearrange("a h -> (a h)")), s_row)
            load(ssd_row[:, 0:W], row(a["ssd_norm"][0]), s_row)
            load(ssd_row[:, W:W + 8], row(a["ssd_d"][0]), s_row)
            load(norm_row[:, 0, :], row(a["hg_norm"][0]), s_row)
            load(norm_row[:, 1, :], row(a["gdn_norm"][0]), s_row)
            load(smallw[:, :, 0:16], cols_of(w_in, COL["ssd_dt"], 16), s_row)
            load(smallw[:, :, 16:32], cols_of(w_in, COL["gdn_ab"], 16), s_row)
            slabs(16, len(slab_plan))

            banks.at(sp, ("yt", 3, NT - 1))
            load(iota[:, :], a["t_iota"], s_late)
            load(router_w, a["router_w"][0].rearrange("(k p) n -> p k n", p=P), s_late)
            load(pick[:, 7, :], row(a["router_bias"][0]), s_late)
            load(pick[:, 6, :], row(a["t_before"]), s_late)
            sp.wait_ge(s_late.sem, 16 * N_LATE)

            for i, name in enumerate(("sh_w1", "sh_w3")):
                load(wsh[:, i, :].rearrange("p (k n) -> p k n", k=KD),
                     a[name][0].rearrange("(k p) n -> p k n", p=P), s_shared)
            load(wsh[:, 2, :].rearrange("p (f n) -> p f n", f=2),
                 a["sh_w2"][0].rearrange("(f p) n -> p f n", p=P), s_shared)
            sp.wait_ge(s_rowsN.sem, 1)
            load(gates_dram, lifted[0:NE, 0, :], s_gstore)
            for p, src in enumerate((lifted[0:NE, 1, :], gate[0:NE, 0, :], gate[0:NE, 1, :])):
                sp.wait_ge(s_rowsN.sem, p + 2)
                load(places_dram[p * NE:(p + 1) * NE, :], src, s_gstore)
            sp.wait_ge(s_gstore.sem, 64)
            sp.wait_ge(s_out.sem, 16 * 6)

        branch_work.close()
        experts(ctx, nc, a, o, psum, x, h2, mod, ident, ss, sq, places, iota, n_middle,
                gates_dram, places_dram, s_out)


def experts(ctx, nc, a, o, psum, x, h2, mod, ident, ss, sq, places, iota, n_middle, gates_dram, places_dram, s_out):
    def sb(name, *shape, dt=F32):
        return ctx.enter_context(nc.sbuf_tensor(name, list(shape), dt))

    def sem(name):
        return ctx.enter_context(nc.semaphore(name))

    NRAW, PIECE = 6, 1024
    HI, LO = 0, 1
    KG = KD // 2
    raw = sb("raw", P, NRAW, PIECE)
    w13 = sb("w13", P, 2, 2, KD, 2, FE, dt=F32R)
    w2 = sb("w2", P, 2, 2, D, dt=F32R)
    xg = sb("xg", P, KD, 2, 2, P, dt=F32R)
    sel = sb("sel", P, NT, 2, P, dt=F32R)
    selT = sb("selT", P, 2, T, dt=F32R)
    hid = sb("hid", P, 2, FE)
    sil = sb("sil", P, 2, FE)
    hTs = sb("hTs", P, 2, 2, P, dt=F32R)
    y = sb("y", P, 2, 2, D, dt=F32R)
    rows = sb("rows", P, 2, 2, T)
    gslot = sb("gslot", P, 2)
    g2row, fg_row = raw[:, 0:2, :], raw[:, 2, :]

    s_filled = sem("job_filled")
    s_read = {"act": sem("act_took"), "dve": sem("dve_took")}
    s_raw = [sem(f"raw{i}_landed") for i in range(NRAW)]
    s_hi = sem("high_split")
    s_lo = {"dve": sem("low_split_dve"), "pool": sem("low_split_pool")}
    s_rows = [sem(f"expert{u}_rows_landed") for u in range(2)]
    s_sel = sem("selection_ready")
    s_selT = sem("selection_transposed")
    s_gslot = sem("gates_by_place_ready")
    s_scat = sem("outputs_added")
    s_g2, s_g2row = sem("gates_broadcast"), sem("gate_rows_ready")
    s_fg = sem("final_gain_landed")
    s_x = sem("tokens_done")
    s_sum, s_pre, s_root, s_inv = sem("last_squares"), sem("last_means"), sem("last_roots"), sem("last_inverses")
    s_fin, s_step = sem("outputs_ready"), sem("last_step")

    GA = [("G", k) for k in range(KD)]
    JOBS = [("H", 0), ("HT", 0), ("H", 1), ("Ya", 0), ("Yb", 0), GA[0], GA[1], ("HT", 1), GA[2], GA[3],
            ("Ya", 1), GA[4], ("Yb", 1)] + GA[5:]
    ADDS = {("H", 0): (1, 0, 5), ("Yb", 0): (1, 5, 9), GA[0]: (1, 9, 12), GA[1]: (0, 0, 2), GA[2]: (0, 2, 4),
            GA[4]: (0, 4, 7), GA[5]: (0, 7, 10), GA[6]: (0, 10, 12)}
    ADDS_LAST = {("H", 0): (1, 0, 4), ("Yb", 0): (1, 4, 12), ("HT", 1): (0, 0, 12)}
    JOBS_LAST = [j for j in JOBS if j[0] != "G"]
    READS = {"act": [j for j in JOBS if j[0] != "G" or j[1] % 2 == 0],
             "dve": [j for j in JOBS if j[0] != "G" or j[1] % 2 == 1]}
    NJ, NR = len(JOBS), len(READS["act"])
    W13P = [(m, kh) for m in range(2) for kh in range(2)]
    PIECES_0 = [(0, q) for q in W13P] + [(1, q) for q in W13P] + [("w2", f) for f in range(2)]
    PIECES = [(0, q) for q in W13P[:3]] + [("w2", f) for f in range(2)] + [(0, W13P[3])] + \
             [(1, q) for q in W13P] + [("w2", f) for f in range(2)]
    LO_BY_0 = ["dve"] * 4 + ["pool"] * 4 + ["dve"] * 2
    LO_BY = ["dve"] * 6 + ["pool"] * 4 + ["dve"] * 2
    N0, NB = len(PIECES_0), len(PIECES)
    W2_NOW = (3, 4)

    def filled(g, job, last=False):
        return g * NJ + (KD + (JOBS_LAST if last else JOBS).index(job) + 1)

    def read(g, by, job, last=False):
        order = [j for j in READS[by] if not (last and j[0] == "G")]
        return g * NR + (KG + order.index(job) + 1)

    def low(g, i):
        by = LO_BY[i]
        return by, g * LO_BY.count(by) + (LO_BY_0.count(by) + LO_BY[:i + 1].count(by))

    def low_0(i):
        by = LO_BY_0[i]
        return by, LO_BY_0[:i + 1].count(by)

    def bank(pos):
        return psum[:, 6 + pos % 2, :]

    def last_reader(job):
        return "act" if job[0] == "G" and job[1] % 2 == 0 else "dve"

    def split_parts(piece):
        to, q = piece
        if to == "w2":
            return [w2[:, part, q, :] for part in (HI, LO)]
        m, kh = q
        return [w13[:, to, part, kh * 4:kh * 4 + 4, m, :] for part in (HI, LO)]

    def raw_view(slot, piece):
        r = raw[:, slot, :]
        return r if piece[0] == "w2" else r.rearrange("p (k n) -> p k n", k=4)

    def raw_place(g, i):
        slot = (N0 + i) % NRAW
        return slot, g * (16 * NB // NRAW) + 16 * ((N0 + i) // NRAW + 1)

    def flat3(w):
        return w.rearrange("p a b n -> p (a b n)")

    def middle_pairs(eng):
        return eng.value_load(n_middle[0:1, 0:1], min_val=NE // 2 - 2, max_val=NT * NE // 2 - 2)

    def pairs(eng, body):
        n = middle_pairs(eng)
        body(0, first=True)
        with eng.Fori(1, n + 1) as g:
            body(g)
        body(n + 1, last=True)

    block = ctx.enter_context(nc.Block())

    @block.tensor
    def _(pe):
        mm = nc.tensor.matmul

        def split_product(out, terms, waits={}):
            n = len(terms) * 3
            i = 0
            for k, ((lh, ll), (rh, rl)) in enumerate(terms):
                if k in waits:
                    pe.wait_ge(*waits[k])
                for lhs, rhs in ((lh, rh), (lh, rl), (ll, rh)):
                    i += 1
                    last = mm(out, lhsT=lhs, rhs=rhs, start=i == 1, stop=i == n)
            return last

        def gather(k, pos):
            out = bank(pos)
            for part in (HI, LO):
                for t in range(NT):
                    last = mm(out[:, part * 256:part * 256 + 256], lhsT=h2[part][:, t, k * P:(k + 1) * P],
                              rhs=sel[:, t, :, :], start=t == 0, stop=t == NT - 1)
            return last

        def scatter(g, u, lo, hi, last=False, stop=False):
            if lo == 0:
                pe.wait_ge(s_selT, 2 * g + (u + 1))
                pe.wait_ge(s_read["dve"], read(g, "dve", ("Yb", u), last))
            for i in range(lo, hi):
                (t, h), part = divmod(i // 2, 2), i % 2
                ins = mm(psum[:, t * 2 + h, :], lhsT=selT[:, u, t * P:(t + 1) * P],
                         rhs=y[:, u, part, h * W:(h + 1) * W], start=False, stop=stop and part == LO)
            if hi == 12:
                ins.then_inc(s_scat, 1)

        pe.wait_ge(s_sel, 1)
        for k in range(KD):
            if k >= 2:
                pe.wait_ge(s_read[("act", "dve")[k % 2]], (k - 2) // 2 + 1)
            gather(k, k).then_inc(s_filled, 1)

        def body(g, first=False, last=False):
            jobs = JOBS_LAST if last else JOBS
            for pos, job in enumerate(jobs):
                kind, u = job
                if pos >= 2:
                    before = jobs[pos - 2]
                    by = last_reader(before)
                    pe.wait_ge(s_read[by], read(g, by, before, last))
                elif kind == "H":
                    pe.wait_ge(s_read["dve"], g * NR + (KG - 1))
                    pe.wait_ge(s_read["act"], g * NR + KG)
                elif first:
                    pe.wait_ge(s_read["dve"], KG)
                if kind == "H":
                    if u == 0:
                        pe.wait_ge(s_lo["dve"], 4 if first else low(g - 1, 5)[1])
                    else:
                        pe.wait_ge(s_lo["pool"], 4 if first else low(g - 1, 9)[1])
                    out = split_product(bank(pos), [((xg[:, k, HI, u, :], xg[:, k, LO, u, :]),
                                                     (w13[:, u, HI, k, :, :], w13[:, u, LO, k, :, :]))
                                                    for k in range(KD)],
                                        {KD - 1: (s_read["dve"], g * NR + KG)} if u == 0 else {})
                elif kind == "HT":
                    pe.wait_ge(s_read["dve"], read(g, "dve", ("H", u), last))
                    for f in range(2):
                        out = nc.tensor.transpose(bank(pos)[:, f * P:(f + 1) * P],
                                                  hid[:, u, f * P:(f + 1) * P], ident[:, :])
                elif kind in ("Ya", "Yb"):
                    h = "ab".index(kind[1])
                    if h == 0:
                        pe.wait_ge(s_read["dve"], read(g, "dve", ("HT", u), last))
                        if u == 0:
                            pe.wait_ge(s_lo["dve"], 6 if first else low(g - 1, 11)[1])
                        else:
                            pe.wait_ge(s_lo["dve"], low(g, 1 if last else W2_NOW[1])[1])
                    hh = slice(h * W, (h + 1) * W)
                    out = split_product(bank(pos), [((hTs[:, HI, f, :], hTs[:, LO, f, :]),
                                                     (w2[:, HI, f, hh], w2[:, LO, f, hh])) for f in range(2)])
                else:
                    if u == 0:
                        pe.wait_ge(s_sel, g + 2)
                    out = gather(u, pos)
                out.then_inc(s_filled, 1)
                adds = (ADDS_LAST if last else ADDS).get(job)
                if adds and adds[0] == 0:
                    scatter(g, *adds, last=last)
                elif adds and not first:
                    scatter(g - 1, *adds)
            if not last:
                return
            for i in range(4):
                cnd, h = divmod(i, 2)
                if i < 2:
                    pe.wait_ge(s_read["dve"], read(g, "dve", (("Ya", "Yb")[i], 1), last))
                else:
                    pe.wait_ge(s_g2row, i - 1)
                for j in range(4):
                    c = mod[:, 5 * KD + h * 4 + j, cnd:cnd + 1]
                    out = mm(bank(i)[:, j * P:(j + 1) * P], lhsT=c.to_broadcast([P, P]), rhs=ident[:, :],
                             start=True, stop=True)
                out.then_inc(s_g2, 1)
                if i == 1:
                    scatter(g, 1, 0, 12, last=last, stop=True)

        pairs(pe, body)

    @block.scalar
    def _(act):
        on = nc.scalar.activation

        def high(piece, slot, landed, free_at):
            if free_at is not None:
                act.wait_ge(s_filled, free_at)
            act.wait_ge(s_raw[slot], landed)
            on(split_parts(piece)[HI], raw_view(slot, piece), ACT.Copy).then_inc(s_hi, 1)

        def high_0(i):
            high(PIECES_0[i], i % NRAW, 16 * (i // NRAW + 1), None)

        def high_of(g, i, last=False):
            if last:
                piece, free_at = PIECES[W2_NOW[i]], filled(g, ("Yb", 0), last)
            else:
                piece = PIECES[i]
                free_at = filled(g, ("Yb", 0) if i in W2_NOW else ("Yb", 1) if piece[0] == "w2" else ("H", piece[0]))
            slot, landed = raw_place(g, i)
            high(piece, slot, landed, free_at)

        for i in range(4):
            high_0(i)
        for i, k in enumerate(range(0, KD, 2)):
            act.wait_ge(s_filled, k + 1)
            on(flat3(xg[:, k]), bank(k), ACT.Copy).then_inc(s_read["act"], 1)
            high_0(4 + i)
        high_0(8)
        high_0(9)

        def take(g, job, last=False):
            kind, u = job
            act.wait_ge(s_filled, filled(g, job, last))
            ps = bank((JOBS_LAST if last else JOBS).index(job))
            if kind == "H":
                ins = on(sil[:, u, :], ps[:, 0:FE], ACT.Silu)
            elif kind == "HT":
                ins = on(hTs[:, HI].rearrange("p f n -> p (f n)"), ps[:, 0:FE], ACT.Copy)
            elif kind == "G":
                ins = on(flat3(xg[:, u]), ps, ACT.Copy)
            else:
                h = "ab".index(kind[1])
                ins = on(y[:, u, HI, h * W:(h + 1) * W], ps, ACT.Copy)
            ins.then_inc(s_read["act"], 1)

        def body(g, first=False, last=False):
            if last:
                steps = [("H", 0), ("HT", 0), ("H", 1), ("Ya", 0), ("Yb", 0), 0, 1, ("HT", 1), ("Ya", 1), ("Yb", 1)]
            else:
                steps = [("H", 0), ("HT", 0), 0, 1, 2, ("H", 1), ("Ya", 0), ("Yb", 0), 3, GA[0], 4,
                         ("HT", 1), GA[2], 5, ("Ya", 1), GA[4], 6, ("Yb", 1), 7, GA[6], 8, 9, 10, 11]
            for s in steps:
                if isinstance(s, int):
                    high_of(g, s, last)
                else:
                    take(g, s, last)

        pairs(act, body)

        for i in range(4):
            act.wait_ge(s_g2, i + 1)
            cnd, h = divmod(i, 2)
            on(g2row[:, cnd, h * W:(h + 1) * W], bank(i), ACT.Copy).then_inc(s_g2row, 1)

        for t in range(NT):
            act.wait_ge(s_x, t + 1)
            on(raw[:, 3 + t, :], x[:, t, :], ACT.Square, accum_out=ss[:, t:t + 1]).then_inc(s_sum, 1)
            act.wait_ge(s_pre, t + 1)
            on(ss[:, t:t + 1], ss[:, t:t + 1], ACT.Sqrt).then_inc(s_root, 1)

    @block.vector
    def _(dve):
        v = nc.vector
        tt, ts, stt = v.tensor_tensor, v.tensor_scalar, v.scalar_tensor_tensor

        def gates_by_place(g, u):
            dve.wait_ge(s_rows[u], 32 * g + 32)
            stt(sq[:, 0:T], rows[:, u, 0, :], iota[:, P:P + 1], rows[:, u, 1, :], ALU.is_equal, ALU.mult,
                accum_out=gslot[:, u:u + 1]).then_inc(s_gslot, 1)

        def select_places(g, u):
            if not (isinstance(g, int) and g == 0):
                dve.wait_ge(s_scat, 2 * g + (u - 1))
            ts(selT[:, u, :], rows[:, u, 0, :], iota[:, P:P + 1], None, ALU.is_equal).then_inc(s_selT, 1)

        def select_tokens(at):
            tt(sel[:, :, :, :], iota[:, None, None, 0:P].to_broadcast([P, NT, 2, P]),
               places[:, :, at][:, :, :, None].to_broadcast([P, NT, 2, P]), ALU.is_equal).then_inc(s_sel, 1)

        def low_part(piece, slot, high_count):
            dve.wait_ge(s_hi, high_count)
            hi, lo = split_parts(piece)
            tt(lo, raw_view(slot, piece), hi.bitcast(F32), ALU.subtract).then_inc(s_lo["dve"], 1)

        select_tokens(slice(0, 2))
        gates_by_place(0, 0)
        for i in (0, 1, 2, 3):
            low_part(PIECES_0[i], i % NRAW, i + 1)
        for k in range(1, KD, 2):
            dve.wait_ge(s_filled, k + 1)
            v.tensor_copy(flat3(xg[:, k]), bank(k)).then_inc(s_read["dve"], 1)
        for i in (8, 9):
            low_part(PIECES_0[i], i % NRAW, i + 1)

        def take(g, job, last=False):
            kind, u = job
            dve.wait_ge(s_filled, filled(g, job, last))
            if kind != "G":
                dve.wait_ge(s_read["act"], read(g, "act", job, last))
            ps = bank((JOBS_LAST if last else JOBS).index(job))
            if kind == "H":
                dve.wait_ge(s_gslot, 2 * g + (u + 1))
                ins = stt(hid[:, u, :], ps[:, FE:], gslot[:, u:u + 1], sil[:, u, :], ALU.mult, ALU.mult)
            elif kind == "HT":
                part = [hTs[:, i].rearrange("p f n -> p (f n)") for i in (HI, LO)]
                ins = tt(part[LO], ps[:, 0:FE], part[HI].bitcast(F32), ALU.subtract)
            elif kind == "G":
                ins = v.tensor_copy(flat3(xg[:, u]), ps)
            else:
                h = "ab".index(kind[1])
                hh = slice(h * W, (h + 1) * W)
                ins = tt(y[:, u, LO, hh], ps, y[:, u, HI, hh].bitcast(F32), ALU.subtract)
            ins.then_inc(s_read["dve"], 1)

        def body(g, first=False, last=False):
            if last:
                steps = [("H", 0), ("HT", 0), "places0", "gates1", ("H", 1), ("Ya", 0), ("Yb", 0), 0, 1, ("HT", 1),
                         "places1", ("Ya", 1), ("Yb", 1)]
            else:
                steps = [("H", 0), ("HT", 0), "tokens", "gates1", "places0", 0, 1, ("H", 1), ("Ya", 0), 2,
                         ("Yb", 0), 3, GA[1], ("HT", 1), 4, "places1", GA[3], 5, ("Ya", 1), ("Yb", 1), "gates0",
                         GA[5], GA[7], 10, 11]
            for s in steps:
                if s == "tokens":
                    dve.wait_ge(s_filled, g * NJ + KD)
                    select_tokens(slice(2, 4) if first else bass.ds(2 * g + 2, 2))
                elif s in ("places0", "places1"):
                    select_places(g, int(s[-1]))
                elif s == "gates1":
                    gates_by_place(g, 1)
                elif s == "gates0":
                    gates_by_place(g + 1, 0)
                elif isinstance(s, int):
                    slot, _ = raw_place(g, s)
                    low_part(PIECES[W2_NOW[s]] if last else PIECES[s], slot, g * NB + (N0 + s + 1))
                else:
                    take(g, s, last)

        pairs(dve, body)

        n = middle_pairs(dve)
        dve.wait_ge(s_scat, 2 * n + 4)
        dve.wait_ge(s_fg, 16)
        dve.wait_ge(s_g2row, 4)
        dve.wait_ge(s_gslot, 2 * n + 4)
        step = 0
        for t in range(NT):
            for h in range(2):
                hh = slice(h * W, (h + 1) * W)
                tt(sq[:, :], psum[:, t * 2 + h, :], g2row[:, min(t, 1), hh], ALU.mult).then_inc(s_step, 1)
                step += 1
                dve.wait_ge(s_step, step)
                ins = tt(x[:, t, hh], x[:, t, hh], sq[:, :], ALU.add)
                if h:
                    ins.then_inc(s_x, 1)
                    dve.wait_ge(s_x, t + 1)
                else:
                    ins.then_inc(s_step, 1)
                    step += 1
                    dve.wait_ge(s_step, step)
        for t in range(NT):
            c = ss[:, t:t + 1]
            dve.wait_ge(s_sum, t + 1)
            ts(c, c, 1.0 / D, EPS, ALU.mult, ALU.add).then_inc(s_pre, 1)
            dve.wait_ge(s_root, t + 1)
            v.reciprocal(c, c).then_inc(s_inv, 1)
            dve.wait_ge(s_inv, t + 1)
            stt(x[:, t, :], x[:, t, :], c, fg_row, ALU.mult, ALU.mult).then_inc(s_fin, 1)

    @block.gpsimd
    def _(pool):
        g_ = nc.gpsimd

        def low_part(piece, slot, high_count):
            pool.wait_ge(s_hi, high_count)
            hi, lo = split_parts(piece)
            g_.tensor_tensor(lo, raw_view(slot, piece), hi.bitcast(F32), ALU.subtract).then_inc(s_lo["pool"], 1)

        for i in (4, 5, 6, 7):
            low_part(PIECES_0[i], i % NRAW, i + 1)

        def body(g, first=False, last=False):
            if last:
                return
            for i in (6, 7, 8, 9):
                slot, _ = raw_place(g, i)
                low_part(PIECES[i], slot, g * NB + (N0 + i + 1))

        pairs(pool, body)

    @block.sync
    def _(sp):
        ew = [a[n][0] for n in ("exp_w1", "exp_w3", "exp_w2")]

        def source(e, piece):
            to, q = piece
            m, part = (2, q) if to == "w2" else q
            w = ew[m][e] if isinstance(e, int) else ew[m][bass.ds(e, 1)].rearrange("a k n -> (a k) n")
            if to == "w2":
                return w[part * P:(part + 1) * P, :]
            return w[part * W:(part + 1) * W, :].rearrange("(k p) n -> p k n", p=P)

        def expert(g, u):
            return 2 * g + u if isinstance(g, int) else (2 * g + u) % NE

        def row_of(g, u):
            if not (isinstance(g, int) and g == 0):
                sp.wait_ge(s_selT, 2 * g + (u - 1))
            n, e = 2 * g + u, expert(g, u)
            for i, (src, at) in enumerate(((places_dram, n), (gates_dram, e))):
                src = src[at:at + 1, :] if isinstance(at, int) else src[bass.ds(at, 1), :]
                sp.dma_start(rows[:, u, i, :], src.to_broadcast([P, T])).then_inc(s_rows[u], 16)

        def piece_0(i):
            if i >= NRAW:
                by, n = low_0(i - NRAW)
                sp.wait_ge(s_lo[by], n)
            piece = PIECES_0[i]
            e = 0 if piece[0] == "w2" else piece[0]
            sp.dma_start(raw_view(i % NRAW, piece), source(e, piece)).then_inc(s_raw[i % NRAW], 16)

        row_of(0, 0)
        for i in range(N0):
            piece_0(i)
        def piece(g, i, first, last):
            which = PIECES[W2_NOW[i]] if last else PIECES[i]
            if i >= NRAW:
                by, n = low(g, i - NRAW)
            elif first:
                by, n = low_0(N0 - NRAW + i)
            else:
                by, n = low(g - 1, i + NRAW)
            sp.wait_ge(s_lo[by], n)
            now = last or i in W2_NOW
            e = expert(g, 1) if now else expert(g + 1, 0 if which[0] == "w2" else which[0])
            slot, _ = raw_place(g, i)
            sp.dma_start(raw_view(slot, which), source(e, which)).then_inc(s_raw[slot], 16)

        def body(g, first=False, last=False):
            row_of(g, 1)
            for i in range(2 if last else NB):
                piece(g, i, first, last)
                if i == NRAW - 1:
                    row_of(g + 1, 0)
            if last:
                by, n = low(g - 1, 10)
                sp.wait_ge(s_lo[by], n)
                sp.dma_start(fg_row, a["final_g"].rearrange("(a n) -> a n", a=1).to_broadcast([P, D])
                             ).then_inc(s_fg, 16)

        pairs(sp, body)

        for t, to in enumerate((o["y_prompt"][0], o["y_sample"][0][0:P], o["y_sample"][0][P:2 * P])):
            sp.wait_ge(s_fin, t + 1)
            sp.dma_start(to, x[:, t, :]).then_inc(s_out.sem, 16)
        sp.wait_ge(s_out.sem, 16 * 9)


def take_states(dve, nc, banks, lane, d, snew, sst, ecum, small_cols, FIRST, halves4, heads8):
    banks.free(nc.vector.tensor_copy(snew[:, d], halves4(banks.at(dve, ("sstate", d, 0)))), ("sstate", d, 0))
    banks.emptied(dve, ("sin", d))
    ps = banks.at(dve, ("sstate", d, 1))
    total = ecum[:, FIRST[d], 4, small_cols["ssd"][d]]
    lane.link(nc.vector.tensor_tensor(heads8(sst[:, d, 1, :]), heads8(sst[:, d, 0, :]),
                                      total[:, :, None].to_broadcast([P, SSD_H, 64]), ALU.mult))
    banks.free(nc.vector.tensor_tensor(sst[:, d, 1, :], sst[:, d, 1, :], ps, ALU.add), ("sstate", d, 1))


OUTS = {"y_prompt": (1, 128, 1024), "y_sample": (1, 256, 1024), "new_hgrn": (1, 1, 2, 4, 128, 128),
        "new_ssd": (1, 1, 2, 8, 64, 128), "new_gdn": (1, 1, 2, 4, 128, 128)}


def kernel(**inputs):
    import concourse.bacc as bacc
    from concourse.bass_utils import run_bass_kernel_spmd

    nc = bacc.Bacc("TRN2", target_bir_lowering=False, num_devices=1)
    arrays, a = {}, {}
    for name, value in {**inputs, **shape_tables()}.items():
        value = np.ascontiguousarray(value)
        arrays[f"in_{name}"] = value
        a[name] = nc.dram_tensor(f"in_{name}", value.shape, mybir.dt.from_np(value.dtype), kind="ExternalInput").ap()
    o = {name: nc.dram_tensor(f"out_{name}", shape, F32, kind="ExternalOutput").ap() for name, shape in OUTS.items()}
    trunk(nc, a, o)
    r = run_bass_kernel_spmd(nc, [arrays], core_ids=[0])
    return tuple(r.results[0][f"out_{name}"] for name in OUTS)
```
